# Optimizing a Trainium2 kernel written in Bass

```python
import math
import jax, jax.numpy as jnp
from jax import lax
import numpy as np

D_MODEL = 2048
BATCH = 1
SEQ = 256
DEPTH = 2
DEC_BATCH = 8
DEC_SEQ = 4
PAST_LEN = 1024
PAGE_SIZE = 128

NORM_EPS = 1e-6
NEG_INF = -1e30
MIX_WIDTH = D_MODEL
D_CONV = MIX_WIDTH // 2
CONV_WIDTH = 31
GLA_HEADS = 4
GLA_DV = MIX_WIDTH // 2
GLA_DK = GLA_DV // 2
GLA_HK = GLA_DK // GLA_HEADS
GLA_HV = GLA_DV // GLA_HEADS
GLA_RANK = 16
GLA_GATE_NORM = 16.0
GLA_CHUNK = 64
D_SGU = MIX_WIDTH // 2
SGU_GROUPS = 4
SGU_GD = D_SGU // SGU_GROUPS
SGU_CHUNK = 128
ATT_HD = 64
ATT_HEADS = (MIX_WIDTH // 2) // ATT_HD
ATT_KV_HEADS = 2
ATT_REP = ATT_HEADS // ATT_KV_HEADS
ATT_WIDTH = ATT_HEADS * ATT_HD
KV_WIDTH = ATT_KV_HEADS * ATT_HD
WINDOW = 128
D_FF = ((8 * D_MODEL + 3 * 256 - 1) // (3 * 256)) * 256
IN_AB = 2 * D_CONV + 2 * GLA_DK + 2 * GLA_DV + GLA_RANK
IN_CD = 2 * D_SGU + ATT_WIDTH + 2 * KV_WIDTH

kernel_name = 'hybrid_conv_gla_sgu_swa_step'

def split_cols(z, sizes):
    idx = np.cumsum(sizes)[:-1].tolist()
    return jnp.split(z, idx, axis=-1)

def rms_norm(x, g):
    xf = x.astype(jnp.float32)
    y = xf * lax.rsqrt(jnp.mean(xf * xf, axis=-1, keepdims=True) + NORM_EPS)
    return (y * g.astype(jnp.float32)).astype(x.dtype)

def layer_norm(x, g, b):
    xf = x.astype(jnp.float32)
    mu = jnp.mean(xf, axis=-1, keepdims=True)
    xc = xf - mu
    y = xc * lax.rsqrt(jnp.mean(xc * xc, axis=-1, keepdims=True) + NORM_EPS)
    return (y * g.astype(jnp.float32) + b.astype(jnp.float32)).astype(x.dtype)

def adaln(c, w, b):
    return jnp.split(jax.nn.silu(c) @ w + b, 6, axis=-1)

def modulate(x, g, shift, scale):
    return rms_norm(x, g) * (1.0 + scale[:, None, :]) + shift[:, None, :]

def swiglu_sublayer(x, shift, scale, gate, g, w_gate, w_up, w_down):
    h = modulate(x, g, shift, scale)
    return x + gate[:, None, :] * ((jax.nn.silu(h @ w_gate) * (h @ w_up)) @ w_down)

def conv_module(za, prev_rows, conv_w, conv_b, ln_g, ln_b):
    u = za[..., :D_CONV] * jax.nn.sigmoid(za[..., D_CONV:])
    u_ext = jnp.concatenate([prev_rows.astype(u.dtype), u], axis=1)
    y = lax.conv_general_dilated(u_ext, conv_w[:, None, :], window_strides=(1,), padding='VALID',
                                 dimension_numbers=('NWC', 'WIO', 'NWC'),
                                 feature_group_count=D_CONV) + conv_b
    y = jax.nn.silu(layer_norm(y, ln_g, ln_b))
    return y, u_ext[:, -(CONV_WIDTH - 1):]

def gla_chunked(q, k, v, log_a, s0):
    B, T, H, dk = q.shape
    L = math.gcd(T, GLA_CHUNK)
    n = T // L

    def to_chunks(z):
        return z.reshape(B, n, L, H, z.shape[-1]).transpose(1, 0, 3, 2, 4)

    mask = jnp.tril(jnp.ones((L, L), dtype=bool))

    def step(S, inp):
        qi, ki, vi, ai = inp
        b = jnp.cumsum(ai, axis=2)
        q_dec = qi * jnp.exp(b)
        att = jnp.einsum('bhtd,bhsd->bhts', q_dec, ki * jnp.exp(-b))
        att = jnp.where(mask, att, 0.0)
        o = jnp.einsum('bhts,bhsv->bhtv', att, vi) + jnp.einsum('bhtd,bhdv->bhtv', q_dec, S)
        b_last = b[:, :, -1:]
        S = S * jnp.exp(b_last[:, :, 0])[..., None] + jnp.einsum(
            'bhsd,bhsv->bhdv', ki * jnp.exp(b_last - b), vi)
        return S, o

    S, o = lax.scan(step, s0, (to_chunks(q), to_chunks(k), to_chunks(v), to_chunks(log_a)))
    o = o.transpose(1, 0, 3, 2, 4).reshape(B, T, H, v.shape[-1])
    return o, S

def gla_mixer(zq, zk, zv, zg, zr, s0, w_gate, b_gate, g_norm):
    B, T, _ = zq.shape
    f32 = jnp.float32

    def heads(z, d):
        return z.reshape(B, T, GLA_HEADS, d).astype(f32)

    log_a = jax.nn.log_sigmoid((zr @ w_gate + b_gate).astype(f32)) / GLA_GATE_NORM
    q = heads(zq, GLA_HK) * (GLA_HK ** -0.5)
    o, s_new = gla_chunked(q, heads(zk, GLA_HK), heads(zv, GLA_HV), heads(log_a, GLA_HK), s0.astype(f32))
    o = rms_norm(o, g_norm) * jax.nn.silu(heads(zg, GLA_HV))
    return o.reshape(B, T, GLA_DV).astype(zq.dtype), s_new.astype(s0.dtype)

def mix_ab(z, conv_prev, gla_prev, conv_w, conv_b, conv_ln_g, conv_ln_b, gla_w_gate, gla_b_gate, gla_g_norm):
    za, zq, zk, zv, zg, zr = split_cols(z, [2 * D_CONV, GLA_DK, GLA_DK, GLA_DV, GLA_DV, GLA_RANK])
    ya, conv_new = conv_module(za, conv_prev, conv_w, conv_b, conv_ln_g, conv_ln_b)
    yb, gla_new = gla_mixer(zq, zk, zv, zg, zr, gla_prev, gla_w_gate, gla_b_gate, gla_g_norm)
    return jnp.concatenate([ya, yb], axis=-1), conv_new, gla_new

def sgu_mixer(zu, zv, w_sp, b_sp, ln_g, ln_b):
    B, T, _ = zu.shape
    L = min(T, SGU_CHUNK)
    n = T // L
    u = jax.nn.gelu(zu)
    v = layer_norm(jax.nn.gelu(zv), ln_g, ln_b)
    w = jnp.where(jnp.tril(jnp.ones((SGU_CHUNK, SGU_CHUNK), dtype=bool)), w_sp, 0.0)[:, :L, :L]
    mixed = jnp.einsum('gts,bnsgc->bntgc', w, v.reshape(B, n, L, SGU_GROUPS, SGU_GD))
    mixed = mixed + b_sp[:, :L].T[:, :, None]
    return u * mixed.reshape(B, T, D_SGU), v

def alibi_slopes():
    s = 2.0 ** (-8.0 * np.arange(1, ATT_HEADS + 1) / ATT_HEADS)
    return jnp.asarray(s, dtype=jnp.float32).reshape(ATT_KV_HEADS, ATT_REP)

def sink_softmax(s, sink):
    m = jnp.maximum(jnp.max(s, axis=-1, keepdims=True), sink)
    p = jnp.exp(s - m)
    return p / (jnp.sum(p, axis=-1, keepdims=True) + jnp.exp(sink - m))

def swa_banded(q, k, v, sinks):
    B, T = q.shape[:2]
    W = WINDOW
    n = T // W
    f32 = jnp.float32

    def with_prev(z):
        zb = z.reshape(B, n, W, ATT_KV_HEADS, ATT_HD)
        prev = jnp.concatenate([jnp.zeros_like(zb[:, :1]), zb[:, :-1]], axis=1)
        return jnp.concatenate([prev, zb], axis=2)

    kb, vb = with_prev(k), with_prev(v)
    qb = q.reshape(B, n, W, ATT_KV_HEADS, ATT_REP, ATT_HD)
    kj = jnp.arange(2 * W)
    dist = jnp.arange(W)[:, None] - kj[None, :] + W
    valid = (dist >= 0) & (dist < W) & ((jnp.arange(n)[:, None, None] * W + kj[None, None, :]) >= W)
    s = jnp.einsum('bnqgrd,bnkgd->bngrqk', qb.astype(f32), kb.astype(f32)) * (ATT_HD ** -0.5)
    s = s - alibi_slopes()[:, :, None, None] * dist.astype(f32)
    s = jnp.where(valid[None, :, None, None], s, NEG_INF)
    p = sink_softmax(s, sinks.astype(f32).reshape(ATT_KV_HEADS, ATT_REP)[None, None, :, :, None, None])
    o = jnp.einsum('bngrqk,bnkgd->bnqgrd', p.astype(v.dtype), vb)
    return o.reshape(B, T, ATT_WIDTH)

def swa_buffered(q, k_all, v_all, sinks):
    B, T = q.shape[:2]
    S = k_all.shape[1]
    f32 = jnp.float32
    dist = (S - T + jnp.arange(T))[:, None] - jnp.arange(S)[None, :]
    valid = (dist >= 0) & (dist < WINDOW)
    s = jnp.einsum('btgrd,bsgd->bgrts', q.astype(f32), k_all.astype(f32)) * (ATT_HD ** -0.5)
    s = s - alibi_slopes()[:, :, None, None] * dist.astype(f32)
    s = jnp.where(valid, s, NEG_INF)
    p = sink_softmax(s, sinks.astype(f32).reshape(ATT_KV_HEADS, ATT_REP)[None, :, :, None, None])
    o = jnp.einsum('bgrts,bsgd->btgrd', p.astype(v_all.dtype), v_all)
    return o.reshape(B, T, ATT_WIDTH)

def mix_cd(z, k_buf, v_buf, buf_len, sgu_w, sgu_b, sgu_ln_g, sgu_ln_b, att_sinks):
    zu, zv, zq, zk, zvv = split_cols(z, [D_SGU, D_SGU, ATT_WIDTH, KV_WIDTH, KV_WIDTH])
    yc, v_rows = sgu_mixer(zu, zv, sgu_w, sgu_b, sgu_ln_g, sgu_ln_b)
    B, T, _ = z.shape
    q = zq.reshape(B, T, ATT_KV_HEADS, ATT_REP, ATT_HD)
    k = zk.reshape(B, T, ATT_KV_HEADS, ATT_HD)
    v = zvv.reshape(B, T, ATT_KV_HEADS, ATT_HD)
    if k_buf is None:
        yd = swa_banded(q, k, v, att_sinks)
        k_all, v_all = k, v
    else:
        k_all = jnp.concatenate([k_buf.astype(k.dtype), k], axis=1)
        v_all = jnp.concatenate([v_buf.astype(v.dtype), v], axis=1)
        yd = swa_buffered(q, k_all, v_all, att_sinks)
    return jnp.concatenate([yc, yd], axis=-1), v_rows, k_all[:, -buf_len:], v_all[:, -buf_len:]

def setup_inputs(seed: int = 0) -> dict:
    key = jax.random.key(seed)
    ks = iter(jax.random.split(key, 40))
    d = D_MODEL
    wb = min(WINDOW, PAST_LEN)

    def nrm(shape, s):
        return jax.random.normal(next(ks), shape, jnp.float32) * s

    return {
        'x_prompt': nrm((BATCH, SEQ, d), 1.0),
        'x_sample': nrm((DEC_BATCH, DEC_SEQ, d), 1.0),
        'c_prompt': nrm((BATCH, d), 1.0),
        'c_sample': nrm((DEC_BATCH, d), 1.0),
        'state_conv': nrm((DEC_BATCH, CONV_WIDTH - 1, D_CONV), 0.5),
        'state_gla': nrm((DEC_BATCH, GLA_HEADS, GLA_HK, GLA_HV), 1.0),
        'cache_k': nrm((DEC_BATCH, wb, ATT_KV_HEADS, ATT_HD), 1.0),
        'cache_v': nrm((DEC_BATCH, wb, ATT_KV_HEADS, ATT_HD), 1.0),
        'w_ada': nrm((DEPTH, d, 6 * d), 0.5 * d ** -0.5),
        'b_ada': nrm((DEPTH, 6 * d), 0.02),
        'g_mix': 1.0 + nrm((DEPTH, d), 0.05),
        'g_ffn': 1.0 + nrm((DEPTH, d), 0.05),
        'w_in_ab': nrm((d, IN_AB), d ** -0.5),
        'conv_w': nrm((CONV_WIDTH, D_CONV), CONV_WIDTH ** -0.5),
        'conv_b': nrm((D_CONV,), 0.02),
        'conv_ln_g': 1.0 + nrm((D_CONV,), 0.05),
        'conv_ln_b': nrm((D_CONV,), 0.02),
        'gla_w_gate': nrm((GLA_RANK, GLA_DK), GLA_RANK ** -0.5),
        'gla_b_gate': nrm((GLA_DK,), 0.02),
        'gla_g_norm': 1.0 + nrm((GLA_HV,), 0.05),
        'w_in_cd': nrm((d, IN_CD), d ** -0.5),
        'sgu_w': nrm((SGU_GROUPS, SGU_CHUNK, SGU_CHUNK), SGU_CHUNK ** -0.5),
        'sgu_b': 1.0 + nrm((SGU_GROUPS, SGU_CHUNK), 0.05),
        'sgu_ln_g': 1.0 + nrm((D_SGU,), 0.05),
        'sgu_ln_b': nrm((D_SGU,), 0.02),
        'att_sinks': nrm((ATT_HEADS,), 1.0),
        'w_out': nrm((DEPTH, MIX_WIDTH, d), MIX_WIDTH ** -0.5),
        'w_ffn_gate': nrm((DEPTH, d, D_FF), d ** -0.5),
        'w_ffn_up': nrm((DEPTH, d, D_FF), d ** -0.5),
        'w_ffn_down': nrm((DEPTH, D_FF, d), D_FF ** -0.5),
        'g_final': 1.0 + nrm((d,), 0.05),
    }

def reference(x_prompt, x_sample, c_prompt, c_sample, state_conv, state_gla, cache_k, cache_v,
              w_ada, b_ada, g_mix, g_ffn, w_in_ab, conv_w, conv_b, conv_ln_g, conv_ln_b,
              gla_w_gate, gla_b_gate, gla_g_norm, w_in_cd, sgu_w, sgu_b, sgu_ln_g, sgu_ln_b,
              att_sinks, w_out, w_ffn_gate, w_ffn_up, w_ffn_down, g_final):
    bp = x_prompt.shape[0]
    buf_len = cache_k.shape[1]
    yp, ys = x_prompt, x_sample
    for layer in range(DEPTH):
        mp = adaln(c_prompt, w_ada[layer], b_ada[layer])
        ms = adaln(c_sample, w_ada[layer], b_ada[layer])
        hp = modulate(yp, g_mix[layer], mp[0], mp[1])
        hs = modulate(ys, g_mix[layer], ms[0], ms[1])
        if layer % 2 == 0:
            conv0 = jnp.zeros((bp, CONV_WIDTH - 1, D_CONV), yp.dtype)
            gla0 = jnp.zeros((bp, GLA_HEADS, GLA_HK, GLA_HV), yp.dtype)
            op, st_conv_p, st_gla_p = mix_ab(hp @ w_in_ab, conv0, gla0, conv_w, conv_b, conv_ln_g,
                                             conv_ln_b, gla_w_gate, gla_b_gate, gla_g_norm)
            os_, st_conv_s, st_gla_s = mix_ab(hs @ w_in_ab, state_conv, state_gla, conv_w, conv_b,
                                              conv_ln_g, conv_ln_b, gla_w_gate, gla_b_gate, gla_g_norm)
        else:
            op, _, k_p, v_p = mix_cd(hp @ w_in_cd, None, None, buf_len, sgu_w, sgu_b,
                                     sgu_ln_g, sgu_ln_b, att_sinks)
            os_, sgu_v_s, k_s, v_s = mix_cd(hs @ w_in_cd, cache_k, cache_v, buf_len, sgu_w, sgu_b,
                                            sgu_ln_g, sgu_ln_b, att_sinks)
        yp = yp + mp[2][:, None, :] * (op @ w_out[layer])
        ys = ys + ms[2][:, None, :] * (os_ @ w_out[layer])
        yp = swiglu_sublayer(yp, mp[3], mp[4], mp[5], g_ffn[layer], w_ffn_gate[layer],
                             w_ffn_up[layer], w_ffn_down[layer])
        ys = swiglu_sublayer(ys, ms[3], ms[4], ms[5], g_ffn[layer], w_ffn_gate[layer],
                             w_ffn_up[layer], w_ffn_down[layer])
    y_prompt = rms_norm(yp, g_final)
    y_sample = rms_norm(ys, g_final)
    return (y_prompt, y_sample, st_conv_p, st_conv_s, st_gla_p, st_gla_s, sgu_v_s, k_p, k_s, v_p, v_s)


_drawn_inputs = setup_inputs


def setup_inputs(seed=0):
    import zlib

    import numpy as np

    out = dict(_drawn_inputs(seed))
    spreads = {}
    factors = {'g_ffn': 2.784,
     'conv_b': 8.0,
     'conv_ln_g': 6.766,
     'conv_ln_b': 23.521,
     'gla_b_gate': 6.276,
     'gla_g_norm': 7.521,
     'sgu_b': 7.628,
     'sgu_ln_b': 2.85,
     'att_sinks': 3.144}
    for name, (base, spread) in spreads.items():
        noise = np.random.default_rng([zlib.crc32(name.encode()), seed]).standard_normal(out[name].shape)
        drawn = base * np.exp(spread * noise) if base else spread * noise
        out[name] = __import__('jax').numpy.asarray(drawn.astype(out[name].dtype))
    for name, factor in factors.items():
        out[name] = (out[name] * factor).astype(out[name].dtype)
    return out
```

```python
from contextlib import ExitStack

import concourse.bass as bass
from concourse import mybir
import numpy as np

F32 = mybir.dt.float32
F32R = mybir.dt.float32r
U32 = mybir.dt.uint32
ALU = mybir.AluOpType
ACT = mybir.ActivationFunctionType
AX = mybir.AxisListType

P = 128
D = 2048
KT = D // P
NP_TOK = 256
NSEQ, TS = 8, 4
T = NP_TOK + NSEQ * TS
S9 = 1 + NSEQ
TAPS, HIST = 31, 30
UW = HIST + NP_TOK
SW = HIST + TS
UE = UW + NSEQ * SW
CT = 8
FF_T = 44
BLK = FF_T // 2
HEADS = 4
SLOT = 2 * KT * P
ADA_N = 512
UNITS = 6 * D // ADA_N
KEYS = P + NSEQ * TS
EPS = 1e-6
GELU_2C = 2.0 * (2.0 / np.pi) ** 0.5
GELU_K = GELU_2C * 0.044715
NEG = -1e30
SLOPES = [float(np.float32(2.0 ** (-8.0 * (h + 1) / 16))) for h in range(16)]

VEC = {}
_at = 0
for _name, _n in (("g_mix", 2 * KT), ("g_ffn", 2 * KT), ("g_final", KT), ("conv_b", CT), ("conv_ln_g", CT),
                  ("conv_ln_b", CT), ("gla_b_gate", HEADS), ("gla_g_norm", 2), ("sgu_ln_g", CT), ("sgu_ln_b", CT),
                  ("b_ada", 2 * 96), ("conv_w", CT * TAPS)):
    VEC[_name] = _at
    _at += _n
NVEC = _at


class Seg:

    def __init__(self, kind, layer, bodies, m, first, unit=None, group=0):
        self.kind, self.layer, self.bodies, self.m = kind, layer, bodies, m
        self.first = first
        self.unit = unit
        self.group = group
        self.steps = bodies * m
        self.ktiles = {"zr": 8, "down": BLK // 2}.get(kind, KT)
        self.two = kind not in ("zr", "down")
        self.width = 2 * self.ktiles * P
        self.act_links = {"gate": 4, "gu": 4, "sgu": 8}.get(kind, 0)
        self.dve_links = {"gate": 2 * TAPS - 1, "zconv": 2 * TAPS - 1, "gu": 2, "out": 4,
                          "down": 2 if group else 4}.get(kind, 0)


def plan():
    segs, norm = [], "norm"
    segs += [Seg("zr", 0, 1, 1, 0), Seg("gate", 0, 4, 2, 0, 8), Seg("zconv", 0, 4, 2, 8, 12, 0),
             Seg("z", 0, 2, 2, 16, 16, 16)]
    segs += ["mix0", Seg("out", 0, 4, 2, 0, 18), norm]
    for layer in range(2):
        if layer:
            segs += [Seg("kv", 1, 1, 1, 0), Seg("q", 1, 2, 2, 1), Seg("sgu", 1, 4, 2, 5), "mix1",
                     Seg("out", 1, 4, 2, 0), norm]
        segs += [Seg("gu", layer, 11, 2, 0, None if layer else 22),
                 Seg("down", layer, 8, 2, 0, None if layer else 33, 0)]
        if layer:
            segs += [Seg("gu", 1, 11, 2, 22)]
        else:
            segs += [Seg("gu", 0, 7, 2, 22, 41), Seg("gu", 0, 4, 2, 36)]
        segs += [Seg("down", layer, 8, 2, 16, None, 1), norm]
    return segs


PLAN = plan()
SEGS = [s for s in PLAN if isinstance(s, Seg)]
_n = _sig = _gel = _x = 0
_q = KT
for _s in SEGS:
    _s.n0, _s.sig0, _s.gel0, _s.q0, _s.x0 = _n, _sig, _gel, _q, _x
    _n += _s.steps
    if _s.kind in ("gate", "gu"):
        _sig += _s.steps
    if _s.kind == "sgu":
        _sig += 2 * _s.steps
        _gel += 2 * _s.steps
        _q += CT
    if _s.kind == "z":
        _q += CT
    if _s.kind == "out" or _s.kind == "down" and _s.group:
        _q += KT
        _x += KT
STEPS = _n
for _a, _b in zip(SEGS, SEGS[1:] + [None]):
    _a.next = _b
for _a, _b in zip(PLAN, PLAN[1:]):
    if isinstance(_a, Seg):
        _a.then_wait = not isinstance(_b, Seg) or "down" in (_a.kind, _b.kind)
SGU_SEG = next(s for s in SEGS if s.kind == "sgu")
Z_SEG = next(s for s in SEGS if s.kind == "z")
SQUARES = [0, 16, 24, 40, 56, 64, 80, 96]
NORM_STATS = [1, 3, 4, 6, 7]
GLA_A = 4 * 18


def lin(i, per, c):
    return c if i is None else i * per + c


class Links:

    def __init__(self, eng, sem):
        self.eng, self.sem, self.n, self.i, self.per = eng, sem, 0, None, 0

    def value(self, n):
        return n if self.i is None else self.i * self.per + n

    def mark(self, ins):
        ins.then_inc(self.sem, 1)
        self.n += 1
        return self.n

    def wait(self, n):
        self.eng.wait_ge(self.sem, self.value(n))

    def link(self, ins):
        self.wait(self.mark(ins))

    def enter(self, i, per):
        self.i, self.per, self.start = i, per, self.n

    def leave(self, turns):
        assert self.n - self.start == self.per, (self.n - self.start, self.per)
        self.n = self.start + turns * self.per
        self.i = None


def build(nc, t, o):
    ctx = ExitStack()
    with ctx:
        def sb(name, shape, dt=F32, stack=ctx):
            return stack.enter_context(nc.sbuf_tensor(name, shape, dt))

        sems = {}

        def sem(name):
            if name not in sems:
                sems[name] = ctx.enter_context(nc.semaphore(name))
            return sems[name]

        x = sb("x", [P, KT, T])
        act_hi = sb("act_hi", [P, KT, T], F32R)
        act_lo = sb("act_lo", [P, KT, T], F32R)
        raw = sb("raw", [P, 2, SLOT])
        w_hi = sb("w_hi", [P, 2, SLOT // 2], F32R)
        w_lo = sb("w_lo", [P, 2, SLOT // 2], F32R)
        aring = sb("aring", [P, 2, 4 * ADA_N])
        vec = sb("vec", [P, NVEC])
        mods = sb("mods", [P, 2 * 96, S9])
        cond = sb("cond", [P, KT, 32])
        adarow = sb("adarow", [P, ADA_N])
        ident = sb("ident", [P, P])
        ones = sb("ones", [P, P])
        sel = sb("sel", [P, S9])
        eps = sb("eps", [P, 1])
        one = sb("one", [P, 1])
        sg = sb("sg", [P, 2, T])
        prod = sb("prod", [P, T])
        sqb = sb("sqb", [P, 2, T])
        ssq = sb("ssq", [P, T])
        rstd = sb("rstd", [P, T])
        xtmp = sb("xtmp", [P, 2, NSEQ, TS])
        amod = sb("amod", [P, KT, S9])
        with ExitStack() as a:
            uext = sb("uext", [P, CT, UE], stack=a)
            z = sb("z", [P, 24, T], stack=a)
            zr = sb("zr", [16, T], stack=a)
            wgate = sb("wgate", [16, HEADS * P], stack=a)
            chunk_start = sb("chunk_start", [P, T], stack=a)
            causal64 = sb("causal64", [P, 2, 64], U32, stack=a)
            causal_s = sb("causal_s", [32, 32], U32, stack=a)
            seqmask = sb("seqmask", [32, NSEQ], stack=a)
            cacc = sb("cacc", [P, T], stack=a)
        with ExitStack() as a:
            gb = sb("gb", [P, T], stack=a)
            geb = sb("geb", [P, T], stack=a)
            gkl = sb("gkl", [P, T], stack=a)
            gs = sb("gs", [P, 4, 256], stack=a)
            vtok = sb("vtok", [P, 2, 256], stack=a)
            vtok_s = sb("vtok_s", [32, 256], stack=a)
            kltok = sb("kltok", [P, 2, P], stack=a)
            klm = sb("klm", [32, NSEQ, P], stack=a)
            att = sb("att", [P, 2, P], stack=a)
            att_s = sb("att_s", [32, 32], stack=a)
        with ExitStack() as a:
            zu = sb("zu", [P, CT, T], stack=a)
            zv = sb("zv", [P, CT, T], stack=a)
            zq = sb("zq", [P, CT, T], stack=a)
            zkv = sb("zkv", [P, 2, T], stack=a)
            dist = sb("dist", [P, 256], stack=a)
            bias_s = sb("bias_s", [P, 4, KEYS], stack=a)
            sinks = sb("sinks", [P, 16 + 4], stack=a)
            vtok1 = sb("vtok1", [P, 2, P], stack=a)
            vnew = sb("vnew", [32, P], stack=a)
            small = sb("small", [P, 6, 16], stack=a)
            qs = sb("qs", [P, NSEQ, CT, TS], stack=a)
            region1 = a.enter_context(ExitStack())
            wsp = sb("wsp", [P, 4, P], stack=region1)
            wsp_s = sb("wsp_s", [32, 4, 32], stack=region1)
            bsp = sb("bsp", [1, 4, T], stack=region1)
            vmix = sb("vmix", [P, 2, 256], stack=region1)
            vmix_s = sb("vmix_s", [32, 256], stack=region1)
            region1.close()
            kcache = sb("kcache", [P, NSEQ, P], stack=a)
            vcache = sb("vcache", [P, NSEQ, P], stack=a)
            ptp = sb("ptp", [P, 2, 512], stack=a)
        with ExitStack() as a:
            sc = sb("sc", [P, 16, 256], stack=a)
        with ExitStack() as a:
            hid_hi = sb("hid_hi", [P, BLK, T], F32R, stack=a)
            hid_lo = sb("hid_lo", [P, BLK, T], F32R, stack=a)
        with ExitStack() as a:
            tn = sb("tn", [P, 2, 4, T], stack=a)
        sb("region", [P, 51712 // 4])
        ps = ctx.enter_context(nc.psum_tensor("ps", [P, 8, 512], F32))
        ADA_BANK, LA_BANK, SEL_BANK, MEAN_BANK, STAT_BANK, M_BANK = 4, 4, 5, 5, 6, 7

        weights_landed = [sem("weights_landed0"), sem("weights_landed1")]
        ada_landed = [sem("ada_landed0"), sem("ada_landed1")]
        y_stored = [sem("y_stored0"), sem("y_stored1")]
        (act_links, act_ready, ada_biased, ada_cols, ada_rows, ada_used, att_ready, att_turned, b_ready,
         cache_stored, centred, cond_landed, cond_log, cond_ready, cond_sig, cond_terms, consts_landed,
         conv_log, conv_ready, conv_sig, conv_stored, conv_terms, conv_y, drained, dve_links, e_ready, exps,
         gelu_arg, gelu_sq, gla_rs, gla_y, gla_yy, gsig_log, gsig_ready, gsig_terms, gstate_stored,
         half_done, hi_done, hid_hi_done, hid_ready, history_landed, history_zero, kl_ready, kl_turned,
         kv_landed, la_ready, la_terms, mean_ready, mean_used, mix0_consts, mix1_consts, mixed_ready,
         mixhi_done, ms_ready, nhi_done, normed, ones_set, os_ready, osq_ready, pool_links, probs_ready,
         probs_s_ready, pt_ready, pt_turned, pts_ready, pts_turned, pv_done, qk_ready, qs_ready, row_max,
         rstd_ready, s_chain, sadd_ready, scored, scores_ready, scores_s_ready, sgu_mixed, sguv_stored,
         sig_log, sig_ready, sig_terms, sink_exp, snew_ready, snew_used, split_done, sq_added, sq_ready,
         stat_ready, state_stored, tn_ready, tn_samples, tok_ready, v_ln, v_turned, vmix_ready, vmix_turned,
         vtok1_ready, vtok1_turned, wsp_ready, x_landed, x_updated, y_ready, yd_ready) = (
            sem(name) for name in (
                "act_links", "act_ready", "ada_biased", "ada_cols", "ada_rows", "ada_used", "att_ready",
                "att_turned", "b_ready", "cache_stored", "centred", "cond_landed", "cond_log", "cond_ready",
                "cond_sig", "cond_terms", "consts_landed", "conv_log", "conv_ready", "conv_sig", "conv_stored",
                "conv_terms", "conv_y", "drained", "dve_links", "e_ready", "exps", "gelu_arg", "gelu_sq", "gla_rs",
                "gla_y", "gla_yy", "gsig_log", "gsig_ready", "gsig_terms", "gstate_stored", "half_done", "hi_done",
                "hid_hi_done", "hid_ready", "history_landed", "history_zero", "kl_ready", "kl_turned", "kv_landed",
                "la_ready", "la_terms", "mean_ready", "mean_used", "mix0_consts", "mix1_consts", "mixed_ready",
                "mixhi_done", "ms_ready", "nhi_done", "normed", "ones_set", "os_ready", "osq_ready", "pool_links",
                "probs_ready", "probs_s_ready", "pt_ready", "pt_turned", "pts_ready", "pts_turned", "pv_done",
                "qk_ready", "qs_ready", "row_max", "rstd_ready", "s_chain", "sadd_ready", "scored", "scores_ready",
                "scores_s_ready", "sgu_mixed", "sguv_stored", "sig_log", "sig_ready", "sig_terms", "sink_exp",
                "snew_ready", "snew_used", "split_done", "sq_added", "sq_ready", "stat_ready", "state_stored",
                "tn_ready", "tn_samples", "tok_ready", "v_ln", "v_turned", "vmix_ready", "vmix_turned",
                "vtok1_ready", "vtok1_turned", "wsp_ready", "x_landed", "x_updated", "y_ready", "yd_ready"))
        src = {"zr": t["w_zr"], "gate": t["w_ab"], "zconv": t["w_ab"], "z": t["w_ab"], "kv": t["w_cd"],
               "q": t["w_cd"], "sgu": t["w_cd"], "out": t["w_out"], "gu": t["w_gu"], "down": t["w_dn"]}
        LAYER_STEPS = {"out": KT // 2, "gu": FF_T, "down": 2 * KT}

        def flat(ap):
            return ap.rearrange("p a n -> p (a n)")

        def at(buf, j, lo=0, hi=None):
            hi = buf.shape[-1] if hi is None else hi
            return flat(buf[:, bass.ds(j, 1), lo:hi])

        def seqs(ap):
            return ap.rearrange("p (b t) -> p b t", t=TS)

        def flat_at(buf, j):
            return buf[:, bass.ds(j, 1)]

        def rows_s(j):
            return at(uext, j, UW, UE).rearrange("p (b w) -> p b w", w=SW)

        def taps_s(j, k):
            return rows_s(j)[:, :, k:k + TS]

        y_all = uext[:, :, 0:NP_TOK]
        y_all_s = uext[:, :, UW:UE].rearrange("p c (b w) -> p c b w", w=SW)[:, :, :, 0:TS]

        def unit_uses(u):
            return lin(u[0], 4, 4 * u[1] + (HEADS if u[1] >= 18 else 0))

        def first_unit(u):
            return u[0] is None and u[1] == 0

        def unit_no(u):
            return lin(u[0], 1, u[1])

        def steps_of(seg, i, base):
            for j in range(seg.m):
                k = seg.m * base + j
                yield lin(i, seg.m, seg.n0 + k), (seg.n0 + k) % 2, lin(i, seg.m, k)

        block = ctx.enter_context(nc.Block())

        @block.sync
        def _(sp):
            def load_step(seg, n, par, ls):
                if not (isinstance(n, int) and n < 2):
                    sp.wait_ge(split_done, n * 2 - 2)
                rows = src[seg.kind][bass.ds(ls + (seg.first + seg.layer * LAYER_STEPS.get(seg.kind, 0)), 1)]
                sp.dma_start(raw[:, par, 0:seg.width], rows.rearrange("a p n -> p (a n)")) \
                    .then_inc(weights_landed[par], 16)

            def load_ada(u, s):
                if not (first_unit(u) and s < 2):
                    sp.wait_ge(ada_used, unit_no(u) * 4 + (s - 1))
                rows = t["w_ada"][bass.ds(unit_no(u) * 4 + s, 1)]
                sp.dma_start(aring[:, s % 2, :], rows.rearrange("a p n -> p (a n)")) \
                    .then_inc(ada_landed[s % 2], 16)

            def body(seg, i, base, last=False):
                for j, (n, par, ls) in enumerate(steps_of(seg, i, base)):
                    if not (last and j == seg.m - 1):
                        load_step(seg, n + 1, 1 - par, ls + 1)
                    elif seg.next:
                        load_step(seg.next, n + 1, 1 - par, 0)
                    if seg.unit is not None:
                        load_ada((i, seg.unit + base), 2 * j)
                        load_ada((i, seg.unit + base), 2 * j + 1)

            def mix0():
                sp.wait_ge(conv_ready, CT)
                sp.dma_start(o["conv_p"], uext[:, :, NP_TOK:UW]).then_inc(conv_stored, 16)
                for j in range(CT):
                    sp.dma_start(o["conv_s"][:, j], rows_s(j)[:, :, TS:SW]).then_inc(conv_stored, 16)
                for h in range(HEADS):
                    if h < 2:
                        sp.wait_ge(ada_used, GLA_A + h - 1)
                    else:
                        sp.wait_ge(state_stored, 16 * (h - 1))
                    sp.dma_start(aring[:, h % 2, :], t["state_glaT"][h]).then_inc(ada_landed[h % 2], 16)
                    if h >= 1:
                        store_states(h - 1)
                store_states(HEADS - 1)
                sp.wait_ge(state_stored, 16 * HEADS)

            def store_states(h):
                sp.wait_ge(s_chain, h + 1)
                sp.dma_start(o["gla_p"][h], gs[:, 3, :]).then_inc(gstate_stored, 16)
                sp.wait_ge(snew_used, 2 * h + 2)
                sp.dma_start(o["gla_s"][h], aring[:, h % 2, :]).then_inc(state_stored, 16)

            def mix1():
                sp.wait_ge(sgu_mixed, CT)
                sp.dma_start(kcache[:], t["cache_kT"]).then_inc(kv_landed, 16)
                sp.dma_start(vcache[:], t["cache_vT"]).then_inc(kv_landed, 16)
                sp.dma_start(o["sgu_v"], zv[:, :, NP_TOK:T]).then_inc(sguv_stored, 16)
                sp.dma_start(o["k_p"], zkv[:, 0, P:NP_TOK]).then_inc(cache_stored, 16)
                sp.dma_start(o["k_s_new"], zkv[:, 0, NP_TOK:T]).then_inc(cache_stored, 16)
                sp.wait_ge(vtok1_ready, 1)
                sp.dma_start(o["v_p"], vtok1[:, 1, :]).then_inc(cache_stored, 16)
                sp.dma_start(o["v_s_new"], vnew[:]).then_inc(cache_stored, 16)
                sp.wait_ge(kv_landed, 32)
                sp.dma_start(o["k_s_old"], kcache[:, :, TS:P]).then_inc(cache_stored, 16)
                sp.dma_start(o["v_s_old"], vcache[TS:P]).then_inc(cache_stored, 16)

            sp.dma_start(cond[:, :, 0:S9], t["cT"]).then_inc(cond_landed, 16)
            sp.dma_start(sel[:], t["sel"]).then_inc(consts_landed, 16)
            sp.dma_start(vec[:], t["vec"]).then_inc(consts_landed, 16)
            sp.dma_start(ident[:], t["ident"]).then_inc(consts_landed, 16)
            for s in range(4):
                load_ada((None, 0), s)
                if s == 1:
                    sp.dma_start(x[:], t["xT"]).then_inc(x_landed, 16)
            with sp.Fori(0, 7) as i:
                for s in range(4):
                    load_ada((i, 1), s)
            load_step(SEGS[0], 0, 0, 0)
            sp.wait_ge(act_ready, KT)
            for name, place in (("gla_w_gate", wgate), ("chunk_start", chunk_start), ("causal64", causal64),
                                ("causal_s", causal_s), ("seqmask", seqmask)):
                sp.dma_start(place[:], t[name]).then_inc(mix0_consts, 16)
            for j in range(CT):
                sp.dma_start(rows_s(j)[:, :, 0:HIST], t["state_convT"][:, j]).then_inc(history_landed, 16)
            for seg in PLAN:
                if seg == "mix0":
                    mix0()
                elif seg == "mix1":
                    mix1()
                elif seg != "norm":
                    if seg.kind == "kv":
                        sp.wait_ge(act_ready, 4 * KT)
                        for name, place in (("dist", dist), ("bias_s", bias_s), ("sinks", sinks), ("sgu_wT", wsp),
                                            ("sgu_wsT", wsp_s), ("sgu_bT", bsp)):
                            sp.dma_start(place[:], t[name]).then_inc(mix1_consts, 16)
                    if seg.bodies == 2:
                        body(seg, None, 0)
                    elif seg.bodies > 2:
                        with sp.Fori(0, seg.bodies - 1) as i:
                            body(seg, i, 0)
                    body(seg, None, seg.bodies - 1, last=True)
            for g in range(4):
                sp.wait_ge(y_ready, g + 1)
                sp.dma_start(o["y"][:, 4 * g:4 * g + 4, :], tn[:, g % 2]).then_inc(y_stored[g % 2], 16)
            for stored in y_stored:
                sp.wait_ge(stored, 32)
            sp.wait_ge(conv_stored, 16 * (CT + 1))
            sp.wait_ge(gstate_stored, 16 * HEADS)
            sp.wait_ge(cache_stored, 16 * 6)
            sp.wait_ge(sguv_stored, 16)

        @block.gpsimd
        def _(pool):
            L = Links(pool, pool_links)
            pool.memset(ones[:], 1.0).then_inc(ones_set, 1)
            pool.memset(eps[:], EPS).then_inc(ones_set, 1)
            pool.memset(one[:], 1.0).then_inc(ones_set, 1)
            pool.memset(cond[:, :, S9:32], 0.0).then_inc(ones_set, 1)

            def sum_squares(n, q):
                for k in range(n):
                    pool.wait_ge(sq_ready, q + k + 1)
                    if k == 0:
                        if q:
                            pool.wait_ge(stat_ready, SQUARES.index(q))
                        pool.tensor_copy(ssq[:], sqb[:, (q + k) % 2]).then_inc(sq_added, 1)
                    else:
                        pool.wait_ge(sq_added, q + k)
                        pool.tensor_tensor(ssq[:], ssq[:], sqb[:, (q + k) % 2], ALU.add).then_inc(sq_added, 1)

            sum_squares(KT, 0)
            pool.wait_ge(act_ready, KT)
            pool.memset(uext[:, :, 0:HIST], 0.0).then_inc(history_zero, 1)
            sum_squares(CT, 16)
            sum_squares(KT, 24)
            sum_squares(KT, 40)
            pool.wait_ge(mix1_consts, 16 * 6)
            pool.affine_select(out=wsp[:], in_=wsp[:], pattern=[[0, 4], [1, P]], compare_op=ALU.is_ge, fill=0.0,
                               base=0, channel_multiplier=-1).then_inc(wsp_ready, 1)
            L.link(pool.affine_select(out=wsp_s[:], in_=wsp_s[:], pattern=[[0, 4], [1, 32]], compare_op=ALU.is_ge,
                                      fill=0.0, base=0, channel_multiplier=-1))
            pool.affine_select(out=wsp_s[:], in_=wsp_s[:], pattern=[[0, 4], [-TS, NSEQ], [0, TS]],
                               compare_op=ALU.is_ge, fill=0.0, base=0, channel_multiplier=1).then_inc(wsp_ready, 1)
            sum_squares(CT, 56)
            sum_squares(KT, 64)
            sum_squares(KT, 80)

        @block.tensor
        def _(pe):
            sets = [0]
            stats = [0]

            def half(seg, n, par, h, first):
                if h == 0 and not (isinstance(n, int) and n < 2):
                    pe.wait_ge(drained, n - 1)
                pe.wait_ge(split_done, n * 2 + (h + 1))
                hi, lo = (hid_hi, hid_lo) if seg.kind == "down" else (act_hi, act_lo)
                bank = ps[:, 2 * par + (h if seg.two else 0), 0:T]
                for k in range(seg.ktiles):
                    kt = k if seg.two else h * seg.ktiles + k
                    if first and kt % 4 == 0 and (h == 0 or not seg.two):
                        pe.wait_ge(act_ready, sets[0] * KT + kt + 4)
                    cols = slice(k * P, (k + 1) * P)
                    begin = k == 0 and (seg.two or h == 0)
                    end = k == seg.ktiles - 1 and (seg.two or h == 1)
                    pe.matmul(bank, w_hi[:, h, cols], hi[:, kt, :], start=begin, stop=False)
                    pe.matmul(bank, w_lo[:, h, cols], hi[:, kt, :], start=False, stop=False)
                    mm = pe.matmul(bank, w_hi[:, h, cols], lo[:, kt, :], start=False, stop=end)
                mm.then_inc(half_done, 1)

            def ada_slot(u, s):
                pe.wait_ge(ada_landed[s % 2], (unit_uses(u) + (s - s % 2)) * 8 + 16)
                if s == 0 and not first_unit(u):
                    pe.wait_ge(ada_rows, unit_no(u))
                for j in range(4):
                    mm = pe.matmul(ps[32 * j:32 * j + 32, ADA_BANK, :], cond[:, 4 * s + j, :],
                                   aring[:, s % 2, j * ADA_N:(j + 1) * ADA_N], start=(s == 0), stop=(s == 3))
                mm.then_inc(ada_used, 1)

            def ada_turn(u):
                pe.wait_ge(ada_rows, unit_no(u) + 1)
                if not first_unit(u):
                    pe.wait_ge(ada_biased, unit_no(u))
                for q in range(4):
                    mm = pe.matmul(ps[:, SEL_BANK, 16 * q:16 * q + S9], adarow[:, q * P:(q + 1) * P], sel[:],
                                   start=True, stop=True)
                mm.then_inc(ada_cols, 1)

            def stat():
                k = stats[0]
                pe.wait_ge(sq_added, SQUARES[k + 1])
                if k:
                    pe.wait_ge(rstd_ready, k)
                pe.matmul(ps[:, STAT_BANK, 0:T], ones[:], ssq[:], start=True, stop=True).then_inc(stat_ready, 1)
                stats[0] += 1

            def body(seg, i, base, first=False):
                for j, (n, par, _) in enumerate(steps_of(seg, i, base)):
                    u = None if seg.unit is None else (i, seg.unit + base)
                    half(seg, n, par, 0, first and j == 0)
                    if u and j == 0:
                        ada_slot(u, 0)
                    if u and j == 1:
                        ada_slot(u, 2)
                        ada_slot(u, 3)
                    half(seg, n, par, 1, first and j == 0)
                    if u and j == 0:
                        ada_slot(u, 1)
                    if u and j == 1:
                        ada_turn(u)

            def mix0():
                pe.wait_ge(conv_ready, CT)
                pe.wait_ge(ada_biased, 18)
                for j in range(CT):
                    pe.matmul(ps[:, MEAN_BANK, 0:NP_TOK], ones[:], y_all[:, j], start=(j == 0), stop=(j == CT - 1))
                for j in range(CT):
                    mm = pe.matmul(ps[:, MEAN_BANK, NP_TOK:T], ones[:], y_all_s[:, j], start=(j == 0), stop=(j == CT - 1))
                mm.then_inc(mean_ready, 1)
                stat()
                pe.wait_ge(mix0_consts, 16 * 5)
                pe.wait_ge(drained, Z_SEG.n0 + Z_SEG.steps)
                pe.wait_ge(rstd_ready, 2)
                for h in range(HEADS):
                    if h:
                        pe.wait_ge(gla_rs, h)
                    pe.matmul(ps[:, LA_BANK, 0:T], wgate[:, h * P:(h + 1) * P], zr[:], start=True, stop=True) \
                        .then_inc(la_ready, 1)
                    if h:
                        pe.wait_ge(tok_ready, 3 * h)
                        pe.wait_ge(att_ready, h)
                    else:
                        pe.wait_ge(mean_used, 1)
                    v = [z[:, 8 + 2 * h + b, :] for b in range(2)]
                    for b in range(2):
                        for c in range(2):
                            pe.transpose(ps[:, 5, (2 * c + b) * P:(2 * c + b + 1) * P], v[b][:, c * P:(c + 1) * P], ident[:])
                        mm = pe.transpose(ps[0:32, 6, 256 + b * P:256 + (b + 1) * P], v[b][:, NP_TOK:T], ident[:])
                    mm.then_inc(v_turned, 1)
                    pe.wait_ge(kl_ready, h + 1)
                    pe.wait_ge(tok_ready, 3 * h + 1)
                    for c in range(2):
                        pe.transpose(ps[:, 6, c * P:(c + 1) * P], gkl[:, c * P:(c + 1) * P], ident[:])
                    pe.transpose(ps[0:32, 7, 0:P], gkl[:, NP_TOK:T], ident[:]).then_inc(kl_turned, 1)
                    pe.wait_ge(qk_ready, h + 1)
                    q, k = z[:, 2 * h, :], z[:, 2 * h + 1, :]
                    for c in range(4):
                        cs = slice(64 * c, 64 * c + 64)
                        pe.matmul(ps[64 * (c % 2):64 * (c % 2) + 64, 4, 64 * (c // 2):64 * (c // 2) + 64],
                                  k[:, cs], q[:, cs], start=True, stop=True)
                    pe.matmul(ps[0:32, 4, P:P + 32], k[:, NP_TOK:T], q[:, NP_TOK:T], start=True, stop=True) \
                        .then_inc(att_turned, 1)
                    pe.wait_ge(tok_ready, 3 * h + 3)
                    if h:
                        pe.wait_ge(snew_used, 2 * h)
                    for c in range(4):
                        rows = slice(64 * (c % 2), 64 * (c % 2) + 64)
                        mm = pe.matmul(ps[:, c % 2, 256 * (c // 2):256 * (c // 2) + 256], kltok[rows, c // 2, :],
                                       vtok[rows, c // 2, :], start=True, stop=True)
                    mm.then_inc(sadd_ready, 1)
                    pe.wait_ge(att_ready, h + 1)
                    pe.wait_ge(s_chain, h + 1)
                    pe.wait_ge(ada_landed[h % 2], 16 * ((GLA_A + h) // 2 + 1))
                    if h:
                        pe.wait_ge(gla_y, h)
                    for b in range(2):
                        vs = slice(b * P, (b + 1) * P)
                        for c in range(4):
                            if c % 2 == 0:
                                pe.matmul(ps[:, 2 + b, 64 * c:64 * c + P], vtok[:, c // 2, vs], att[:, c // 2, :],
                                          start=True, stop=False, skip_group_check=True)
                            if c:
                                pe.matmul(ps[:, 2 + b, 64 * c:64 * c + 64], gs[:, c - 1, vs], q[:, 64 * c:64 * c + 64],
                                          start=False, stop=True, skip_group_check=True)
                        pe.matmul(ps[:, 2 + b, NP_TOK:T], vtok_s[:, vs], att_s[:], start=True, stop=False)
                        for s in range(NSEQ):
                            cols = slice(NP_TOK + TS * s, NP_TOK + TS * s + TS)
                            mm = pe.matmul(ps[:, 2 + b, cols], aring[:, h % 2, 256 * s + b * P:256 * s + (b + 1) * P],
                                           q[:, cols], start=False, stop=(s == NSEQ - 1))
                    mm.then_inc(gla_yy, 1)
                    for r in range(2):
                        if r:
                            pe.wait_ge(snew_used, 2 * h + 1)
                        for s in range(4):
                            mm = pe.matmul(ps[:, s // 2, 256 * (s % 2):256 * (s % 2) + 256], klm[:, 4 * r + s, :],
                                           vtok_s[:], start=True, stop=True)
                        mm.then_inc(snew_ready, 1)
                        if r:
                            pe.wait_ge(osq_ready, h + 1)
                    for b in range(2):
                        mm = pe.matmul(ps[:, 4, 0:T], ones[:], sqb[:, b], start=(b == 0), stop=(b == 1))
                    mm.then_inc(ms_ready, 1)
                pe.wait_ge(snew_used, 2 * HEADS)
                pe.wait_ge(gla_y, HEADS)
                pe.wait_ge(gla_rs, HEADS)

            def mix1():
                pe.wait_ge(drained, SGU_SEG.n0 + SGU_SEG.steps)
                for j in range(CT):
                    mm = pe.matmul(ps[:, MEAN_BANK, 0:T], ones[:], zv[:, j, :], start=(j == 0), stop=(j == CT - 1))
                mm.then_inc(mean_ready, 1)
                stat()
                pe.wait_ge(mix1_consts, 16 * 6)
                pe.wait_ge(wsp_ready, 2)
                pe.wait_ge(mean_used, 2)
                pe.wait_ge(rstd_ready, stats[0])
                for g in range(4):
                    pe.wait_ge(v_ln, 2 * g + 2)
                    if g:
                        pe.wait_ge(vmix_ready, g)
                    for b in range(2):
                        for c in range(2):
                            pe.transpose(ps[:, 5, (2 * c + b) * P:(2 * c + b + 1) * P], zv[:, 2 * g + b, c * P:(c + 1) * P], ident[:])
                        mm = pe.transpose(ps[0:32, 6, b * P:(b + 1) * P], zv[:, 2 * g + b, NP_TOK:T], ident[:])
                    mm.then_inc(vmix_turned, 1)
                    pe.wait_ge(vmix_ready, g + 1)
                    for b in range(2):
                        if g:
                            pe.wait_ge(sgu_mixed, 2 * g + b - 1)
                        bank = ps[:, b, 0:T]
                        vs = slice(b * P, (b + 1) * P)
                        pe.matmul(bank, ones[0:1, :], bsp[0:1, g, :], start=True, stop=False)
                        for c in range(2):
                            pe.matmul(bank[:, c * P:(c + 1) * P], vmix[:, c, vs], wsp[:, g, :], start=False, stop=False)
                        pe.matmul(bank[:, NP_TOK:T], vmix_s[:, vs], wsp_s[:, g, :], start=False, stop=True) \
                            .then_inc(mixed_ready, 1)
                pe.wait_ge(vmix_ready, 4)
                for c in range(2):
                    pe.transpose(ps[:, 5, c * P:(c + 1) * P], zkv[:, 1, c * P:(c + 1) * P], ident[:])
                pe.transpose(ps[0:32, 5, 256:384], zkv[:, 1, NP_TOK:T], ident[:]).then_inc(vtok1_turned, 1)
                for blk in range(2):
                    k0 = 0 if blk else P
                    for h in range(16):
                        g, r = h // 8, h % 8
                        gp = slice(64 * g, 64 * g + 64)
                        if 16 * blk + h >= 4:
                            pe.wait_ge(scored, 16 * blk + h - 3)
                        elif h < 2:
                            pe.wait_ge(sgu_mixed, CT)
                        if blk and h == 2:
                            pe.wait_ge(yd_ready, 1)
                        pe.matmul(ps[:, h % 4, k0:256], zq[gp, r, blk * P:(blk + 1) * P],
                                  zkv[gp, 0, blk * P - P + k0:(blk + 1) * P], start=True, stop=True).then_inc(scores_ready, 1)
                    pe.wait_ge(vtok1_ready, 1)
                    for h in range(16):
                        g, r = h // 8, h % 8
                        turn = 16 * blk + h
                        pe.wait_ge(probs_ready, turn + 1)
                        if turn >= 2:
                            pe.wait_ge(pt_ready, turn - 1)
                        for kb in range(1 - blk, 2):
                            mm = pe.transpose(ps[:, 6 + turn % 2, kb * P:(kb + 1) * P], sc[:, h, kb * P:(kb + 1) * P], ident[:])
                        mm.then_inc(pt_turned, 1)
                        pe.wait_ge(pt_ready, turn + 1)
                        if h == 0:
                            pe.wait_ge(scored, 16 * blk + 16)
                        for kb in range(1 - blk, 2):
                            mm = pe.matmul(ps[64 * g:64 * g + 64, 2 + r // 4, (r % 4) * P:(r % 4 + 1) * P],
                                           vtok1[:, blk - 1 + kb, 64 * g:64 * g + 64], ptp[:, turn % 2, kb * P:(kb + 1) * P],
                                           start=(kb == 1 - blk), stop=(kb == 1))
                        mm.then_inc(pv_done, 1)
                pe.wait_ge(kv_landed, 32)
                pe.wait_ge(qs_ready, 1)
                pe.wait_ge(yd_ready, 2)
                for s in range(NSEQ):
                    for g in range(2):
                        gp = slice(64 * g, 64 * g + 64)
                        out = ps[32 * (s % 4):32 * (s % 4) + 32, 2 * (s // 4) + g, 0:KEYS]
                        rows = qs[gp, s].rearrange("p r t -> p (r t)")
                        pe.matmul(out[:, 0:P], rows, kcache[gp, s, :], start=True, stop=True)
                        mm = pe.matmul(out[:, P:KEYS], rows, zkv[gp, 0, NP_TOK:T], start=True, stop=True)
                mm.then_inc(scores_s_ready, 1)
                pe.wait_ge(probs_s_ready, 1)
                for c in range(4):
                    pe.transpose(ps[:, 4, c * P:(c + 1) * P], sc[:, c, 0:P], ident[:])
                for c in range(4):
                    mm = pe.transpose(ps[0:32, 5, c * P:(c + 1) * P], sc[:, c, P:KEYS], ident[:])
                mm.then_inc(pts_turned, 1)
                pe.wait_ge(pts_ready, 1)
                for s in range(NSEQ):
                    for g in range(2):
                        c = 2 * (s // 4) + g
                        out = ps[64 * g:64 * g + 64, 0, 32 * s:32 * s + 32]
                        cols = slice(c * P + 32 * (s % 4), c * P + 32 * (s % 4) + 32)
                        pe.matmul(out, vcache[:, s, 64 * g:64 * g + 64], ptp[:, 0, cols], start=True, stop=False)
                        mm = pe.matmul(out, vnew[:, 64 * g:64 * g + 64], ptp[0:32, 1, cols], start=False, stop=True)
                mm.then_inc(os_ready, 1)
                pe.wait_ge(act_ready, KT * (sets[0] + 1))

            pe.wait_ge(consts_landed, 48)
            pe.wait_ge(cond_ready, 1)
            pe.wait_ge(ones_set, 4)
            for s in range(4):
                ada_slot((None, 0), s)
            ada_turn((None, 0))
            with pe.Fori(0, 7) as i:
                for s in range(4):
                    ada_slot((i, 1), s)
                ada_turn((i, 1))
            stat()
            fresh, blocks = True, 0
            for seg in PLAN:
                if seg in ("norm", "mix0", "mix1"):
                    {"norm": stat, "mix0": mix0, "mix1": mix1}[seg]()
                    fresh = True
                    continue
                if seg.kind == "down":
                    blocks += 1
                    pe.wait_ge(hid_ready, BLK * blocks)
                start = 0
                if fresh and seg.kind != "down":
                    body(seg, None, 0, first=True)
                    start = 1
                    sets[0] += 1
                    fresh = False
                if seg.bodies > start:
                    if seg.bodies - start > 1:
                        with pe.Fori(0, seg.bodies - start) as i:
                            body(seg, i, start)
                    else:
                        body(seg, None, start)

        @block.scalar
        def _(act):
            L = Links(act, act_links)
            sums = [0]

            def split(seg, n, par, h):
                act.wait_ge(weights_landed[par], (n - par) * 8 + 16)
                if not (isinstance(n, int) and n == 0):
                    act.wait_ge(half_done, n * 2 + (h - 1))
                w = seg.width // 2
                act.activation(w_hi[:, h, 0:w], raw[:, par, h * w:(h + 1) * w], ACT.Copy).then_inc(hi_done, 1)

            def log_terms(out, in_, scale=1.0, bias=0.0):
                L.link(act.activation(out, in_, ACT.Abs, scale=scale, bias=bias))
                L.link(act.activation(out, out, ACT.Exp, scale=-1.0))
                return act.activation(out, out, ACT.Ln, bias=one[0:out.shape[0], :])

            def make_rstd(n, bank=STAT_BANK):
                L.link(act.activation(rstd[:], ps[:, bank, 0:T], ACT.Ln, scale=1.0 / n, bias=eps[:]))
                return act.activation(rstd[:], rstd[:], ACT.Exp, scale=-0.5)

            def stat_rstd(n):
                sums[0] += 1
                act.wait_ge(stat_ready, sums[0])
                make_rstd(n).then_inc(rstd_ready, 1)

            def wait_square(q):
                if not (isinstance(q, int) and q < 2):
                    act.wait_ge(sq_added, q - 1)

            def epilogue(seg, n, par, ls):
                b0, b1 = ps[:, 2 * par, 0:T], ps[:, 2 * par + 1, 0:T]
                act.wait_ge(half_done, n * 2 + 2)
                if seg.kind != "zr":
                    act.wait_ge(drained, n)
                if seg.kind == "zr":
                    act.activation(zr[:], ps[0:16, 2 * par, 0:T], ACT.Copy).then_inc(drained, 1)
                elif seg.kind in ("zconv", "z"):
                    act.activation(at(z, ls * 2 + seg.group), b0, ACT.Copy)
                    act.activation(at(z, ls * 2 + (seg.group + 1)), b1, ACT.Copy).then_inc(drained, 1)
                elif seg.kind == "kv":
                    act.activation(zkv[:, 0, :], b0, ACT.Copy)
                    act.activation(zkv[:, 1, :], b1, ACT.Copy).then_inc(drained, 1)
                elif seg.kind == "q":
                    act.activation(at(zq, ls * 2), b0, ACT.Copy, scale=0.125)
                    act.activation(at(zq, ls * 2 + 1), b1, ACT.Copy, scale=0.125).then_inc(drained, 1)
                elif seg.kind in ("gate", "gu"):
                    k = ls + seg.sig0
                    log_terms(sg[:, 0], b1 if seg.kind == "gate" else b0).then_inc(sig_terms, 1)
                    act.wait_ge(sig_log, k + 1)
                    act.activation(sg[:, 0], sg[:, 0], ACT.Exp).then_inc(sig_ready, 1)
                    if seg.kind == "gu":
                        act.wait_ge(drained, n + 1)
                        act.activation(at(hid_hi, ls + seg.first % BLK), prod[:], ACT.Copy).then_inc(hid_hi_done, 1)
                elif seg.kind == "sgu":
                    for b, bank in enumerate((b0, b1)):
                        act.activation(sqb[:, b], bank, ACT.Square, scale=GELU_K ** 0.5).then_inc(gelu_sq, 1)
                    for b in range(2):
                        act.wait_ge(gelu_arg, ls * 2 + (seg.gel0 + b + 1))
                        log_terms(sg[:, b], sqb[:, b]).then_inc(sig_terms, 1)
                    for b in range(2):
                        act.wait_ge(sig_log, ls * 2 + (seg.sig0 + b + 1))
                        act.activation(sg[:, b], sg[:, b], ACT.Exp).then_inc(sig_ready, 1)
                elif seg.kind == "out" or seg.group:
                    for b in range(2 if seg.two else 1):
                        j = ls * 2 + b if seg.two else ls
                        act.wait_ge(x_updated, j + (seg.x0 + 1))
                        q = j + seg.q0
                        wait_square(q)
                        act.activation(sqb[:, b if seg.two else (seg.q0 + par + seg.n0) % 2], at(x, j), ACT.Square).then_inc(sq_ready, 1)

            def ada_copy(u):
                act.wait_ge(ada_used, unit_no(u) * 4 + 4)
                if not first_unit(u):
                    act.wait_ge(ada_cols, unit_no(u))
                act.activation(adarow[:], ps[:, ADA_BANK, :], ACT.Copy).then_inc(ada_rows, 1)

            def body(seg, i, base, last=False):
                for j, (n, par, ls) in enumerate(steps_of(seg, i, base)):
                    end = last and j == seg.m - 1
                    nxt = seg.next if end else seg
                    hurry = end and seg.then_wait
                    if nxt:
                        split(nxt, n + 1, 1 - par, 0)
                    if seg.unit is not None and j == 1:
                        ada_copy((i, seg.unit + base))
                    if nxt and not hurry:
                        split(nxt, n + 1, 1 - par, 1)
                    epilogue(seg, n, par, ls)
                    if nxt and hurry:
                        split(nxt, n + 1, 1 - par, 1)

            def norm(k, final=False):
                stat_rstd(D)
                layer, part = divmod(k, 2)
                shift = layer * 96 + part * 48
                for g in range(4):
                    act.wait_ge(tn_ready, 4 * k + g + 1)
                    for b in range(4):
                        j = 4 * g + b
                        if final:
                            ins = act.activation(tn[:, g % 2, b, :], tn[:, g % 2, b, :], ACT.Copy,
                                                 scale=vec[:, VEC["g_final"] + j:VEC["g_final"] + j + 1])
                        else:
                            ins = act.activation(tn[:, g % 2, b, 0:NP_TOK], tn[:, g % 2, b, 0:NP_TOK], ACT.Identity,
                                                 scale=amod[:, j, 0:1], bias=mods[:, shift + j, 0:1])
                    if final:
                        ins.then_inc(y_ready, 1)
                        continue
                    L.link(ins)
                    act.wait_ge(tn_samples, 4 * k + g + 1)
                    act.activation(act_hi[:, 4 * g:4 * g + 4, :], tn[:, g % 2], ACT.Copy).then_inc(nhi_done, 1)

            def mix0():
                act.wait_ge(centred, 1)
                for j in range(CT):
                    q = 16 + j
                    wait_square(q)
                    act.activation(sqb[:, q % 2, 0:NP_TOK], y_all[:, j], ACT.Square)
                    act.activation(seqs(sqb[:, q % 2, NP_TOK:T]), y_all_s[:, j], ACT.Square).then_inc(sq_ready, 1)
                stat_rstd(CT * P)
                act.wait_ge(normed, 1)
                for j in range(CT + 1):
                    if j < CT:
                        if j >= 2:
                            act.wait_ge(act_ready, KT + j - 1)
                        gj, bj = VEC["conv_ln_g"] + j, VEC["conv_ln_b"] + j
                        act.activation(sqb[:, j % 2, 0:NP_TOK], y_all[:, j], ACT.Identity, scale=vec[:, gj:gj + 1],
                                       bias=vec[:, bj:bj + 1])
                        L.link(act.activation(seqs(sqb[:, j % 2, NP_TOK:T]), y_all_s[:, j], ACT.Identity,
                                              scale=vec[:, gj:gj + 1], bias=vec[:, bj:bj + 1]))
                        log_terms(sg[:, j % 2], sqb[:, j % 2]).then_inc(conv_terms, 1)
                    if j:
                        act.wait_ge(conv_log, j)
                        act.activation(sg[:, (j - 1) % 2], sg[:, (j - 1) % 2], ACT.Exp).then_inc(conv_sig, 1)
                        act.wait_ge(conv_y, j)
                        act.activation(act_hi[:, j - 1, :], sqb[:, (j - 1) % 2], ACT.Copy).then_inc(mixhi_done, 1)
                act.wait_ge(act_ready, KT + CT)
                act.wait_ge(conv_stored, 16 * (CT + 1))
                for h in range(HEADS):
                    act.wait_ge(la_ready, h + 1)
                    if h:
                        act.wait_ge(act_ready, KT + CT + 2 * h)
                    bg = VEC["gla_b_gate"] + h
                    log_terms(sg[:, 0], ps[:, LA_BANK, 0:T], bias=vec[:, bg:bg + 1]).then_inc(la_terms, 1)
                    act.wait_ge(v_turned, h + 1)
                    act.activation(vtok[:].rearrange("p c n -> p (c n)"), ps[:, 5, :], ACT.Copy)
                    act.activation(vtok_s[:], ps[0:32, 6, 256:512], ACT.Copy).then_inc(tok_ready, 1)
                    act.wait_ge(b_ready, h + 1)
                    act.activation(geb[:], gb[:], ACT.Exp, scale=1.0 / 16)
                    act.activation(prod[:], gb[:], ACT.Exp, scale=-1.0 / 16)
                    act.activation(sg[:, 0], sg[:, 0], ACT.Exp, scale=1.0 / 16).then_inc(e_ready, 1)
                    act.wait_ge(kl_turned, h + 1)
                    act.activation(kltok[:].rearrange("p c n -> p (c n)"), ps[:, 6, 0:256], ACT.Copy).then_inc(tok_ready, 1)
                    act.wait_ge(qk_ready, h + 1)
                    log_terms(sg[:], z[:, 16 + 2 * h:18 + 2 * h, :]).then_inc(gsig_terms, 1)
                    act.wait_ge(gsig_log, h + 1)
                    act.activation(sg[:], sg[:], ACT.Exp).then_inc(gsig_ready, 1)
                    act.wait_ge(gla_yy, h + 1)
                    act.activation(sqb[:], ps[:, 2:4, 0:T], ACT.Square).then_inc(osq_ready, 1)
                    act.wait_ge(ms_ready, h + 1)
                    make_rstd(256, 4).then_inc(gla_rs, 1)
                    act.wait_ge(gla_y, h + 1)
                    act.activation(act_hi[:, CT + 2 * h:CT + 2 * h + 2, :], sqb[:], ACT.Copy).then_inc(mixhi_done, 1)

            def mix1():
                act.wait_ge(centred, 2)
                for j in range(CT):
                    q = 56 + j
                    wait_square(q)
                    act.activation(sqb[:, q % 2], zv[:, j, :], ACT.Square).then_inc(sq_ready, 1)
                stat_rstd(CT * P)
                act.wait_ge(normed, 2)
                for j in range(CT):
                    gj, bj = VEC["sgu_ln_g"] + j, VEC["sgu_ln_b"] + j
                    act.activation(zv[:, j, :], zv[:, j, :], ACT.Identity, scale=vec[:, gj:gj + 1],
                                   bias=vec[:, bj:bj + 1]).then_inc(v_ln, 1)
                for g in range(4):
                    act.wait_ge(vmix_turned, g + 1)
                    if g:
                        act.wait_ge(mixed_ready, 2 * g)
                    act.activation(vmix[:].rearrange("p c n -> p (c n)"), ps[:, 5, :], ACT.Copy)
                    act.activation(vmix_s[:], ps[0:32, 6, 0:256], ACT.Copy).then_inc(vmix_ready, 1)
                act.wait_ge(vtok1_turned, 1)
                act.activation(vtok1[:].rearrange("p c n -> p (c n)"), ps[:, 5, 0:256], ACT.Copy)
                act.activation(vnew[:], ps[0:32, 5, 256:384], ACT.Copy).then_inc(vtok1_ready, 1)
                act.wait_ge(sgu_mixed, CT)
                act.activation(act_hi[:, 0:CT, :], zu[:], ACT.Copy).then_inc(mixhi_done, 1)
                for blk in range(2):
                    k0 = 0 if blk else P
                    act.wait_ge(row_max, blk + 1)
                    act.activation(small[:, 2, :], small[:, 2, :], ACT.Exp).then_inc(sink_exp, 1)
                    for h in range(16):
                        act.activation(sc[:, h, k0:256], sc[:, h, k0:256], ACT.Exp, bias=small[:, 1, h:h + 1],
                                       accum_out=small[:, 3, h:h + 1]).then_inc(exps, 1)
                    for h in range(16):
                        turn = 16 * blk + h
                        act.wait_ge(pt_turned, turn + 1)
                        if turn >= 2:
                            act.wait_ge(pv_done, turn - 1)
                        act.activation(ptp[:, turn % 2, k0:256], ps[:, 6 + turn % 2, k0:256], ACT.Copy).then_inc(pt_ready, 1)
                act.wait_ge(row_max, 3)
                act.activation(small[:, 2, 0:4], small[:, 2, 0:4], ACT.Exp).then_inc(sink_exp, 1)
                for c in range(4):
                    act.activation(sc[:, c, 0:KEYS], sc[:, c, 0:KEYS], ACT.Exp, bias=small[:, 1, c:c + 1],
                                   accum_out=small[:, 3, c:c + 1]).then_inc(exps, 1)
                act.wait_ge(pts_turned, 1)
                act.wait_ge(pv_done, 32)
                act.activation(ptp[:, 0, :], ps[:, 4, :], ACT.Copy)
                act.activation(ptp[0:32, 1, :], ps[0:32, 5, :], ACT.Copy).then_inc(pts_ready, 1)
                act.wait_ge(yd_ready, 3)
                act.activation(act_hi[:, CT:KT, :], zq[:], ACT.Copy).then_inc(mixhi_done, 1)

            act.preload_act_table_set("natural_log_exp_and_others")
            act.wait_ge(ones_set, 4)
            act.wait_ge(cond_landed, 16)
            cols = sg[:, 0, 0:KT * S9].rearrange("p (k s) -> p k s", s=S9)
            log_terms(cols, cond[:, :, 0:S9]).then_inc(cond_terms, 1)
            act.wait_ge(cond_log, 1)
            act.activation(cols, cols, ACT.Exp).then_inc(cond_sig, 1)
            act.wait_ge(x_landed, 16)
            for j in range(KT):
                wait_square(j)
                act.activation(sqb[:, j % 2], x[:, j, :], ACT.Square).then_inc(sq_ready, 1)
            act.wait_ge(cond_ready, 1)
            ada_copy((None, 0))
            with act.Fori(0, 7) as i:
                ada_copy((i, 1))
            split(SEGS[0], 0, 0, 0)
            split(SEGS[0], 0, 0, 1)
            norms = 0
            for seg in ["norm"] + PLAN:
                if seg == "norm":
                    norm(norms, final=norms == 4)
                    norms += 1
                elif seg == "mix0":
                    mix0()
                elif seg == "mix1":
                    mix1()
                else:
                    if seg.bodies == 2:
                        body(seg, None, 0)
                    elif seg.bodies > 2:
                        with act.Fori(0, seg.bodies - 1) as i:
                            L.enter(i, seg.act_links)
                            body(seg, i, 0)
                            L.leave(seg.bodies - 1)
                    body(seg, None, seg.bodies - 1, last=True)

        @block.vector
        def _(dve):
            L = Links(dve, dve_links)

            def split_lo(seg, n, par, h):
                dve.wait_ge(hi_done, n * 2 + (h + 1))
                w = seg.width // 2
                dve.tensor_tensor(w_lo[:, h, 0:w], raw[:, par, h * w:(h + 1) * w], w_hi[:, h, 0:w].bitcast(F32),
                                  ALU.subtract).then_inc(split_done, 1)

            def resid(seg, bank, j, b, first_inc, last_inc):
                g = (seg.layer * 96 + (2 if seg.kind == "out" else 5) * KT) + j
                tmp = xtmp[:, b]
                if last_inc:
                    if not (isinstance(j, int) and j + seg.x0 < 1):
                        dve.wait_ge(x_updated, j + seg.x0)
                if L.n:
                    L.wait(L.n)
                m = L.mark(dve.tensor_tensor(tmp, seqs(bank[:, NP_TOK:T]),
                                             at(mods, g, 1, S9).unsqueeze(2).to_broadcast([P, NSEQ, TS]), ALU.mult))
                ins = dve.scalar_tensor_tensor(at(x, j, 0, NP_TOK), bank[:, 0:NP_TOK], at(mods, g, 0, 1),
                                               at(x, j, 0, NP_TOK), ALU.mult, ALU.add)
                if first_inc:
                    ins.then_inc(first_inc, 1)
                L.wait(m)
                ins = dve.tensor_tensor(seqs(at(x, j, NP_TOK, T)), seqs(at(x, j, NP_TOK, T)), tmp, ALU.add)
                if last_inc:
                    ins.then_inc(last_inc, 1)
                else:
                    L.mark(ins)

            def epilogue(seg, n, par, ls):
                if seg.kind in ("zr", "zconv", "z", "kv", "q"):
                    return
                b0, b1 = ps[:, 2 * par, 0:T], ps[:, 2 * par + 1, 0:T]
                dve.wait_ge(half_done, n * 2 + 2)
                dve.wait_ge(drained, n)
                if seg.kind in ("gate", "gu"):
                    k = ls + seg.sig0
                    s, gate_bank = sg[:, 0], b1 if seg.kind == "gate" else b0
                    dve.wait_ge(sig_terms, k + 1)
                    dve.scalar_tensor_tensor(s, gate_bank, 0.0, s, ALU.min, ALU.subtract).then_inc(sig_log, 1)
                    dve.wait_ge(sig_ready, k + 1)
                    if seg.kind == "gate":
                        dve.tensor_tensor(at(uext, ls, HIST, UW), b0[:, 0:NP_TOK], s[:, 0:NP_TOK], ALU.mult)
                        dve.tensor_tensor(rows_s(ls)[:, :, HIST:SW], seqs(b0[:, NP_TOK:T]), seqs(s[:, NP_TOK:T]),
                                          ALU.mult).then_inc(drained, 1)
                    else:
                        hid = ls + (seg.sig0 - CT - (2 * CT if seg.layer else 0))
                        if not (isinstance(hid, int) and hid == 0):
                            dve.wait_ge(hid_ready, hid)
                        L.link(dve.tensor_tensor(prod[:], b0, s, ALU.mult))
                        dve.tensor_tensor(prod[:], prod[:], b1, ALU.mult).then_inc(drained, 1)
                        j = ls + seg.first % BLK
                        dve.wait_ge(hid_hi_done, hid + 1)
                        dve.tensor_tensor(at(hid_lo, j), prod[:], at(hid_hi, j).bitcast(F32), ALU.subtract) \
                            .then_inc(hid_ready, 1)
                elif seg.kind == "sgu":
                    for b, bank in enumerate((b0, b1)):
                        dve.wait_ge(gelu_sq, ls * 2 + (seg.gel0 + b + 1))
                        dve.scalar_tensor_tensor(sqb[:, b], sqb[:, b], GELU_2C, bank, ALU.add, ALU.mult) \
                            .then_inc(gelu_arg, 1)
                    for b in range(2):
                        dve.wait_ge(sig_terms, ls * 2 + (seg.sig0 + b + 1))
                        dve.scalar_tensor_tensor(sg[:, b], sqb[:, b], 0.0, sg[:, b], ALU.min, ALU.subtract) \
                            .then_inc(sig_log, 1)
                    for b, (bank, out) in enumerate(((b0, zu), (b1, zv))):
                        dve.wait_ge(sig_ready, ls * 2 + (seg.sig0 + b + 1))
                        ins = dve.tensor_tensor(at(out, ls), bank, sg[:, b], ALU.mult)
                    ins.then_inc(drained, 1)
                elif seg.kind == "out":
                    resid(seg, b0, ls * 2, 0, None, x_updated)
                    resid(seg, b1, ls * 2 + 1, 1, drained, x_updated)
                else:
                    resid(seg, b0, ls, 0, drained, x_updated if seg.group else None)

            def conv(j, taps, marks):
                w = VEC["conv_w"]
                if 0 in taps:
                    if not (isinstance(j, int) and j == 0):
                        dve.wait_ge(conv_ready, j)
                    if L.n:
                        L.wait(L.n)
                for k in taps:
                    wk = flat_at(vec, j * TAPS + (w + k))
                    for s in range(2):
                        row = taps_s(j, k) if s else at(uext, j, k, k + NP_TOK)
                        acc = seqs(cacc[:, NP_TOK:T]) if s else cacc[:, 0:NP_TOK]
                        out = acc if k < TAPS - 1 else taps_s(j, 0) if s else at(uext, j, 0, NP_TOK)
                        if marks[s]:
                            L.wait(marks[s])
                        if k == 0:
                            ins = dve.tensor_scalar(out, row, wk, flat_at(vec, j + VEC["conv_b"]), ALU.mult, ALU.add)
                        else:
                            ins = dve.scalar_tensor_tensor(out, row, wk, acc, ALU.mult, ALU.add)
                        if k == TAPS - 1 and s:
                            ins.then_inc(conv_ready, 1)
                        else:
                            marks[s] = L.mark(ins)

            def ada_bias(u):
                dve.wait_ge(ada_cols, unit_no(u) + 1)
                b = bass.ds(unit_no(u) * 4 + VEC["b_ada"], 4)
                dve.tensor_tensor(mods[:, bass.ds(unit_no(u) * 4, 4), :],
                                  ps[:, SEL_BANK, 0:64].rearrange("p (q s) -> p q s", s=16)[:, :, 0:S9],
                                  vec[:, b].unsqueeze(2).to_broadcast([P, 4, S9]), ALU.add).then_inc(ada_biased, 1)

            def body(seg, i, base, last=False):
                marks = [0, 0]
                for j, (n, par, ls) in enumerate(steps_of(seg, i, base)):
                    end = last and j == seg.m - 1
                    nxt = seg.next if end else seg
                    hurry = end and seg.then_wait
                    if nxt:
                        split_lo(nxt, n + 1, 1 - par, 0)
                        if not hurry:
                            split_lo(nxt, n + 1, 1 - par, 1)
                    epilogue(seg, n, par, ls)
                    if nxt and hurry:
                        split_lo(nxt, n + 1, 1 - par, 1)
                    if seg.unit is not None and j == 1:
                        ada_bias((i, seg.unit + base))
                    if seg.kind in ("gate", "zconv"):
                        tile = lin(i, 1, base + (4 if seg.kind == "zconv" else 0))
                        dve.wait_ge(drained, n + 1)
                        conv(tile, range(0, 16) if j == 0 else range(16, TAPS), marks)

            def norm(k, final=False):
                layer, part = divmod(k, 2)
                if not final:
                    scale = layer * 96 + part * 48 + KT
                    g = VEC["g_ffn" if part else "g_mix"] + KT * layer
                    L.link(dve.scalar_tensor_tensor(amod[:], mods[:, scale:scale + KT, :], 1.0,
                                                    vec[:, g:g + KT].unsqueeze(2).to_broadcast([P, KT, S9]),
                                                    ALU.add, ALU.mult))
                shift = layer * 96 + part * 48
                base = KT * [0, 2, 3, 5, 6][k]
                if base:
                    dve.wait_ge(act_ready, base)
                dve.wait_ge(rstd_ready, NORM_STATS[k])

                def scaled(g):
                    if final and g >= 2:
                        dve.wait_ge(y_stored[g % 2], 16)
                    elif g >= 2:
                        dve.wait_ge(act_ready, base + 4 * (g - 1))
                    dve.tensor_tensor(tn[:, g % 2], x[:, 4 * g:4 * g + 4, :],
                                      rstd[:].unsqueeze(1).to_broadcast([P, 4, T]), ALU.mult).then_inc(tn_ready, 1)

                def samples(g):
                    dve.wait_ge(tn_ready, 4 * k + g + 1)
                    cols = tn[:, g % 2, :, NP_TOK:T].rearrange("p k (b t) -> p k b t", t=TS)
                    js = slice(4 * g, 4 * g + 4)
                    L.link(dve.tensor_tensor(cols, cols, amod[:, js, 1:S9].unsqueeze(3).to_broadcast([P, 4, NSEQ, TS]), ALU.mult))
                    dve.tensor_tensor(cols, cols, mods[:, shift + 4 * g:shift + 4 * g + 4, 1:S9].unsqueeze(3)
                                      .to_broadcast([P, 4, NSEQ, TS]), ALU.add).then_inc(tn_samples, 1)

                def lo(g):
                    dve.wait_ge(nhi_done, 4 * k + g + 1)
                    js = slice(4 * g, 4 * g + 4)
                    dve.tensor_tensor(act_lo[:, js, :], tn[:, g % 2], act_hi[:, js, :].bitcast(F32), ALU.subtract) \
                        .then_inc(act_ready, 4)

                for g in range(4):
                    scaled(g)
                    if not final:
                        samples(g)
                        if g:
                            lo(g - 1)
                if not final:
                    lo(3)

            def centre(k, y, y_s):
                dve.wait_ge(mean_ready, k)
                dve.tensor_scalar(prod[:], ps[:, MEAN_BANK, 0:T], 1.0 / (CT * P), None, ALU.mult).then_inc(mean_used, 1)
                dve.wait_ge(mean_used, k)
                apply_stat(y, y_s, prod, ALU.subtract).then_inc(centred, 1)

            def apply_stat(y, y_s, by, op):
                if y_s is None:
                    return dve.tensor_tensor(y, y, by[:].unsqueeze(1).to_broadcast([P, CT, T]), op)
                dve.tensor_tensor(y, y, by[:, 0:NP_TOK].unsqueeze(1).to_broadcast([P, CT, NP_TOK]), op)
                for s in range(NSEQ):
                    cols = by[:, NP_TOK + TS * s:NP_TOK + TS * (s + 1)].unsqueeze(1).to_broadcast([P, CT, TS])
                    ins = dve.tensor_tensor(y_s[:, :, s], y_s[:, :, s], cols, op)
                return ins

            def mix0():
                centre(1, y_all, y_all_s)
                dve.wait_ge(rstd_ready, 2)
                apply_stat(y_all, y_all_s, rstd, ALU.mult).then_inc(normed, 1)
                for j in range(CT + 1):
                    if j < CT:
                        dve.wait_ge(conv_terms, j + 1)
                        b = j % 2
                        dve.scalar_tensor_tensor(sg[:, b], sqb[:, b], 0.0, sg[:, b], ALU.min, ALU.subtract) \
                            .then_inc(conv_log, 1)
                    if j:
                        b = (j - 1) % 2
                        dve.wait_ge(conv_sig, j)
                        dve.tensor_tensor(sqb[:, b], sqb[:, b], sg[:, b], ALU.mult).then_inc(conv_y, 1)
                        dve.wait_ge(mixhi_done, j)
                        dve.tensor_tensor(act_lo[:, j - 1, :], sqb[:, b], act_hi[:, j - 1, :].bitcast(F32), ALU.subtract) \
                            .then_inc(act_ready, 1)
                dve.wait_ge(mix0_consts, 16 * 5)
                dve.wait_ge(conv_stored, 16 * (CT + 1))
                L.link(dve.memset(att[:], 0.0))
                L.link(dve.memset(att_s[:], 0.0))
                for h in range(HEADS):
                    q, k = z[:, 2 * h, :], z[:, 2 * h + 1, :]
                    dve.wait_ge(la_ready, h + 1)
                    dve.wait_ge(act_ready, KT + CT + 2 * h)
                    bg = VEC["gla_b_gate"] + h
                    dve.wait_ge(la_terms, h + 1)
                    L.link(dve.tensor_scalar(sg[:, 1], ps[:, LA_BANK, 0:T], vec[:, bg:bg + 1], 0.0, ALU.add, ALU.min))
                    L.link(dve.tensor_tensor(sg[:, 1], sg[:, 1], sg[:, 0], ALU.subtract))
                    L.link(dve.tensor_tensor_scan(gb[:], chunk_start[:], sg[:, 1], 0.0, ALU.mult, ALU.add))
                    chunks = gb[:, 0:NP_TOK].rearrange("p (c s) -> p c s", s=64)
                    dve.tensor_tensor(sg[:, 0, 0:NP_TOK].rearrange("p (c s) -> p c s", s=64),
                                      chunks[:, :, 63:64].to_broadcast([P, 4, 64]), chunks, ALU.subtract)
                    dve.tensor_tensor(seqs(sg[:, 0, NP_TOK:T]), seqs(gb[:, NP_TOK:T])[:, :, 3:4].to_broadcast([P, NSEQ, TS]),
                                      seqs(gb[:, NP_TOK:T]), ALU.subtract).then_inc(b_ready, 1)
                    dve.wait_ge(e_ready, h + 1)
                    dve.tensor_tensor(gkl[:], k, sg[:, 0], ALU.mult).then_inc(kl_ready, 1)
                    dve.wait_ge(kl_ready, h + 1)
                    dve.tensor_tensor(k, k, prod[:], ALU.mult)
                    dve.scalar_tensor_tensor(q, q, float(P) ** -0.5, geb[:], ALU.mult, ALU.mult).then_inc(qk_ready, 1)
                    dve.wait_ge(kl_turned, h + 1)
                    dve.tensor_tensor(klm[:], ps[0:32, 7, 0:P].unsqueeze(1).to_broadcast([32, NSEQ, P]),
                                      seqmask[:].unsqueeze(2).to_broadcast([32, NSEQ, P]), ALU.mult).then_inc(tok_ready, 1)
                    dve.wait_ge(att_turned, h + 1)
                    for c in range(2):
                        rows = slice(64 * c, 64 * c + 64)
                        dve.copy_predicated(att[rows, :, rows], causal64[rows], ps[rows, 4, 0:P].rearrange("p (c s) -> p c s", s=64))
                    dve.copy_predicated(att_s[:], causal_s[:], ps[0:32, 4, P:P + 32]).then_inc(att_ready, 1)
                    dve.wait_ge(sadd_ready, h + 1)
                    if h:
                        dve.wait_ge(gstate_stored, 16 * h)
                    adds = [ps[:, c % 2, 256 * (c // 2):256 * (c // 2) + 256] for c in range(4)]
                    L.link(dve.tensor_copy(gs[:, 0, :], adds[0]))
                    for c in range(1, 4):
                        ins = dve.scalar_tensor_tensor(gs[:, c, :], gs[:, c - 1, :], geb[:, 64 * c + 63:64 * c + 64],
                                                       adds[c], ALU.mult, ALU.add)
                        if c < 3:
                            L.link(ins)
                    ins.then_inc(s_chain, 1)
                    dve.wait_ge(gsig_terms, h + 1)
                    dve.scalar_tensor_tensor(sg[:], z[:, 16 + 2 * h:18 + 2 * h, :], 0.0, sg[:], ALU.min, ALU.subtract) \
                        .then_inc(gsig_log, 1)
                    dve.wait_ge(gla_yy, h + 1)
                    for r in range(2):
                        dve.wait_ge(snew_ready, 2 * h + r + 1)
                        for s in range(4):
                            b = 4 * r + s
                            st = aring[:, h % 2, 256 * b:256 * (b + 1)]
                            ins = dve.scalar_tensor_tensor(st, st, geb[:, NP_TOK + TS * b + 3:NP_TOK + TS * b + 4],
                                                           ps[:, s // 2, 256 * (s % 2):256 * (s % 2) + 256], ALU.mult, ALU.add)
                        ins.then_inc(snew_used, 1)
                    dve.wait_ge(gsig_ready, h + 1)
                    for b in range(2):
                        gn = VEC["gla_g_norm"] + b
                        ins = dve.scalar_tensor_tensor(sg[:, b], z[:, 16 + 2 * h + b, :], vec[:, gn:gn + 1], sg[:, b],
                                                       ALU.mult, ALU.mult)
                    L.link(ins)
                    dve.wait_ge(gla_rs, h + 1)
                    m = L.mark(dve.tensor_tensor(sqb[:], ps[:, 2:4, 0:T], rstd[:].unsqueeze(1).to_broadcast([P, 2, T]), ALU.mult))
                    L.wait(m)
                    dve.tensor_tensor(sqb[:], sqb[:], sg[:], ALU.mult).then_inc(gla_y, 1)
                    dve.wait_ge(mixhi_done, CT + h + 1)
                    js = slice(CT + 2 * h, CT + 2 * h + 2)
                    dve.tensor_tensor(act_lo[:, js, :], sqb[:], act_hi[:, js, :].bitcast(F32), ALU.subtract) \
                        .then_inc(act_ready, 2)
                dve.wait_ge(gstate_stored, 16 * HEADS)

            def attend(rows, n, sink):
                L.link(dve.tensor_reduce(small[:, 0, 0:n], rows, AX.X, ALU.max))
                L.link(dve.tensor_tensor(small[:, 0, 0:n], small[:, 0, 0:n], sink, ALU.max))
                L.link(dve.tensor_scalar(small[:, 1, 0:n], small[:, 0, 0:n], -1.0, None, ALU.mult))
                dve.tensor_tensor(small[:, 2, 0:n], sink, small[:, 0, 0:n], ALU.subtract).then_inc(row_max, 1)

            def denominators(n):
                L.link(dve.tensor_tensor(small[:, 4, 0:n], small[:, 3, 0:n], small[:, 2, 0:n], ALU.add))
                L.link(dve.reciprocal(small[:, 5, 0:n], small[:, 4, 0:n]))

            def mix1():
                centre(2, zv[:], None)
                dve.wait_ge(rstd_ready, 5)
                apply_stat(zv[:], None, rstd, ALU.mult).then_inc(normed, 1)
                for j in range(CT):
                    dve.wait_ge(mixed_ready, j + 1)
                    dve.tensor_tensor(zu[:, j, :], zu[:, j, :], ps[:, j % 2, 0:T], ALU.mult).then_inc(sgu_mixed, 1)
                dve.wait_ge(mixhi_done, CT + HEADS + 1)
                dve.tensor_tensor(act_lo[:, 0:CT, :], zu[:], act_hi[:, 0:CT, :].bitcast(F32), ALU.subtract).then_inc(act_ready, CT)
                dve.wait_ge(mix1_consts, 16 * 6)
                dve.wait_ge(sguv_stored, 16)
                dve.wait_ge(act_ready, 4 * KT + CT)
                dve.tensor_copy(qs[:], zq[:, :, NP_TOK:T].rearrange("p r (b t) -> p b r t", t=TS)).then_inc(qs_ready, 1)
                for blk in range(2):
                    k0 = 0 if blk else P
                    for h in range(16):
                        dve.wait_ge(scores_ready, 16 * blk + h + 1)
                        if blk:
                            dve.wait_ge(pt_turned, h + 1)
                        dve.scalar_tensor_tensor(sc[:, h, k0:256], dist[:, k0:256], SLOPES[h], ps[:, h % 4, k0:256],
                                                 ALU.mult, ALU.add).then_inc(scored, 1)
                    dve.wait_ge(scored, 16 * blk + 16)
                    attend(sc[:, :, k0:256], 16, sinks[:, 0:16])
                    dve.wait_ge(exps, 16 * blk + 16)
                    dve.wait_ge(sink_exp, blk + 1)
                    denominators(16)
                    for h in range(16):
                        dve.tensor_scalar(sc[:, h, k0:256], sc[:, h, k0:256], small[:, 5, h:h + 1], None, ALU.mult) \
                            .then_inc(probs_ready, 1)
                    dve.wait_ge(pv_done, 16 * blk + 16)
                    dve.wait_ge(qs_ready, 1)
                    dve.tensor_copy(zq[:, :, blk * P:(blk + 1) * P],
                                    ps[:, 2:4, :].rearrange("p a (r n) -> p (a r) n", n=P)).then_inc(yd_ready, 1)
                dve.wait_ge(scores_s_ready, 1)
                L.link(dve.tensor_tensor(sc[:, 0:4, 0:KEYS], ps[:, 0:4, 0:KEYS], bias_s[:], ALU.add))
                attend(sc[:, 0:4, 0:KEYS], 4, sinks[:, 16:20])
                dve.wait_ge(exps, 36)
                dve.wait_ge(sink_exp, 3)
                denominators(4)
                dve.tensor_tensor(sc[:, 0:4, 0:KEYS], sc[:, 0:4, 0:KEYS], small[:, 5, 0:4].unsqueeze(2).to_broadcast([P, 4, KEYS]),
                                  ALU.mult).then_inc(probs_s_ready, 1)
                dve.wait_ge(os_ready, 1)
                for s in range(NSEQ):
                    ins = dve.tensor_copy(zq[:, :, NP_TOK + TS * s:NP_TOK + TS * (s + 1)],
                                          ps[:, 0, 32 * s:32 * s + 32].rearrange("p (r t) -> p r t", t=TS))
                ins.then_inc(yd_ready, 1)
                dve.wait_ge(mixhi_done, CT + HEADS + 2)
                dve.tensor_tensor(act_lo[:, CT:KT, :], zq[:], act_hi[:, CT:KT, :].bitcast(F32), ALU.subtract).then_inc(act_ready, CT)
                dve.wait_ge(cache_stored, 16 * 6)

            cols = sg[:, 0, 0:KT * S9].rearrange("p (k s) -> p k s", s=S9)
            dve.wait_ge(cond_terms, 1)
            dve.scalar_tensor_tensor(cols, cond[:, :, 0:S9], 0.0, cols, ALU.min, ALU.subtract).then_inc(cond_log, 1)
            dve.wait_ge(cond_sig, 1)
            dve.tensor_tensor(cond[:, :, 0:S9], cond[:, :, 0:S9], cols, ALU.mult).then_inc(cond_ready, 1)
            dve.wait_ge(consts_landed, 48)
            ada_bias((None, 0))
            with dve.Fori(0, 7) as i:
                ada_bias((i, 1))
            split_lo(SEGS[0], 0, 0, 0)
            split_lo(SEGS[0], 0, 0, 1)
            norms = 0
            for seg in ["norm"] + PLAN:
                if seg == "norm":
                    dve.wait_ge(ada_biased, [8, 22, 48, 48, 48][norms])
                    norm(norms, final=norms == 4)
                    norms += 1
                    if norms == 1:
                        dve.wait_ge(history_landed, 16 * CT)
                        dve.wait_ge(history_zero, 1)
                elif seg == "mix0":
                    mix0()
                elif seg == "mix1":
                    mix1()
                else:
                    if seg.bodies == 2:
                        body(seg, None, 0)
                    elif seg.bodies > 2:
                        with dve.Fori(0, seg.bodies - 1) as i:
                            L.enter(i, seg.dve_links)
                            body(seg, i, 0)
                            L.leave(seg.bodies - 1)
                    body(seg, None, seg.bodies - 1, last=True)



def tiles(w):
    k, n = w.shape
    return w.reshape(k // P, P, n // P, P).transpose(2, 1, 0, 3).reshape(n // P, P, k)


def paired(a, b):
    return np.concatenate([a, b], axis=2)


def columns(v):
    return v.reshape(-1, P).T


def kernel(**inputs):
    import concourse.bacc as bacc
    from concourse.bass_utils import run_bass_kernel_spmd

    a = {k: np.asarray(v) for k, v in inputs.items()}
    f = {}
    tokens = np.concatenate([a["x_prompt"][0], a["x_sample"].reshape(NSEQ * TS, D)])
    f["xT"] = tokens.T.reshape(KT, P, T).transpose(1, 0, 2)
    f["cT"] = np.concatenate([a["c_prompt"], a["c_sample"]]).T.reshape(KT, P, S9).transpose(1, 0, 2)
    conv_w = a["conv_w"].T.reshape(CT, P, TAPS).transpose(1, 0, 2).reshape(P, CT * TAPS)
    f["vec"] = np.concatenate([columns(a[n].reshape(-1)) for n in VEC if n != "conv_w"] + [conv_w], axis=1)
    f["w_ada"] = a["w_ada"].reshape(2, 4, 4, P, UNITS, ADA_N).transpose(0, 4, 1, 3, 2, 5).reshape(8 * UNITS, P, 4 * ADA_N)
    ab = tiles(a["w_in_ab"][:, :40 * P])
    f["w_ab"] = np.concatenate([paired(ab[0:8], ab[8:16]), paired(ab[16:20], ab[20:24]), paired(ab[24:40:2], ab[25:40:2])])
    f["w_zr"] = tiles(np.pad(a["w_in_ab"][:, 40 * P:], ((0, 0), (0, P - 16))))
    cd = a["w_in_cd"]
    q0, kv0 = 2 * CT * P, 3 * CT * P
    q = cd[:, q0:kv0].reshape(D, 2, CT, 64).transpose(0, 2, 1, 3).reshape(D, CT * P)
    u, v, q, kv = tiles(cd[:, 0:CT * P]), tiles(cd[:, CT * P:q0]), tiles(q), tiles(cd[:, kv0:])
    f["w_cd"] = np.concatenate([paired(kv[0:1], kv[1:2]), paired(q[0::2], q[1::2]), paired(u, v)])
    wo1 = a["w_out"][1]
    wo1 = np.concatenate([wo1[:CT * P], wo1[CT * P:].reshape(2, CT, 64, D).transpose(1, 0, 2, 3).reshape(CT * P, D)])
    wo = [tiles(a["w_out"][0]), tiles(wo1)]
    f["w_out"] = np.concatenate([paired(w[0::2], w[1::2]) for w in wo])
    f["w_gu"] = np.concatenate([paired(tiles(a["w_ffn_gate"][i]), tiles(a["w_ffn_up"][i])) for i in range(2)])
    f["w_dn"] = np.concatenate([tiles(half) for i in range(2) for half in np.split(a["w_ffn_down"][i], 2)])
    f["gla_w_gate"] = a["gla_w_gate"]
    f["state_convT"] = a["state_conv"].transpose(2, 0, 1).reshape(CT, P, NSEQ, HIST).transpose(1, 0, 2, 3)
    f["state_glaT"] = a["state_gla"].transpose(1, 2, 0, 3).reshape(HEADS, P, NSEQ * 256)
    f["cache_kT"] = a["cache_k"].transpose(2, 3, 0, 1).reshape(P, NSEQ, P)
    f["cache_vT"] = a["cache_v"].transpose(1, 0, 2, 3).reshape(P, NSEQ, P)
    f["sgu_wT"] = a["sgu_w"].transpose(2, 0, 1)
    f["sgu_wsT"] = np.tile(a["sgu_w"][:, :TS, :TS].transpose(2, 0, 1), (NSEQ, 1, NSEQ))
    f["sgu_bT"] = np.concatenate([a["sgu_b"], a["sgu_b"], np.tile(a["sgu_b"][:, :TS], (1, NSEQ))], axis=1)[None]
    sinks_p = np.broadcast_to(a["att_sinks"], (P, 16))
    sinks_s = np.tile(np.repeat(a["att_sinks"].reshape(2, 8), TS, axis=1).T, (4, 2))
    f["sinks"] = np.concatenate([sinks_p, sinks_s], axis=1)
    f["ident"] = np.eye(P)
    f["sel"] = np.tile(np.eye(32, S9), (4, 1))
    t_ = np.arange(T)
    f["chunk_start"] = np.broadcast_to(np.where(t_ < NP_TOK, t_ % 64 != 0, t_ % TS != 0), (P, T))
    s_, q_ = np.arange(64)[:, None], np.arange(64)[None]
    f["causal64"] = np.tile((s_ <= q_)[:, None], (2, 2, 1)).astype(np.uint32)
    i_, j_ = np.arange(32)[:, None], np.arange(32)[None]
    f["causal_s"] = ((i_ // TS == j_ // TS) & (i_ <= j_)).astype(np.uint32)
    f["seqmask"] = i_ // TS == np.arange(NSEQ)[None]
    d = np.arange(P)[:, None] - np.arange(256)[None] + P
    f["dist"] = np.where((d >= 0) & (d < P), -d, NEG)
    seq4, head, tok = np.arange(P) // 32, np.arange(P) // TS % 8, np.arange(P) % TS
    bias = np.full((P, 2, 2, KEYS), NEG)
    for pair in range(2):
        for g in range(2):
            slope = np.array(SLOPES)[g * 8 + head][:, None]
            dc = P + tok[:, None] - np.arange(P)[None]
            bias[:, pair, g, :P] = np.where(dc < P, -slope * dc, NEG)
            dn = tok[:, None] - j_ % TS
            own = (j_ // TS == (4 * pair + seq4)[:, None]) & (dn >= 0)
            bias[:, pair, g, P:] = np.where(own, -slope * dn, NEG)
    f["bias_s"] = bias.reshape(P, 4, KEYS)
    outs = {"y": (P, KT, T), "conv_p": (P, CT, HIST), "conv_s": (P, CT, NSEQ, HIST), "gla_p": (HEADS, P, 256),
            "gla_s": (HEADS, P, NSEQ * 256), "sgu_v": (P, CT, NSEQ * TS), "k_p": (P, P), "k_s_new": (P, NSEQ * TS),
            "k_s_old": (P, NSEQ, P - TS), "v_p": (P, P), "v_s_new": (NSEQ * TS, P), "v_s_old": (P - TS, NSEQ, P)}

    nc = bacc.Bacc("TRN2", target_bir_lowering=False, num_devices=1)
    arrays, t, o = {}, {}, {}
    for name, v in f.items():
        v = np.ascontiguousarray(v, dtype=v.dtype if v.dtype == np.uint32 else np.float32)
        arrays[f"in_{name}"] = v
        t[name] = nc.dram_tensor(f"in_{name}", v.shape, mybir.dt.from_np(v.dtype), kind="ExternalInput").ap()
    for name, shape in outs.items():
        o[name] = nc.dram_tensor(f"out_{name}", shape, F32, kind="ExternalOutput").ap()
    build(nc, t, o)
    res = run_bass_kernel_spmd(nc, [arrays], core_ids=[0]).results[0]
    r = {name: np.asarray(res[f"out_{name}"]) for name in outs}
    y = r["y"].transpose(2, 1, 0).reshape(T, D)
    k_s = np.concatenate([r["k_s_old"], r["k_s_new"].reshape(P, NSEQ, TS)], axis=2).transpose(1, 2, 0)
    v_s = np.concatenate([r["v_s_old"].transpose(1, 0, 2), r["v_s_new"].reshape(NSEQ, TS, P)], axis=1)
    return (y[:NP_TOK].reshape(1, NP_TOK, D), y[NP_TOK:].reshape(NSEQ, TS, D),
            r["conv_p"].transpose(2, 1, 0).reshape(1, HIST, CT * P),
            r["conv_s"].transpose(2, 3, 1, 0).reshape(NSEQ, HIST, CT * P),
            r["gla_p"].reshape(1, HEADS, P, 256),
            r["gla_s"].reshape(HEADS, P, NSEQ, 256).transpose(2, 0, 1, 3),
            r["sgu_v"].transpose(2, 1, 0).reshape(NSEQ, TS, CT * P),
            r["k_p"].T.reshape(1, P, 2, 64), k_s.reshape(NSEQ, P, 2, 64),
            r["v_p"].reshape(1, P, 2, 64), v_s.reshape(NSEQ, P, 2, 64))
```

```python
from contextlib import ExitStack

import concourse.bass as bass
from concourse import mybir
import numpy as np

F32 = mybir.dt.float32
F32R = mybir.dt.float32r
U32 = mybir.dt.uint32
ALU = mybir.AluOpType
ACT = mybir.ActivationFunctionType
AX = mybir.AxisListType

P = 128
D = 2048
KT = D // P
NP_TOK = 256
NSEQ, TS = 8, 4
T = NP_TOK + NSEQ * TS
S9 = 1 + NSEQ
TAPS, HIST = 31, 30
UW = HIST + NP_TOK
SW = HIST + TS
UE = UW + NSEQ * SW
CT = 8
FF_T = 44
BLK = FF_T // 2
HEADS = 4
SLOT = 2 * KT * P
ADA_N = 512
UNITS = 6 * D // ADA_N
PRE = 8
KEYS = P + NSEQ * TS
EPS = 1e-6
GELU_2C = 2.0 * (2.0 / np.pi) ** 0.5
GELU_K = GELU_2C * 0.044715
NEG = -1e30
SLOPES = [float(np.float32(2.0 ** (-8.0 * (h + 1) / 16))) for h in range(16)]

VEC = {}
_at = 0
for _name, _n in (("g_mix", 2 * KT), ("g_ffn", 2 * KT), ("g_final", KT), ("conv_b", CT), ("conv_ln_g", CT),
                  ("conv_ln_b", CT), ("gla_b_gate", HEADS), ("gla_g_norm", 2), ("sgu_ln_g", CT), ("sgu_ln_b", CT),
                  ("b_ada", 2 * 96), ("conv_w", CT * TAPS)):
    VEC[_name] = _at
    _at += _n
NVEC = _at


class Seg:

    def __init__(self, kind, layer, bodies, m, first, unit=None, group=0):
        self.kind, self.layer, self.bodies, self.m = kind, layer, bodies, m
        self.first = first
        self.unit = unit
        self.group = group
        self.steps = bodies * m
        self.ktiles = {"zr": 8, "down": BLK // 2}.get(kind, KT)
        self.two = kind not in ("zr", "down")
        self.width = 2 * self.ktiles * P
        self.act_links = {"gate": 4, "gu": 4, "sgu": 8}.get(kind, 0)
        self.dve_links = {"gate": 2 * TAPS - 1, "zconv": 2 * TAPS - 1, "gu": 2, "out": 4,
                          "down": 2 if group else 4}.get(kind, 0)


def plan():
    segs, norm = [], "norm"
    segs += [Seg("zr", 0, 1, 1, 0), Seg("gate", 0, 4, 2, 0, 8), Seg("zconv", 0, 4, 2, 8, 12, 0),
             Seg("z", 0, 2, 2, 16, 16, 16)]
    segs += ["mix0", Seg("out", 0, 4, 2, 0, 18), norm]
    for layer in range(2):
        if layer:
            segs += [Seg("kv", 1, 1, 1, 0), Seg("q", 1, 2, 2, 1), Seg("sgu", 1, 4, 2, 5), "mix1",
                     Seg("out", 1, 4, 2, 0), norm]
        segs += [Seg("gu", layer, 11, 2, 0, None if layer else 22),
                 Seg("down", layer, 8, 2, 0, None if layer else 33, 0)]
        if layer:
            segs += [Seg("gu", 1, 11, 2, 22)]
        else:
            segs += [Seg("gu", 0, 7, 2, 22, 41), Seg("gu", 0, 4, 2, 36)]
        segs += [Seg("down", layer, 8, 2, 16, None, 1), norm]
    return segs


PLAN = plan()
SEGS = [s for s in PLAN if isinstance(s, Seg)]
_n = _sig = _gel = _x = 0
_q = KT
for _s in SEGS:
    _s.n0, _s.sig0, _s.gel0, _s.q0, _s.x0 = _n, _sig, _gel, _q, _x
    _n += _s.steps
    if _s.kind in ("gate", "gu"):
        _sig += _s.steps
    if _s.kind == "sgu":
        _sig += 2 * _s.steps
        _gel += 2 * _s.steps
        _q += CT
    if _s.kind == "z":
        _q += CT
    if _s.kind == "out" or _s.kind == "down" and _s.group:
        _q += KT
        _x += KT
STEPS = _n
for _a, _b in zip(SEGS, SEGS[1:] + [None]):
    _a.next = _b
_kinds = set()
for _s in SEGS:
    _s.opens = _s.kind not in _kinds and _s.kind in ("gate", "out", "gu")
    _kinds.add(_s.kind)
    _s.peel = int(_s.bodies == 2 or _s.opens or _s.kind == "out")
for _a, _b in zip(PLAN, PLAN[1:]):
    if isinstance(_a, Seg):
        _a.then_wait = not isinstance(_b, Seg) or "down" in (_a.kind, _b.kind)
SGU_SEG = next(s for s in SEGS if s.kind == "sgu")
Z_SEG = next(s for s in SEGS if s.kind == "z")
SQUARES = [0, 16, 24, 40, 56, 64, 80, 96]
NORM_STATS = [1, 3, 4, 6, 7]
GLA_A = 4 * 18


def lin(i, per, c):
    return c if i is None else i * per + c


class Links:

    def __init__(self, eng, sem):
        self.eng, self.sem, self.n, self.i, self.per = eng, sem, 0, None, 0

    def value(self, n):
        return n if self.i is None else self.i * self.per + n

    def mark(self, ins):
        ins.then_inc(self.sem, 1)
        self.n += 1
        return self.n

    def wait(self, n):
        self.eng.wait_ge(self.sem, self.value(n))

    def link(self, ins):
        self.wait(self.mark(ins))

    def enter(self, i, per):
        self.i, self.per, self.start = i, per, self.n

    def leave(self, turns):
        assert self.n - self.start == self.per, (self.n - self.start, self.per)
        self.n = self.start + turns * self.per
        self.i = None


def build(nc, t, o):
    ctx = ExitStack()
    with ctx:
        def sb(name, shape, dt=F32, stack=ctx):
            return stack.enter_context(nc.sbuf_tensor(name, shape, dt))

        sems = {}

        def sem(name):
            if name not in sems:
                sems[name] = ctx.enter_context(nc.semaphore(name))
            return sems[name]

        x = sb("x", [P, KT, T])
        act_hi = sb("act_hi", [P, KT, T], F32R)
        act_lo = sb("act_lo", [P, KT, T], F32R)
        raw = sb("raw", [P, 2, SLOT])
        w_hi = sb("w_hi", [P, 2, SLOT // 2], F32R)
        w_lo = sb("w_lo", [P, 2, SLOT // 2], F32R)
        aring = sb("aring", [P, 2, 4 * ADA_N])
        vec = sb("vec", [P, NVEC])
        mods = sb("mods", [P, 2 * 96, S9])
        cond = sb("cond", [P, KT, 32])
        adarow = sb("adarow", [P, ADA_N])
        ident = sb("ident", [P, P])
        ones = sb("ones", [P, P])
        sel = sb("sel", [P, S9])
        eps = sb("eps", [P, 1])
        one = sb("one", [P, 1])
        sg = sb("sg", [P, 2, T])
        prod = sb("prod", [P, T])
        sqb = sb("sqb", [P, 2, T])
        ssq = sb("ssq", [P, T])
        rstd = sb("rstd", [P, T])
        xtmp = sb("xtmp", [P, 2, NSEQ, TS])
        amod = sb("amod", [P, KT, S9])
        with ExitStack() as a:
            uext = sb("uext", [P, CT, UE], stack=a)
            z = sb("z", [P, 24, T], stack=a)
            zr = sb("zr", [16, T], stack=a)
            wgate = sb("wgate", [16, HEADS * P], stack=a)
            chunk_start = sb("chunk_start", [P, T], stack=a)
            causal64 = sb("causal64", [P, 2, 64], U32, stack=a)
            causal_s = sb("causal_s", [32, 32], U32, stack=a)
            seqmask = sb("seqmask", [32, NSEQ], stack=a)
            cacc = sb("cacc", [P, T], stack=a)
        with ExitStack() as a:
            gb = sb("gb", [P, T], stack=a)
            geb = sb("geb", [P, T], stack=a)
            gkl = sb("gkl", [P, T], stack=a)
            gs = sb("gs", [P, 4, 256], stack=a)
            vtok = sb("vtok", [P, 2, 256], stack=a)
            vtok_s = sb("vtok_s", [32, 256], stack=a)
            kltok = sb("kltok", [P, 2, P], stack=a)
            klm = sb("klm", [32, NSEQ, P], stack=a)
            att = sb("att", [P, 2, P], stack=a)
            att_s = sb("att_s", [32, 32], stack=a)
        with ExitStack() as a:
            zu = sb("zu", [P, CT, T], stack=a)
            zv = sb("zv", [P, CT, T], stack=a)
            zq = sb("zq", [P, CT, T], stack=a)
            zkv = sb("zkv", [P, 2, T], stack=a)
            dist = sb("dist", [P, 256], stack=a)
            bias_s = sb("bias_s", [P, 4, KEYS], stack=a)
            sinks = sb("sinks", [P, 16 + 4], stack=a)
            vtok1 = sb("vtok1", [P, 2, P], stack=a)
            vnew = sb("vnew", [32, P], stack=a)
            small = sb("small", [P, 6, 16], stack=a)
            qs = sb("qs", [P, NSEQ, CT, TS], stack=a)
            region1 = a.enter_context(ExitStack())
            wsp = sb("wsp", [P, 4, P], stack=region1)
            wsp_s = sb("wsp_s", [32, 4, 32], stack=region1)
            bsp = sb("bsp", [1, 4, T], stack=region1)
            vmix = sb("vmix", [P, 2, 256], stack=region1)
            vmix_s = sb("vmix_s", [32, 256], stack=region1)
            region1.close()
            kcache = sb("kcache", [P, NSEQ, P], stack=a)
            vcache = sb("vcache", [P, NSEQ, P], stack=a)
            ptp = sb("ptp", [P, 2, 512], stack=a)
        with ExitStack() as a:
            sc = sb("sc", [P, 16, 256], stack=a)
        with ExitStack() as a:
            hid_hi = sb("hid_hi", [P, BLK, T], F32R, stack=a)
            hid_lo = sb("hid_lo", [P, BLK, T], F32R, stack=a)
        with ExitStack() as a:
            tn = sb("tn", [P, 2, 4, T], stack=a)
        sb("region", [P, 51712 // 4])
        ps = ctx.enter_context(nc.psum_tensor("ps", [P, 8, 512], F32))
        ADA_BANK, LA_BANK, SEL_BANK, MEAN_BANK, STAT_BANK, M_BANK = 4, 4, 5, 5, 6, 7

        weights_landed = [sem("weights_landed0"), sem("weights_landed1")]
        ada_landed = [sem("ada_landed0"), sem("ada_landed1")]
        cond_w_landed = [sem(f"cond_w_landed{s}") for s in range(4)]
        y_stored = [sem("y_stored0"), sem("y_stored1")]
        (act_links, act_ready, ada_biased, ada_cols, ada_rows, ada_used, att_ready, att_turned, b_ready,
         cache_stored, centred, cond_landed, cond_log, cond_ready, cond_sig, cond_terms, consts_landed,
         conv_affined, conv_log, conv_ready, conv_sig, conv_stored, conv_terms, conv_y, drained, dve_links,
         e_ready, exps, gelu_arg, gelu_sq, gla_rs, gla_y, gla_yy, gsig_log, gsig_ready, gsig_terms,
         gstate_stored, half_done, hi_done, hid_hi_done, hid_ready, history_landed, history_zero, kl_ready,
         kl_turned, kv_landed, la_ready, la_terms, mean_ready, mean_used, mix0_consts, mix1_consts,
         mixed_ready, mixhi_done, ms_ready, nhi_done, normed, ones_set, os_ready, osq_ready, pool_links,
         probs_ready, probs_s_ready, pt_ready, pt_turned, pts_ready, pts_turned, pv_done, qk_ready, qs_ready,
         row_max, rstd_ready, s_chain, sadd_ready, scored, scores_ready, scores_s_ready, sgu_mixed,
         sguv_stored, sig_log, sig_ready, sig_terms, sink_exp, snew_ready, snew_used, split_done, sq_added,
         sq_ready, stat_ready, state_stored, tn_ready, tn_samples, tok_ready, v_ln, v_turned, vmix_ready,
         vmix_turned, vtok1_ready, vtok1_turned, wsp_ready, x_landed, x_updated, y_ready, yd_ready) = (
            sem(name) for name in (
                "act_links", "act_ready", "ada_biased", "ada_cols", "ada_rows", "ada_used", "att_ready",
                "att_turned", "b_ready", "cache_stored", "centred", "cond_landed", "cond_log", "cond_ready",
                "cond_sig", "cond_terms", "consts_landed", "conv_affined", "conv_log", "conv_ready", "conv_sig",
                "conv_stored", "conv_terms", "conv_y", "drained", "dve_links", "e_ready", "exps", "gelu_arg",
                "gelu_sq", "gla_rs", "gla_y", "gla_yy", "gsig_log", "gsig_ready", "gsig_terms", "gstate_stored",
                "half_done", "hi_done", "hid_hi_done", "hid_ready", "history_landed", "history_zero", "kl_ready",
                "kl_turned", "kv_landed", "la_ready", "la_terms", "mean_ready", "mean_used", "mix0_consts",
                "mix1_consts", "mixed_ready", "mixhi_done", "ms_ready", "nhi_done", "normed", "ones_set",
                "os_ready", "osq_ready", "pool_links", "probs_ready", "probs_s_ready", "pt_ready", "pt_turned",
                "pts_ready", "pts_turned", "pv_done", "qk_ready", "qs_ready", "row_max", "rstd_ready", "s_chain",
                "sadd_ready", "scored", "scores_ready", "scores_s_ready", "sgu_mixed", "sguv_stored", "sig_log",
                "sig_ready", "sig_terms", "sink_exp", "snew_ready", "snew_used", "split_done", "sq_added",
                "sq_ready", "stat_ready", "state_stored", "tn_ready", "tn_samples", "tok_ready", "v_ln", "v_turned",
                "vmix_ready", "vmix_turned", "vtok1_ready", "vtok1_turned", "wsp_ready", "x_landed", "x_updated",
                "y_ready", "yd_ready"))
        src = {"zr": t["w_zr"], "gate": t["w_ab"], "zconv": t["w_ab"], "z": t["w_ab"], "kv": t["w_cd"],
               "q": t["w_cd"], "sgu": t["w_cd"], "out": t["w_out"], "gu": t["w_gu"], "down": t["w_dn"]}
        LAYER_STEPS = {"out": KT // 2, "gu": FF_T, "down": 2 * KT}

        def flat(ap):
            return ap.rearrange("p a n -> p (a n)")

        def at(buf, j, lo=0, hi=None):
            hi = buf.shape[-1] if hi is None else hi
            return flat(buf[:, bass.ds(j, 1), lo:hi])

        def seqs(ap):
            return ap.rearrange("p (b t) -> p b t", t=TS)

        def flat_at(buf, j):
            return buf[:, bass.ds(j, 1)]

        def rows_s(j):
            return at(uext, j, UW, UE).rearrange("p (b w) -> p b w", w=SW)

        def taps_s(j, k):
            return rows_s(j)[:, :, k:k + TS]

        y_all = uext[:, :, 0:NP_TOK]
        y_all_s = uext[:, :, UW:UE].rearrange("p c (b w) -> p c b w", w=SW)[:, :, :, 0:TS]

        def unit_uses(u):
            return lin(u[0], 4, 4 * (u[1] - PRE) + (HEADS if u[1] >= 18 else 0))

        def first_unit(u):
            return u[0] is None and u[1] == 0

        def unit_no(u):
            return lin(u[0], 1, u[1])

        def steps_of(seg, i, base):
            for j in range(seg.m):
                k = seg.m * base + j
                yield lin(i, seg.m, seg.n0 + k), (seg.n0 + k) % 2, lin(i, seg.m, k)

        def pre_slot(s):
            return raw[:, s // 2, (s % 2) * 4 * ADA_N:(s % 2 + 1) * 4 * ADA_N]

        block = ctx.enter_context(nc.Block())

        @block.sync
        def _(sp):
            def load_step(seg, n, par, ls):
                if not (isinstance(n, int) and n < 2):
                    sp.wait_ge(split_done, n * 2 - 2)
                rows = src[seg.kind][bass.ds(ls + (seg.first + seg.layer * LAYER_STEPS.get(seg.kind, 0)), 1)]
                sp.dma_start(raw[:, par, 0:seg.width], rows.rearrange("a p n -> p (a n)")) \
                    .then_inc(weights_landed[par], 16)

            def load_ada(u, s):
                if not (u[0] is None and u[1] == PRE and s < 2):
                    sp.wait_ge(ada_used, unit_no(u) * 4 + (s - 1))
                rows = t["w_ada"][bass.ds(unit_no(u) * 4 + s, 1)]
                sp.dma_start(aring[:, s % 2, :], rows.rearrange("a p n -> p (a n)")) \
                    .then_inc(ada_landed[s % 2], 16)

            def load_pre(u, s):
                if not first_unit(u):
                    sp.wait_ge(ada_used, unit_no(u) * 4 + (s - 3))
                rows = t["w_ada"][bass.ds(unit_no(u) * 4 + s, 1)]
                sp.dma_start(pre_slot(s), rows.rearrange("a p n -> p (a n)")).then_inc(cond_w_landed[s], 16)

            def body(seg, i, base, last=False):
                for j, (n, par, ls) in enumerate(steps_of(seg, i, base)):
                    if seg.kind == "zr":
                        sp.wait_ge(ada_used, 4 * PRE)
                    if j == 0 and base == 0 and i is None and seg.kind == "out":
                        pass
                    elif not (last and j == seg.m - 1):
                        load_step(seg, n + 1, 1 - par, ls + 1)
                    elif seg.next:
                        load_step(seg.next, n + 1, 1 - par, 0)
                    if seg.unit is not None:
                        load_ada((i, seg.unit + base), 2 * j)
                        load_ada((i, seg.unit + base), 2 * j + 1)

            def mix0():
                sp.wait_ge(conv_ready, CT)
                sp.dma_start(o["conv_p"], uext[:, :, NP_TOK:UW]).then_inc(conv_stored, 16)
                for j in range(CT):
                    sp.dma_start(o["conv_s"][:, j], rows_s(j)[:, :, TS:SW]).then_inc(conv_stored, 16)
                for h in range(HEADS):
                    if h < 2:
                        sp.wait_ge(ada_used, GLA_A + h - 1)
                    else:
                        sp.wait_ge(state_stored, 16 * (h - 1))
                    sp.dma_start(aring[:, h % 2, :], t["state_glaT"][h]).then_inc(ada_landed[h % 2], 16)
                    if h >= 1:
                        store_states(h - 1)
                store_states(HEADS - 1)
                sp.wait_ge(state_stored, 16 * HEADS)

            def store_states(h):
                sp.wait_ge(s_chain, h + 1)
                sp.dma_start(o["gla_p"][h], gs[:, 3, :]).then_inc(gstate_stored, 16)
                sp.wait_ge(snew_used, 2 * h + 2)
                sp.dma_start(o["gla_s"][h], aring[:, h % 2, :]).then_inc(state_stored, 16)

            def mix1():
                sp.wait_ge(sgu_mixed, CT)
                sp.dma_start(kcache[:], t["cache_kT"]).then_inc(kv_landed, 16)
                sp.dma_start(vcache[:], t["cache_vT"]).then_inc(kv_landed, 16)
                sp.dma_start(o["sgu_v"], zv[:, :, NP_TOK:T]).then_inc(sguv_stored, 16)
                sp.dma_start(o["k_p"], zkv[:, 0, P:NP_TOK]).then_inc(cache_stored, 16)
                sp.dma_start(o["k_s_new"], zkv[:, 0, NP_TOK:T]).then_inc(cache_stored, 16)
                sp.wait_ge(vtok1_ready, 1)
                sp.dma_start(o["v_p"], vtok1[:, 1, :]).then_inc(cache_stored, 16)
                sp.dma_start(o["v_s_new"], vnew[:]).then_inc(cache_stored, 16)
                sp.wait_ge(kv_landed, 32)
                sp.dma_start(o["k_s_old"], kcache[:, :, TS:P]).then_inc(cache_stored, 16)
                sp.dma_start(o["v_s_old"], vcache[TS:P]).then_inc(cache_stored, 16)

            sp.dma_start(cond[:, :, 0:S9], t["cT"]).then_inc(cond_landed, 16)
            sp.dma_start(sel[:], t["sel"]).then_inc(consts_landed, 16)
            sp.dma_start(vec[:], t["vec"]).then_inc(consts_landed, 16)
            sp.dma_start(ident[:], t["ident"]).then_inc(consts_landed, 16)
            for s in range(4):
                load_pre((None, 0), s)
            sp.dma_start(x[:], t["xT"]).then_inc(x_landed, 16)
            with sp.Fori(0, PRE - 1) as i:
                for s in range(4):
                    load_pre((i, 1), s)
            sp.wait_ge(ada_used, 4 * PRE - 3)
            load_step(SEGS[0], 0, 0, 0)
            for seg, after in zip(PLAN, PLAN[1:] + [None]):
                if seg in ("mix0", "mix1"):
                    load_step(after, after.n0 + 1, (after.n0 + 1) % 2, 1)
                if seg == "mix0":
                    mix0()
                elif seg == "mix1":
                    mix1()
                elif seg != "norm":
                    if seg.kind == "gate":
                        sp.wait_ge(act_ready, KT)
                        for name, place in (("gla_w_gate", wgate), ("chunk_start", chunk_start), ("causal64", causal64),
                                            ("causal_s", causal_s), ("seqmask", seqmask)):
                            sp.dma_start(place[:], t[name]).then_inc(mix0_consts, 16)
                        for j in range(CT):
                            sp.dma_start(rows_s(j)[:, :, 0:HIST], t["state_convT"][:, j]).then_inc(history_landed, 16)
                    if seg.kind == "q":
                        sp.wait_ge(act_ready, 4 * KT)
                        for name, place in (("dist", dist), ("bias_s", bias_s), ("sinks", sinks), ("sgu_wT", wsp),
                                            ("sgu_wsT", wsp_s), ("sgu_bT", bsp)):
                            sp.dma_start(place[:], t[name]).then_inc(mix1_consts, 16)
                    if seg.peel:
                        body(seg, None, 0)
                    turns = seg.bodies - 1 - seg.peel
                    if turns:
                        with sp.Fori(0, turns) as i:
                            body(seg, i, seg.peel)
                    body(seg, None, seg.bodies - 1, last=True)
            for g in range(4):
                sp.wait_ge(y_ready, g + 1)
                sp.dma_start(o["y"][:, 4 * g:4 * g + 4, :], tn[:, g % 2]).then_inc(y_stored[g % 2], 16)
            for stored in y_stored:
                sp.wait_ge(stored, 32)
            sp.wait_ge(conv_stored, 16 * (CT + 1))
            sp.wait_ge(gstate_stored, 16 * HEADS)
            sp.wait_ge(cache_stored, 16 * 6)
            sp.wait_ge(sguv_stored, 16)

        @block.gpsimd
        def _(pool):
            L = Links(pool, pool_links)
            pool.memset(ones[:], 1.0).then_inc(ones_set, 1)
            pool.memset(eps[:], EPS).then_inc(ones_set, 1)
            pool.memset(one[:], 1.0).then_inc(ones_set, 1)
            pool.memset(cond[:, :, S9:32], 0.0).then_inc(ones_set, 1)

            def sum_squares(n, q):
                for k in range(n):
                    pool.wait_ge(sq_ready, q + k + 1)
                    if k == 0:
                        if q:
                            pool.wait_ge(stat_ready, SQUARES.index(q))
                        pool.tensor_copy(ssq[:], sqb[:, (q + k) % 2]).then_inc(sq_added, 1)
                    else:
                        pool.wait_ge(sq_added, q + k)
                        pool.tensor_tensor(ssq[:], ssq[:], sqb[:, (q + k) % 2], ALU.add).then_inc(sq_added, 1)

            sum_squares(KT, 0)
            pool.wait_ge(act_ready, KT)
            pool.memset(uext[:, :, 0:HIST], 0.0).then_inc(history_zero, 1)
            sum_squares(CT, 16)
            sum_squares(KT, 24)
            sum_squares(KT, 40)
            pool.wait_ge(mix1_consts, 16 * 6)
            pool.affine_select(out=wsp[:], in_=wsp[:], pattern=[[0, 4], [1, P]], compare_op=ALU.is_ge, fill=0.0,
                               base=0, channel_multiplier=-1).then_inc(wsp_ready, 1)
            L.link(pool.affine_select(out=wsp_s[:], in_=wsp_s[:], pattern=[[0, 4], [1, 32]], compare_op=ALU.is_ge,
                                      fill=0.0, base=0, channel_multiplier=-1))
            pool.affine_select(out=wsp_s[:], in_=wsp_s[:], pattern=[[0, 4], [-TS, NSEQ], [0, TS]],
                               compare_op=ALU.is_ge, fill=0.0, base=0, channel_multiplier=1).then_inc(wsp_ready, 1)
            sum_squares(CT, 56)
            sum_squares(KT, 64)
            sum_squares(KT, 80)

        @block.tensor
        def _(pe):
            sets = [0]
            stats = [0]

            def half(seg, n, par, h, first, hidden=None):
                if h == 0 and not (isinstance(n, int) and n < 2):
                    pe.wait_ge(drained, n - 1)
                pe.wait_ge(split_done, n * 2 + (h + 1))
                hi, lo = (hid_hi, hid_lo) if seg.kind == "down" else (act_hi, act_lo)
                bank = ps[:, 2 * par + (h if seg.two else 0), 0:T]
                for k in range(seg.ktiles):
                    kt = k if seg.two else h * seg.ktiles + k
                    if first and kt % 4 == 0 and (h == 0 or not seg.two):
                        pe.wait_ge(act_ready, sets[0] * KT + kt + 4)
                    if hidden is not None:
                        pe.wait_ge(hid_ready, hidden + kt + 1)
                    cols = slice(k * P, (k + 1) * P)
                    begin = k == 0 and (seg.two or h == 0)
                    end = k == seg.ktiles - 1 and (seg.two or h == 1)
                    pe.matmul(bank, w_hi[:, h, cols], hi[:, kt, :], start=begin, stop=False)
                    pe.matmul(bank, w_lo[:, h, cols], hi[:, kt, :], start=False, stop=False)
                    mm = pe.matmul(bank, w_hi[:, h, cols], lo[:, kt, :], start=False, stop=end)
                mm.then_inc(half_done, 1)

            def ada_slot(u, s, pre=False):
                if pre:
                    slot = pre_slot(s)
                    pe.wait_ge(cond_w_landed[s], unit_no(u) * 16 + 16)
                else:
                    slot = aring[:, s % 2, :]
                    pe.wait_ge(ada_landed[s % 2], (unit_uses(u) + (s - s % 2)) * 8 + 16)
                if s == 0 and not first_unit(u):
                    pe.wait_ge(ada_rows, unit_no(u))
                for j in range(4):
                    mm = pe.matmul(ps[32 * j:32 * j + 32, ADA_BANK, :], cond[:, 4 * s + j, :],
                                   slot[:, j * ADA_N:(j + 1) * ADA_N], start=(s == 0), stop=(s == 3))
                mm.then_inc(ada_used, 1)

            def ada_turn(u):
                pe.wait_ge(ada_rows, unit_no(u) + 1)
                if not first_unit(u):
                    pe.wait_ge(ada_biased, unit_no(u))
                for q in range(4):
                    mm = pe.matmul(ps[:, SEL_BANK, 16 * q:16 * q + S9], adarow[:, q * P:(q + 1) * P], sel[:],
                                   start=True, stop=True)
                mm.then_inc(ada_cols, 1)

            def stat():
                k = stats[0]
                pe.wait_ge(sq_added, SQUARES[k + 1])
                if k:
                    pe.wait_ge(rstd_ready, k)
                pe.matmul(ps[:, STAT_BANK, 0:T], ones[:], ssq[:], start=True, stop=True).then_inc(stat_ready, 1)
                stats[0] += 1

            def conv_mean():
                pe.wait_ge(conv_ready, CT)
                for j in range(CT):
                    pe.matmul(ps[:, M_BANK, 0:NP_TOK], ones[:], y_all[:, j], start=(j == 0), stop=(j == CT - 1))
                for j in range(CT):
                    mm = pe.matmul(ps[:, M_BANK, NP_TOK:T], ones[:], y_all_s[:, j], start=(j == 0), stop=(j == CT - 1))
                mm.then_inc(mean_ready, 1)

            def body(seg, i, base, first=False, hidden=None):
                for j, (n, par, ls) in enumerate(steps_of(seg, i, base)):
                    u = None if seg.unit is None else (i, seg.unit + base)
                    half(seg, n, par, 0, first and j == 0, hidden if j == 0 else None)
                    if seg.kind == "z" and ls == 2:
                        stat()
                    if u and j == 0:
                        ada_slot(u, 0)
                    if u and j == 1:
                        ada_slot(u, 2)
                        ada_slot(u, 3)
                    half(seg, n, par, 1, first and j == 0, hidden if j == 0 else None)
                    if seg.kind == "z" and ls == 0:
                        conv_mean()
                    if u and j == 0:
                        ada_slot(u, 1)
                    if u and j == 1:
                        ada_turn(u)

            def mix0():
                pe.wait_ge(mix0_consts, 16 * 5)
                pe.wait_ge(drained, Z_SEG.n0 + Z_SEG.steps)
                pe.wait_ge(rstd_ready, 2)
                for h in range(HEADS):
                    if h:
                        pe.wait_ge(gla_rs, h)
                    pe.matmul(ps[:, LA_BANK, 0:T], wgate[:, h * P:(h + 1) * P], zr[:], start=True, stop=True) \
                        .then_inc(la_ready, 1)
                    if h:
                        pe.wait_ge(tok_ready, 3 * h)
                        pe.wait_ge(att_ready, h)
                    else:
                        pe.wait_ge(mean_used, 1)
                        pe.wait_ge(ada_biased, 18)
                    v = [z[:, 8 + 2 * h + b, :] for b in range(2)]
                    for b in range(2):
                        for c in range(2):
                            pe.transpose(ps[:, 5, (2 * c + b) * P:(2 * c + b + 1) * P], v[b][:, c * P:(c + 1) * P], ident[:])
                        mm = pe.transpose(ps[0:32, 6, 256 + b * P:256 + (b + 1) * P], v[b][:, NP_TOK:T], ident[:])
                    mm.then_inc(v_turned, 1)
                    pe.wait_ge(kl_ready, h + 1)
                    pe.wait_ge(tok_ready, 3 * h + 1)
                    for c in range(2):
                        pe.transpose(ps[:, 6, c * P:(c + 1) * P], gkl[:, c * P:(c + 1) * P], ident[:])
                    pe.transpose(ps[0:32, 7, 0:P], gkl[:, NP_TOK:T], ident[:]).then_inc(kl_turned, 1)
                    pe.wait_ge(qk_ready, h + 1)
                    q, k = z[:, 2 * h, :], z[:, 2 * h + 1, :]
                    for c in range(4):
                        cs = slice(64 * c, 64 * c + 64)
                        pe.matmul(ps[64 * (c % 2):64 * (c % 2) + 64, 4, 64 * (c // 2):64 * (c // 2) + 64],
                                  k[:, cs], q[:, cs], start=True, stop=True)
                    pe.matmul(ps[0:32, 4, P:P + 32], k[:, NP_TOK:T], q[:, NP_TOK:T], start=True, stop=True) \
                        .then_inc(att_turned, 1)
                    pe.wait_ge(tok_ready, 3 * h + 3)
                    if h:
                        pe.wait_ge(snew_used, 2 * h)
                    for c in range(4):
                        rows = slice(64 * (c % 2), 64 * (c % 2) + 64)
                        mm = pe.matmul(ps[:, c % 2, 256 * (c // 2):256 * (c // 2) + 256], kltok[rows, c // 2, :],
                                       vtok[rows, c // 2, :], start=True, stop=True)
                    mm.then_inc(sadd_ready, 1)
                    pe.wait_ge(att_ready, h + 1)
                    pe.wait_ge(s_chain, h + 1)
                    pe.wait_ge(ada_landed[h % 2], 16 * ((GLA_A - 4 * PRE + h) // 2 + 1))
                    if h:
                        pe.wait_ge(gla_y, h)
                    for b in range(2):
                        vs = slice(b * P, (b + 1) * P)
                        for c in range(4):
                            if c % 2 == 0:
                                pe.matmul(ps[:, 2 + b, 64 * c:64 * c + P], vtok[:, c // 2, vs], att[:, c // 2, :],
                                          start=True, stop=False, skip_group_check=True)
                            if c:
                                pe.matmul(ps[:, 2 + b, 64 * c:64 * c + 64], gs[:, c - 1, vs], q[:, 64 * c:64 * c + 64],
                                          start=False, stop=True, skip_group_check=True)
                        pe.matmul(ps[:, 2 + b, NP_TOK:T], vtok_s[:, vs], att_s[:], start=True, stop=False)
                        for s in range(NSEQ):
                            cols = slice(NP_TOK + TS * s, NP_TOK + TS * s + TS)
                            mm = pe.matmul(ps[:, 2 + b, cols], aring[:, h % 2, 256 * s + b * P:256 * s + (b + 1) * P],
                                           q[:, cols], start=False, stop=(s == NSEQ - 1))
                    mm.then_inc(gla_yy, 1)
                    for r in range(2):
                        if r:
                            pe.wait_ge(snew_used, 2 * h + 1)
                        for s in range(4):
                            mm = pe.matmul(ps[:, s // 2, 256 * (s % 2):256 * (s % 2) + 256], klm[:, 4 * r + s, :],
                                           vtok_s[:], start=True, stop=True)
                        mm.then_inc(snew_ready, 1)
                        if r:
                            pe.wait_ge(osq_ready, h + 1)
                    for b in range(2):
                        mm = pe.matmul(ps[:, 4, 0:T], ones[:], sqb[:, b], start=(b == 0), stop=(b == 1))
                    mm.then_inc(ms_ready, 1)
                pe.wait_ge(snew_used, 2 * HEADS)
                pe.wait_ge(gla_y, HEADS)
                pe.wait_ge(gla_rs, HEADS)

            def mix1():
                pe.wait_ge(drained, SGU_SEG.n0 + SGU_SEG.steps)
                for j in range(CT):
                    mm = pe.matmul(ps[:, MEAN_BANK, 0:T], ones[:], zv[:, j, :], start=(j == 0), stop=(j == CT - 1))
                mm.then_inc(mean_ready, 1)
                stat()
                pe.wait_ge(mix1_consts, 16 * 6)
                pe.wait_ge(wsp_ready, 2)
                pe.wait_ge(mean_used, 2)
                pe.wait_ge(rstd_ready, stats[0])
                for g in range(4):
                    pe.wait_ge(v_ln, 2 * g + 2)
                    if g:
                        pe.wait_ge(vmix_ready, g)
                    for b in range(2):
                        for c in range(2):
                            pe.transpose(ps[:, 5, (2 * c + b) * P:(2 * c + b + 1) * P], zv[:, 2 * g + b, c * P:(c + 1) * P], ident[:])
                        mm = pe.transpose(ps[0:32, 6, b * P:(b + 1) * P], zv[:, 2 * g + b, NP_TOK:T], ident[:])
                    mm.then_inc(vmix_turned, 1)
                    pe.wait_ge(vmix_ready, g + 1)
                    for b in range(2):
                        if g:
                            pe.wait_ge(sgu_mixed, 2 * g + b - 1)
                        bank = ps[:, b, 0:T]
                        vs = slice(b * P, (b + 1) * P)
                        pe.matmul(bank, ones[0:1, :], bsp[0:1, g, :], start=True, stop=False)
                        for c in range(2):
                            pe.matmul(bank[:, c * P:(c + 1) * P], vmix[:, c, vs], wsp[:, g, :], start=False, stop=False)
                        pe.matmul(bank[:, NP_TOK:T], vmix_s[:, vs], wsp_s[:, g, :], start=False, stop=True) \
                            .then_inc(mixed_ready, 1)
                pe.wait_ge(vmix_ready, 4)
                for c in range(2):
                    pe.transpose(ps[:, 5, c * P:(c + 1) * P], zkv[:, 1, c * P:(c + 1) * P], ident[:])
                pe.transpose(ps[0:32, 5, 256:384], zkv[:, 1, NP_TOK:T], ident[:]).then_inc(vtok1_turned, 1)
                for blk in range(2):
                    k0 = 0 if blk else P
                    for h in range(16):
                        g, r = h // 8, h % 8
                        gp = slice(64 * g, 64 * g + 64)
                        if 16 * blk + h >= 4:
                            pe.wait_ge(scored, 16 * blk + h - 3)
                        elif h < 2:
                            pe.wait_ge(sgu_mixed, CT)
                        if blk and h == 2:
                            pe.wait_ge(yd_ready, 1)
                        pe.matmul(ps[:, h % 4, k0:256], zq[gp, r, blk * P:(blk + 1) * P],
                                  zkv[gp, 0, blk * P - P + k0:(blk + 1) * P], start=True, stop=True).then_inc(scores_ready, 1)
                    pe.wait_ge(vtok1_ready, 1)
                    for h in range(16):
                        g, r = h // 8, h % 8
                        turn = 16 * blk + h
                        pe.wait_ge(probs_ready, turn + 1)
                        if turn >= 2:
                            pe.wait_ge(pt_ready, turn - 1)
                        for kb in range(1 - blk, 2):
                            mm = pe.transpose(ps[:, 6 + turn % 2, kb * P:(kb + 1) * P], sc[:, h, kb * P:(kb + 1) * P], ident[:])
                        mm.then_inc(pt_turned, 1)
                        pe.wait_ge(pt_ready, turn + 1)
                        if h == 0:
                            pe.wait_ge(scored, 16 * blk + 16)
                        for kb in range(1 - blk, 2):
                            mm = pe.matmul(ps[64 * g:64 * g + 64, 2 + r // 4, (r % 4) * P:(r % 4 + 1) * P],
                                           vtok1[:, blk - 1 + kb, 64 * g:64 * g + 64], ptp[:, turn % 2, kb * P:(kb + 1) * P],
                                           start=(kb == 1 - blk), stop=(kb == 1))
                        mm.then_inc(pv_done, 1)
                pe.wait_ge(kv_landed, 32)
                pe.wait_ge(qs_ready, 1)
                pe.wait_ge(yd_ready, 2)
                for s in range(NSEQ):
                    for g in range(2):
                        gp = slice(64 * g, 64 * g + 64)
                        out = ps[32 * (s % 4):32 * (s % 4) + 32, 2 * (s // 4) + g, 0:KEYS]
                        rows = qs[gp, s].rearrange("p r t -> p (r t)")
                        pe.matmul(out[:, 0:P], rows, kcache[gp, s, :], start=True, stop=True)
                        mm = pe.matmul(out[:, P:KEYS], rows, zkv[gp, 0, NP_TOK:T], start=True, stop=True)
                mm.then_inc(scores_s_ready, 1)
                pe.wait_ge(probs_s_ready, 1)
                for c in range(4):
                    pe.transpose(ps[:, 4, c * P:(c + 1) * P], sc[:, c, 0:P], ident[:])
                for c in range(4):
                    mm = pe.transpose(ps[0:32, 5, c * P:(c + 1) * P], sc[:, c, P:KEYS], ident[:])
                mm.then_inc(pts_turned, 1)
                pe.wait_ge(pts_ready, 1)
                for s in range(NSEQ):
                    for g in range(2):
                        c = 2 * (s // 4) + g
                        out = ps[64 * g:64 * g + 64, 0, 32 * s:32 * s + 32]
                        cols = slice(c * P + 32 * (s % 4), c * P + 32 * (s % 4) + 32)
                        pe.matmul(out, vcache[:, s, 64 * g:64 * g + 64], ptp[:, 0, cols], start=True, stop=False)
                        mm = pe.matmul(out, vnew[:, 64 * g:64 * g + 64], ptp[0:32, 1, cols], start=False, stop=True)
                mm.then_inc(os_ready, 1)
                pe.wait_ge(act_ready, KT * (sets[0] + 1))

            pe.wait_ge(consts_landed, 48)
            pe.wait_ge(cond_ready, 1)
            pe.wait_ge(ones_set, 4)
            for s in range(4):
                ada_slot((None, 0), s, pre=True)
            ada_turn((None, 0))
            with pe.Fori(0, PRE - 1) as i:
                for s in range(4):
                    ada_slot((i, 1), s, pre=True)
                ada_turn((i, 1))
            stat()
            fresh, blocks = True, 0
            for seg in PLAN:
                if seg in ("norm", "mix0", "mix1"):
                    {"norm": stat, "mix0": mix0, "mix1": mix1}[seg]()
                    fresh = True
                    continue
                if seg.kind == "down":
                    blocks += 1
                start = 0
                if (seg.opens or seg.bodies == 2) and not fresh:
                    body(seg, None, 0)
                    start = 1
                if seg.kind == "down":
                    body(seg, None, 0, hidden=BLK * (blocks - 1))
                    start = 1
                if fresh and seg.kind != "down":
                    body(seg, None, 0, first=True)
                    start = 1
                    sets[0] += 1
                    fresh = False
                if seg.bodies > start:
                    if seg.bodies - start > 1:
                        with pe.Fori(0, seg.bodies - start) as i:
                            body(seg, i, start)
                    else:
                        body(seg, None, start)

        @block.scalar
        def _(act):
            L = Links(act, act_links)
            sums = [0]

            def split(seg, n, par, h):
                act.wait_ge(weights_landed[par], (n - par) * 8 + 16)
                if not (isinstance(n, int) and n == 0):
                    act.wait_ge(half_done, n * 2 + (h - 1))
                w = seg.width // 2
                act.activation(w_hi[:, h, 0:w], raw[:, par, h * w:(h + 1) * w], ACT.Copy).then_inc(hi_done, 1)

            def log_terms(out, in_, scale=1.0, bias=0.0):
                L.link(act.activation(out, in_, ACT.Abs, scale=scale, bias=bias))
                L.link(act.activation(out, out, ACT.Exp, scale=-1.0))
                return act.activation(out, out, ACT.Ln, bias=one[0:out.shape[0], :])

            def make_rstd(n, bank=STAT_BANK):
                L.link(act.activation(rstd[:], ps[:, bank, 0:T], ACT.Ln, scale=1.0 / n, bias=eps[:]))
                return act.activation(rstd[:], rstd[:], ACT.Exp, scale=-0.5)

            def stat_rstd(n):
                sums[0] += 1
                act.wait_ge(stat_ready, sums[0])
                make_rstd(n).then_inc(rstd_ready, 1)

            def wait_square(q):
                if not (isinstance(q, int) and q < 2):
                    act.wait_ge(sq_added, q - 1)

            def epilogue(seg, n, par, ls):
                b0, b1 = ps[:, 2 * par, 0:T], ps[:, 2 * par + 1, 0:T]
                act.wait_ge(half_done, n * 2 + 2)
                if seg.kind != "zr":
                    act.wait_ge(drained, n)
                if seg.kind == "zr":
                    act.activation(zr[:], ps[0:16, 2 * par, 0:T], ACT.Copy).then_inc(drained, 1)
                elif seg.kind in ("zconv", "z"):
                    act.activation(at(z, ls * 2 + seg.group), b0, ACT.Copy)
                    act.activation(at(z, ls * 2 + (seg.group + 1)), b1, ACT.Copy).then_inc(drained, 1)
                elif seg.kind == "kv":
                    act.activation(zkv[:, 0, :], b0, ACT.Copy)
                    act.activation(zkv[:, 1, :], b1, ACT.Copy).then_inc(drained, 1)
                elif seg.kind == "q":
                    act.activation(at(zq, ls * 2), b0, ACT.Copy, scale=0.125)
                    act.activation(at(zq, ls * 2 + 1), b1, ACT.Copy, scale=0.125).then_inc(drained, 1)
                elif seg.kind in ("gate", "gu"):
                    k = ls + seg.sig0
                    log_terms(sg[:, 0], b1 if seg.kind == "gate" else b0).then_inc(sig_terms, 1)
                    act.wait_ge(sig_log, k + 1)
                    act.activation(sg[:, 0], sg[:, 0], ACT.Exp).then_inc(sig_ready, 1)
                    if seg.kind == "gu":
                        act.wait_ge(drained, n + 1)
                        act.activation(at(hid_hi, ls + seg.first % BLK), prod[:], ACT.Copy).then_inc(hid_hi_done, 1)
                elif seg.kind == "sgu":
                    for b, bank in enumerate((b0, b1)):
                        act.activation(sqb[:, b], bank, ACT.Square, scale=GELU_K ** 0.5).then_inc(gelu_sq, 1)
                    for b in range(2):
                        act.wait_ge(gelu_arg, ls * 2 + (seg.gel0 + b + 1))
                        log_terms(sg[:, b], sqb[:, b]).then_inc(sig_terms, 1)
                    for b in range(2):
                        act.wait_ge(sig_log, ls * 2 + (seg.sig0 + b + 1))
                        act.activation(sg[:, b], sg[:, b], ACT.Exp).then_inc(sig_ready, 1)
                elif seg.kind == "out" or seg.group:
                    for b in range(2 if seg.two else 1):
                        j = ls * 2 + b if seg.two else ls
                        act.wait_ge(x_updated, j + (seg.x0 + 1))
                        q = j + seg.q0
                        wait_square(q)
                        act.activation(sqb[:, b if seg.two else (seg.q0 + par + seg.n0) % 2], at(x, j), ACT.Square).then_inc(sq_ready, 1)

            def ada_copy(u):
                act.wait_ge(ada_used, unit_no(u) * 4 + 4)
                if not first_unit(u):
                    act.wait_ge(ada_cols, unit_no(u))
                act.activation(adarow[:], ps[:, ADA_BANK, :], ACT.Copy).then_inc(ada_rows, 1)

            def conv_squares():
                for j in range(CT):
                    q = 16 + j
                    wait_square(q)
                    act.activation(sqb[:, q % 2, 0:NP_TOK], y_all[:, j], ACT.Square)
                    act.activation(seqs(sqb[:, q % 2, NP_TOK:T]), y_all_s[:, j], ACT.Square).then_inc(sq_ready, 1)

            def conv_affine():
                for j in range(CT):
                    gj, bj = VEC["conv_ln_g"] + j, VEC["conv_ln_b"] + j
                    for y in (y_all[:, j], y_all_s[:, j]):
                        ins = act.activation(y, y, ACT.Identity, scale=vec[:, gj:gj + 1], bias=vec[:, bj:bj + 1])
                ins.then_inc(conv_affined, 1)

            def conv_silu(k):
                if k < CT // 2:
                    s, js = (sg, sqb)[k % 2], slice(2 * k, 2 * k + 2)
                    if k >= 2:
                        act.wait_ge(conv_y, k - 1)
                    L.mark(act.activation(s[:, :, 0:NP_TOK], y_all[:, js], ACT.Abs))
                    for b in range(2):
                        ins = act.activation(seqs(s[:, b, NP_TOK:T]), y_all_s[:, 2 * k + b], ACT.Abs)
                        L.mark(ins)
                    L.wait(L.n)
                    L.link(act.activation(s[:], s[:], ACT.Exp, scale=-1.0))
                    act.activation(s[:], s[:], ACT.Ln, bias=one[:]).then_inc(conv_terms, 1)
                if k:
                    s = (sg, sqb)[(k - 1) % 2]
                    act.wait_ge(conv_log, k)
                    act.activation(s[:], s[:], ACT.Exp).then_inc(conv_sig, 1)

            def body(seg, i, base, last=False):
                for j, (n, par, ls) in enumerate(steps_of(seg, i, base)):
                    end = last and j == seg.m - 1
                    nxt = seg.next if end else seg
                    hurry = end and seg.then_wait
                    if nxt:
                        split(nxt, n + 1, 1 - par, 0)
                    if seg.unit is not None and j == 1:
                        ada_copy((i, seg.unit + base))
                    if seg.kind == "z" and ls == 2:
                        stat_rstd(CT * P)
                    if seg.kind == "z" and ls == 3:
                        act.wait_ge(conv_affined, 1)
                        for k in range(3):
                            conv_silu(k)
                    if nxt and not hurry:
                        split(nxt, n + 1, 1 - par, 1)
                    epilogue(seg, n, par, ls)
                    if seg.kind == "z" and ls == 1:
                        act.wait_ge(centred, 1)
                        conv_squares()
                    if seg.kind == "z" and ls == 2:
                        act.wait_ge(normed, 1)
                        conv_affine()
                    if nxt and hurry:
                        split(nxt, n + 1, 1 - par, 1)

            def norm(k, final=False):
                stat_rstd(D)
                layer, part = divmod(k, 2)
                shift = layer * 96 + part * 48
                for g in range(4):
                    act.wait_ge(tn_ready, 4 * k + g + 1)
                    for b in range(4):
                        j = 4 * g + b
                        if final:
                            ins = act.activation(tn[:, g % 2, b, :], tn[:, g % 2, b, :], ACT.Copy,
                                                 scale=vec[:, VEC["g_final"] + j:VEC["g_final"] + j + 1])
                        else:
                            ins = act.activation(tn[:, g % 2, b, 0:NP_TOK], tn[:, g % 2, b, 0:NP_TOK], ACT.Identity,
                                                 scale=amod[:, j, 0:1], bias=mods[:, shift + j, 0:1])
                    if final:
                        ins.then_inc(y_ready, 1)
                        continue
                    L.link(ins)
                    act.wait_ge(tn_samples, 4 * k + g + 1)
                    act.activation(act_hi[:, 4 * g:4 * g + 4, :], tn[:, g % 2], ACT.Copy).then_inc(nhi_done, 1)

            def mix0():
                conv_silu(3)
                conv_silu(4)
                act.wait_ge(conv_y, CT // 2)
                act.activation(act_hi[:, 0:CT, 0:NP_TOK], y_all, ACT.Copy)
                for s in range(NSEQ):
                    ins = act.activation(act_hi[:, 0:CT, NP_TOK + TS * s:NP_TOK + TS * (s + 1)], y_all_s[:, :, s], ACT.Copy)
                ins.then_inc(mixhi_done, CT)
                act.wait_ge(act_ready, KT + CT)
                act.wait_ge(conv_stored, 16 * (CT + 1))
                for h in range(HEADS):
                    act.wait_ge(la_ready, h + 1)
                    if h:
                        act.wait_ge(act_ready, KT + CT + 2 * h)
                    bg = VEC["gla_b_gate"] + h
                    log_terms(sg[:, 0], ps[:, LA_BANK, 0:T], bias=vec[:, bg:bg + 1]).then_inc(la_terms, 1)
                    act.wait_ge(v_turned, h + 1)
                    act.activation(vtok[:].rearrange("p c n -> p (c n)"), ps[:, 5, :], ACT.Copy)
                    act.activation(vtok_s[:], ps[0:32, 6, 256:512], ACT.Copy).then_inc(tok_ready, 1)
                    act.wait_ge(b_ready, h + 1)
                    act.activation(geb[:], gb[:], ACT.Exp, scale=1.0 / 16)
                    act.activation(prod[:], gb[:], ACT.Exp, scale=-1.0 / 16)
                    act.activation(sg[:, 0], sg[:, 0], ACT.Exp, scale=1.0 / 16).then_inc(e_ready, 1)
                    act.wait_ge(kl_turned, h + 1)
                    act.activation(kltok[:].rearrange("p c n -> p (c n)"), ps[:, 6, 0:256], ACT.Copy).then_inc(tok_ready, 1)
                    act.wait_ge(qk_ready, h + 1)
                    log_terms(sg[:], z[:, 16 + 2 * h:18 + 2 * h, :]).then_inc(gsig_terms, 1)
                    act.wait_ge(gsig_log, h + 1)
                    act.activation(sg[:], sg[:], ACT.Exp).then_inc(gsig_ready, 1)
                    act.wait_ge(gla_yy, h + 1)
                    act.activation(sqb[:], ps[:, 2:4, 0:T], ACT.Square).then_inc(osq_ready, 1)
                    act.wait_ge(ms_ready, h + 1)
                    make_rstd(256, 4).then_inc(gla_rs, 1)
                    act.wait_ge(gla_y, h + 1)
                    act.activation(act_hi[:, CT + 2 * h:CT + 2 * h + 2, :], sqb[:], ACT.Copy).then_inc(mixhi_done, 1)

            def mix1():
                act.wait_ge(centred, 2)
                for j in range(CT):
                    q = 56 + j
                    wait_square(q)
                    act.activation(sqb[:, q % 2], zv[:, j, :], ACT.Square).then_inc(sq_ready, 1)
                stat_rstd(CT * P)
                act.wait_ge(normed, 2)
                for j in range(CT):
                    gj, bj = VEC["sgu_ln_g"] + j, VEC["sgu_ln_b"] + j
                    act.activation(zv[:, j, :], zv[:, j, :], ACT.Identity, scale=vec[:, gj:gj + 1],
                                   bias=vec[:, bj:bj + 1]).then_inc(v_ln, 1)
                for g in range(4):
                    act.wait_ge(vmix_turned, g + 1)
                    if g:
                        act.wait_ge(mixed_ready, 2 * g)
                    act.activation(vmix[:].rearrange("p c n -> p (c n)"), ps[:, 5, :], ACT.Copy)
                    act.activation(vmix_s[:], ps[0:32, 6, 0:256], ACT.Copy).then_inc(vmix_ready, 1)
                act.wait_ge(vtok1_turned, 1)
                act.activation(vtok1[:].rearrange("p c n -> p (c n)"), ps[:, 5, 0:256], ACT.Copy)
                act.activation(vnew[:], ps[0:32, 5, 256:384], ACT.Copy).then_inc(vtok1_ready, 1)
                act.wait_ge(sgu_mixed, CT)
                act.activation(act_hi[:, 0:CT, :], zu[:], ACT.Copy).then_inc(mixhi_done, 1)
                for blk in range(2):
                    k0 = 0 if blk else P
                    act.wait_ge(row_max, blk + 1)
                    act.activation(small[:, 2, :], small[:, 2, :], ACT.Exp).then_inc(sink_exp, 1)
                    for h in range(16):
                        act.activation(sc[:, h, k0:256], sc[:, h, k0:256], ACT.Exp, bias=small[:, 1, h:h + 1],
                                       accum_out=small[:, 3, h:h + 1]).then_inc(exps, 1)
                    for h in range(16):
                        turn = 16 * blk + h
                        act.wait_ge(pt_turned, turn + 1)
                        if turn >= 2:
                            act.wait_ge(pv_done, turn - 1)
                        act.activation(ptp[:, turn % 2, k0:256], ps[:, 6 + turn % 2, k0:256], ACT.Copy).then_inc(pt_ready, 1)
                act.wait_ge(row_max, 3)
                act.activation(small[:, 2, 0:4], small[:, 2, 0:4], ACT.Exp).then_inc(sink_exp, 1)
                for c in range(4):
                    act.activation(sc[:, c, 0:KEYS], sc[:, c, 0:KEYS], ACT.Exp, bias=small[:, 1, c:c + 1],
                                   accum_out=small[:, 3, c:c + 1]).then_inc(exps, 1)
                act.wait_ge(pts_turned, 1)
                act.wait_ge(pv_done, 32)
                act.activation(ptp[:, 0, :], ps[:, 4, :], ACT.Copy)
                act.activation(ptp[0:32, 1, :], ps[0:32, 5, :], ACT.Copy).then_inc(pts_ready, 1)
                act.wait_ge(yd_ready, 3)
                act.activation(act_hi[:, CT:KT, :], zq[:], ACT.Copy).then_inc(mixhi_done, 1)

            act.preload_act_table_set("natural_log_exp_and_others")
            act.wait_ge(ones_set, 4)
            act.wait_ge(cond_landed, 16)
            cols = sg[:, 0, 0:KT * S9].rearrange("p (k s) -> p k s", s=S9)
            log_terms(cols, cond[:, :, 0:S9]).then_inc(cond_terms, 1)
            act.wait_ge(cond_log, 1)
            act.activation(cols, cols, ACT.Exp).then_inc(cond_sig, 1)
            def squares_of_x(j):
                for b in range(2):
                    wait_square(j + b)
                    act.activation(sqb[:, b], at(x, j + b), ACT.Square).then_inc(sq_ready, 1)

            act.wait_ge(cond_ready, 1)
            ada_copy((None, 0))
            act.wait_ge(x_landed, 16)
            squares_of_x(0)
            with act.Fori(0, PRE - 1) as i:
                ada_copy((i, 1))
                squares_of_x(2 * i + 2)
            split(SEGS[0], 0, 0, 0)
            split(SEGS[0], 0, 0, 1)
            norms = 0
            for seg in ["norm"] + PLAN:
                if seg == "norm":
                    norm(norms, final=norms == 4)
                    norms += 1
                elif seg == "mix0":
                    mix0()
                elif seg == "mix1":
                    mix1()
                else:
                    if seg.peel:
                        body(seg, None, 0)
                    turns = seg.bodies - 1 - seg.peel
                    if turns:
                        with act.Fori(0, turns) as i:
                            L.enter(i, seg.act_links)
                            body(seg, i, seg.peel)
                            L.leave(turns)
                    body(seg, None, seg.bodies - 1, last=True)

        @block.vector
        def _(dve):
            L = Links(dve, dve_links)

            def split_lo(seg, n, par, h):
                dve.wait_ge(hi_done, n * 2 + (h + 1))
                w = seg.width // 2
                dve.tensor_tensor(w_lo[:, h, 0:w], raw[:, par, h * w:(h + 1) * w], w_hi[:, h, 0:w].bitcast(F32),
                                  ALU.subtract).then_inc(split_done, 1)

            def resid(seg, bank, j, b, first_inc, last_inc):
                g = (seg.layer * 96 + (2 if seg.kind == "out" else 5) * KT) + j
                tmp = xtmp[:, b]
                if last_inc:
                    if not (isinstance(j, int) and j + seg.x0 < 1):
                        dve.wait_ge(x_updated, j + seg.x0)
                if L.n:
                    L.wait(L.n)
                m = L.mark(dve.tensor_tensor(tmp, seqs(bank[:, NP_TOK:T]),
                                             at(mods, g, 1, S9).unsqueeze(2).to_broadcast([P, NSEQ, TS]), ALU.mult))
                ins = dve.scalar_tensor_tensor(at(x, j, 0, NP_TOK), bank[:, 0:NP_TOK], at(mods, g, 0, 1),
                                               at(x, j, 0, NP_TOK), ALU.mult, ALU.add)
                if first_inc:
                    ins.then_inc(first_inc, 1)
                L.wait(m)
                ins = dve.tensor_tensor(seqs(at(x, j, NP_TOK, T)), seqs(at(x, j, NP_TOK, T)), tmp, ALU.add)
                if last_inc:
                    ins.then_inc(last_inc, 1)
                else:
                    L.mark(ins)

            def epilogue(seg, n, par, ls):
                if seg.kind in ("zr", "zconv", "z", "kv", "q"):
                    return
                b0, b1 = ps[:, 2 * par, 0:T], ps[:, 2 * par + 1, 0:T]
                dve.wait_ge(half_done, n * 2 + 2)
                dve.wait_ge(drained, n)
                if seg.kind in ("gate", "gu"):
                    k = ls + seg.sig0
                    s, gate_bank = sg[:, 0], b1 if seg.kind == "gate" else b0
                    dve.wait_ge(sig_terms, k + 1)
                    dve.scalar_tensor_tensor(s, gate_bank, 0.0, s, ALU.min, ALU.subtract).then_inc(sig_log, 1)
                    dve.wait_ge(sig_ready, k + 1)
                    if seg.kind == "gate":
                        dve.tensor_tensor(at(uext, ls, HIST, UW), b0[:, 0:NP_TOK], s[:, 0:NP_TOK], ALU.mult)
                        dve.tensor_tensor(rows_s(ls)[:, :, HIST:SW], seqs(b0[:, NP_TOK:T]), seqs(s[:, NP_TOK:T]),
                                          ALU.mult).then_inc(drained, 1)
                    else:
                        hid = ls + (seg.sig0 - CT - (2 * CT if seg.layer else 0))
                        if not (isinstance(hid, int) and hid == 0):
                            dve.wait_ge(hid_ready, hid)
                        L.link(dve.tensor_tensor(prod[:], b0, s, ALU.mult))
                        dve.tensor_tensor(prod[:], prod[:], b1, ALU.mult).then_inc(drained, 1)
                        j = ls + seg.first % BLK
                        dve.wait_ge(hid_hi_done, hid + 1)
                        dve.tensor_tensor(at(hid_lo, j), prod[:], at(hid_hi, j).bitcast(F32), ALU.subtract) \
                            .then_inc(hid_ready, 1)
                elif seg.kind == "sgu":
                    for b, bank in enumerate((b0, b1)):
                        dve.wait_ge(gelu_sq, ls * 2 + (seg.gel0 + b + 1))
                        dve.scalar_tensor_tensor(sqb[:, b], sqb[:, b], GELU_2C, bank, ALU.add, ALU.mult) \
                            .then_inc(gelu_arg, 1)
                    for b in range(2):
                        dve.wait_ge(sig_terms, ls * 2 + (seg.sig0 + b + 1))
                        dve.scalar_tensor_tensor(sg[:, b], sqb[:, b], 0.0, sg[:, b], ALU.min, ALU.subtract) \
                            .then_inc(sig_log, 1)
                    for b, (bank, out) in enumerate(((b0, zu), (b1, zv))):
                        dve.wait_ge(sig_ready, ls * 2 + (seg.sig0 + b + 1))
                        ins = dve.tensor_tensor(at(out, ls), bank, sg[:, b], ALU.mult)
                    ins.then_inc(drained, 1)
                elif seg.kind == "out":
                    resid(seg, b0, ls * 2, 0, None, x_updated)
                    resid(seg, b1, ls * 2 + 1, 1, drained, x_updated)
                else:
                    resid(seg, b0, ls, 0, drained, x_updated if seg.group else None)

            def conv(j, taps, marks):
                w = VEC["conv_w"]
                if 0 in taps:
                    if not (isinstance(j, int) and j == 0):
                        dve.wait_ge(conv_ready, j)
                    if L.n:
                        L.wait(L.n)
                for k in taps:
                    wk = flat_at(vec, j * TAPS + (w + k))
                    for s in range(2):
                        row = taps_s(j, k) if s else at(uext, j, k, k + NP_TOK)
                        acc = seqs(cacc[:, NP_TOK:T]) if s else cacc[:, 0:NP_TOK]
                        out = acc if k < TAPS - 1 else taps_s(j, 0) if s else at(uext, j, 0, NP_TOK)
                        if marks[s]:
                            L.wait(marks[s])
                        if k == 0:
                            ins = dve.tensor_scalar(out, row, wk, flat_at(vec, j + VEC["conv_b"]), ALU.mult, ALU.add)
                        else:
                            ins = dve.scalar_tensor_tensor(out, row, wk, acc, ALU.mult, ALU.add)
                        if k == TAPS - 1 and s:
                            ins.then_inc(conv_ready, 1)
                        else:
                            marks[s] = L.mark(ins)

            def ada_bias(u):
                dve.wait_ge(ada_cols, unit_no(u) + 1)
                b = bass.ds(unit_no(u) * 4 + VEC["b_ada"], 4)
                dve.tensor_tensor(mods[:, bass.ds(unit_no(u) * 4, 4), :],
                                  ps[:, SEL_BANK, 0:64].rearrange("p (q s) -> p q s", s=16)[:, :, 0:S9],
                                  vec[:, b].unsqueeze(2).to_broadcast([P, 4, S9]), ALU.add).then_inc(ada_biased, 1)

            def body(seg, i, base, last=False):
                marks = [0, 0]
                convolves, opening = seg.kind in ("gate", "zconv"), seg.kind == "gate" and i is None and base == 0
                tile = lin(i, 1, base + (4 if seg.kind == "zconv" else 0))
                for j, (n, par, ls) in enumerate(steps_of(seg, i, base)):
                    end = last and j == seg.m - 1
                    nxt = seg.next if end else seg
                    hurry = end and seg.then_wait
                    if nxt:
                        split_lo(nxt, n + 1, 1 - par, 0)
                        if seg.kind == "z" and ls == 3:
                            for k in range(3):
                                conv_silu(k)
                        if convolves and not (opening and j == 0):
                            conv(tile, range(8) if j == 0 else range(16, 24) if not opening else range(16, 20), marks)
                        if not hurry:
                            split_lo(nxt, n + 1, 1 - par, 1)
                    if seg.kind == "z" and ls == 0:
                        centre(1, y_all, y_all_s, M_BANK)
                    if seg.kind == "z" and ls == 2:
                        dve.wait_ge(rstd_ready, 2)
                        apply_stat(y_all, y_all_s, rstd, ALU.mult).then_inc(normed, 1)
                    epilogue(seg, n, par, ls)
                    if nxt and hurry:
                        split_lo(nxt, n + 1, 1 - par, 1)
                    if seg.unit is not None and j == 1:
                        ada_bias((i, seg.unit + base))
                    if convolves and opening and j == 0:
                        dve.wait_ge(drained, n + 1)
                        conv(tile, range(16), marks)
                    elif convolves:
                        conv(tile, range(8, 16) if j == 0 else range(24, TAPS) if not opening else range(20, TAPS), marks)

            def norm(k, final=False):
                layer, part = divmod(k, 2)
                if not final:
                    scale = layer * 96 + part * 48 + KT
                    g = VEC["g_ffn" if part else "g_mix"] + KT * layer
                    L.link(dve.scalar_tensor_tensor(amod[:], mods[:, scale:scale + KT, :], 1.0,
                                                    vec[:, g:g + KT].unsqueeze(2).to_broadcast([P, KT, S9]),
                                                    ALU.add, ALU.mult))
                shift = layer * 96 + part * 48
                base = KT * [0, 2, 3, 5, 6][k]
                if base:
                    dve.wait_ge(act_ready, base)
                dve.wait_ge(rstd_ready, NORM_STATS[k])

                def scaled(g):
                    if final and g >= 2:
                        dve.wait_ge(y_stored[g % 2], 16)
                    elif g >= 2:
                        dve.wait_ge(act_ready, base + 4 * (g - 1))
                    dve.tensor_tensor(tn[:, g % 2], x[:, 4 * g:4 * g + 4, :],
                                      rstd[:].unsqueeze(1).to_broadcast([P, 4, T]), ALU.mult).then_inc(tn_ready, 1)

                def samples(g):
                    dve.wait_ge(tn_ready, 4 * k + g + 1)
                    cols = tn[:, g % 2, :, NP_TOK:T].rearrange("p k (b t) -> p k b t", t=TS)
                    js = slice(4 * g, 4 * g + 4)
                    L.link(dve.tensor_tensor(cols, cols, amod[:, js, 1:S9].unsqueeze(3).to_broadcast([P, 4, NSEQ, TS]), ALU.mult))
                    dve.tensor_tensor(cols, cols, mods[:, shift + 4 * g:shift + 4 * g + 4, 1:S9].unsqueeze(3)
                                      .to_broadcast([P, 4, NSEQ, TS]), ALU.add).then_inc(tn_samples, 1)

                def lo(g):
                    dve.wait_ge(nhi_done, 4 * k + g + 1)
                    js = slice(4 * g, 4 * g + 4)
                    dve.tensor_tensor(act_lo[:, js, :], tn[:, g % 2], act_hi[:, js, :].bitcast(F32), ALU.subtract) \
                        .then_inc(act_ready, 4)

                for g in range(4):
                    scaled(g)
                    if not final:
                        samples(g)
                        if g:
                            lo(g - 1)
                if not final:
                    lo(3)

            def centre(k, y, y_s, bank):
                dve.wait_ge(mean_ready, k)
                dve.tensor_scalar(prod[:], ps[:, bank, 0:T], 1.0 / (CT * P), None, ALU.mult).then_inc(mean_used, 1)
                dve.wait_ge(mean_used, k)
                apply_stat(y, y_s, prod, ALU.subtract).then_inc(centred, 1)

            def apply_stat(y, y_s, by, op):
                if y_s is None:
                    return dve.tensor_tensor(y, y, by[:].unsqueeze(1).to_broadcast([P, CT, T]), op)
                dve.tensor_tensor(y, y, by[:, 0:NP_TOK].unsqueeze(1).to_broadcast([P, CT, NP_TOK]), op)
                for s in range(NSEQ):
                    cols = by[:, NP_TOK + TS * s:NP_TOK + TS * (s + 1)].unsqueeze(1).to_broadcast([P, CT, TS])
                    ins = dve.tensor_tensor(y_s[:, :, s], y_s[:, :, s], cols, op)
                return ins

            def conv_silu(k):
                if k < CT // 2:
                    s, js = (sg, sqb)[k % 2], slice(2 * k, 2 * k + 2)
                    dve.wait_ge(conv_terms, k + 1)
                    dve.scalar_tensor_tensor(s[:, :, 0:NP_TOK], y_all[:, js], 0.0, s[:, :, 0:NP_TOK], ALU.min, ALU.subtract)
                    for b in range(2):
                        ss = seqs(s[:, b, NP_TOK:T])
                        ins = dve.scalar_tensor_tensor(ss, y_all_s[:, 2 * k + b], 0.0, ss, ALU.min, ALU.subtract)
                    ins.then_inc(conv_log, 1)
                if k:
                    s, js = (sg, sqb)[(k - 1) % 2], slice(2 * k - 2, 2 * k)
                    dve.wait_ge(conv_sig, k)
                    dve.tensor_tensor(y_all[:, js], y_all[:, js], s[:, :, 0:NP_TOK], ALU.mult)
                    for b in range(2):
                        y = y_all_s[:, 2 * k - 2 + b]
                        ins = dve.tensor_tensor(y, y, seqs(s[:, b, NP_TOK:T]), ALU.mult)
                    ins.then_inc(conv_y, 1)

            def mix0():
                conv_silu(3)
                conv_silu(4)
                dve.wait_ge(mixhi_done, CT)
                dve.tensor_tensor(act_lo[:, 0:CT, 0:NP_TOK], y_all, act_hi[:, 0:CT, 0:NP_TOK].bitcast(F32), ALU.subtract)
                for s in range(NSEQ):
                    cols = slice(NP_TOK + TS * s, NP_TOK + TS * (s + 1))
                    ins = dve.tensor_tensor(act_lo[:, 0:CT, cols], y_all_s[:, :, s], act_hi[:, 0:CT, cols].bitcast(F32), ALU.subtract)
                ins.then_inc(act_ready, CT)
                dve.wait_ge(mix0_consts, 16 * 5)
                dve.wait_ge(conv_stored, 16 * (CT + 1))
                dve.wait_ge(act_ready, KT + CT)
                L.link(dve.memset(att[:], 0.0))
                L.link(dve.memset(att_s[:], 0.0))
                for h in range(HEADS):
                    q, k = z[:, 2 * h, :], z[:, 2 * h + 1, :]
                    dve.wait_ge(la_ready, h + 1)
                    dve.wait_ge(act_ready, KT + CT + 2 * h)
                    bg = VEC["gla_b_gate"] + h
                    dve.wait_ge(la_terms, h + 1)
                    L.link(dve.tensor_scalar(sg[:, 1], ps[:, LA_BANK, 0:T], vec[:, bg:bg + 1], 0.0, ALU.add, ALU.min))
                    L.link(dve.tensor_tensor(sg[:, 1], sg[:, 1], sg[:, 0], ALU.subtract))
                    L.link(dve.tensor_tensor_scan(gb[:], chunk_start[:], sg[:, 1], 0.0, ALU.mult, ALU.add))
                    chunks = gb[:, 0:NP_TOK].rearrange("p (c s) -> p c s", s=64)
                    dve.tensor_tensor(sg[:, 0, 0:NP_TOK].rearrange("p (c s) -> p c s", s=64),
                                      chunks[:, :, 63:64].to_broadcast([P, 4, 64]), chunks, ALU.subtract)
                    dve.tensor_tensor(seqs(sg[:, 0, NP_TOK:T]), seqs(gb[:, NP_TOK:T])[:, :, 3:4].to_broadcast([P, NSEQ, TS]),
                                      seqs(gb[:, NP_TOK:T]), ALU.subtract).then_inc(b_ready, 1)
                    dve.wait_ge(e_ready, h + 1)
                    dve.tensor_tensor(gkl[:], k, sg[:, 0], ALU.mult).then_inc(kl_ready, 1)
                    dve.wait_ge(kl_ready, h + 1)
                    dve.tensor_tensor(k, k, prod[:], ALU.mult)
                    dve.scalar_tensor_tensor(q, q, float(P) ** -0.5, geb[:], ALU.mult, ALU.mult).then_inc(qk_ready, 1)
                    dve.wait_ge(kl_turned, h + 1)
                    dve.tensor_tensor(klm[:], ps[0:32, 7, 0:P].unsqueeze(1).to_broadcast([32, NSEQ, P]),
                                      seqmask[:].unsqueeze(2).to_broadcast([32, NSEQ, P]), ALU.mult).then_inc(tok_ready, 1)
                    dve.wait_ge(att_turned, h + 1)
                    for c in range(2):
                        rows = slice(64 * c, 64 * c + 64)
                        dve.copy_predicated(att[rows, :, rows], causal64[rows], ps[rows, 4, 0:P].rearrange("p (c s) -> p c s", s=64))
                    dve.copy_predicated(att_s[:], causal_s[:], ps[0:32, 4, P:P + 32]).then_inc(att_ready, 1)
                    dve.wait_ge(sadd_ready, h + 1)
                    if h:
                        dve.wait_ge(gstate_stored, 16 * h)
                    adds = [ps[:, c % 2, 256 * (c // 2):256 * (c // 2) + 256] for c in range(4)]
                    L.link(dve.tensor_copy(gs[:, 0, :], adds[0]))
                    for c in range(1, 4):
                        ins = dve.scalar_tensor_tensor(gs[:, c, :], gs[:, c - 1, :], geb[:, 64 * c + 63:64 * c + 64],
                                                       adds[c], ALU.mult, ALU.add)
                        if c < 3:
                            L.link(ins)
                    ins.then_inc(s_chain, 1)
                    dve.wait_ge(gsig_terms, h + 1)
                    dve.scalar_tensor_tensor(sg[:], z[:, 16 + 2 * h:18 + 2 * h, :], 0.0, sg[:], ALU.min, ALU.subtract) \
                        .then_inc(gsig_log, 1)
                    dve.wait_ge(gla_yy, h + 1)
                    for r in range(2):
                        dve.wait_ge(snew_ready, 2 * h + r + 1)
                        for s in range(4):
                            b = 4 * r + s
                            st = aring[:, h % 2, 256 * b:256 * (b + 1)]
                            ins = dve.scalar_tensor_tensor(st, st, geb[:, NP_TOK + TS * b + 3:NP_TOK + TS * b + 4],
                                                           ps[:, s // 2, 256 * (s % 2):256 * (s % 2) + 256], ALU.mult, ALU.add)
                        ins.then_inc(snew_used, 1)
                    dve.wait_ge(gsig_ready, h + 1)
                    for b in range(2):
                        gn = VEC["gla_g_norm"] + b
                        ins = dve.scalar_tensor_tensor(sg[:, b], z[:, 16 + 2 * h + b, :], vec[:, gn:gn + 1], sg[:, b],
                                                       ALU.mult, ALU.mult)
                    L.link(ins)
                    dve.wait_ge(gla_rs, h + 1)
                    m = L.mark(dve.tensor_tensor(sqb[:], ps[:, 2:4, 0:T], rstd[:].unsqueeze(1).to_broadcast([P, 2, T]), ALU.mult))
                    L.wait(m)
                    dve.tensor_tensor(sqb[:], sqb[:], sg[:], ALU.mult).then_inc(gla_y, 1)
                    dve.wait_ge(mixhi_done, CT + h + 1)
                    js = slice(CT + 2 * h, CT + 2 * h + 2)
                    dve.tensor_tensor(act_lo[:, js, :], sqb[:], act_hi[:, js, :].bitcast(F32), ALU.subtract) \
                        .then_inc(act_ready, 2)
                dve.wait_ge(gstate_stored, 16 * HEADS)

            def attend(rows, n, sink):
                L.link(dve.tensor_reduce(small[:, 0, 0:n], rows, AX.X, ALU.max))
                L.link(dve.tensor_tensor(small[:, 0, 0:n], small[:, 0, 0:n], sink, ALU.max))
                L.link(dve.tensor_scalar(small[:, 1, 0:n], small[:, 0, 0:n], -1.0, None, ALU.mult))
                dve.tensor_tensor(small[:, 2, 0:n], sink, small[:, 0, 0:n], ALU.subtract).then_inc(row_max, 1)

            def denominators(n):
                L.link(dve.tensor_tensor(small[:, 4, 0:n], small[:, 3, 0:n], small[:, 2, 0:n], ALU.add))
                L.link(dve.reciprocal(small[:, 5, 0:n], small[:, 4, 0:n]))

            def mix1():
                centre(2, zv[:], None, MEAN_BANK)
                dve.wait_ge(rstd_ready, 5)
                apply_stat(zv[:], None, rstd, ALU.mult).then_inc(normed, 1)
                for j in range(CT):
                    dve.wait_ge(mixed_ready, j + 1)
                    dve.tensor_tensor(zu[:, j, :], zu[:, j, :], ps[:, j % 2, 0:T], ALU.mult).then_inc(sgu_mixed, 1)
                dve.wait_ge(mixhi_done, CT + HEADS + 1)
                dve.tensor_tensor(act_lo[:, 0:CT, :], zu[:], act_hi[:, 0:CT, :].bitcast(F32), ALU.subtract).then_inc(act_ready, CT)
                dve.wait_ge(mix1_consts, 16 * 6)
                dve.wait_ge(sguv_stored, 16)
                dve.wait_ge(act_ready, 4 * KT + CT)
                dve.tensor_copy(qs[:], zq[:, :, NP_TOK:T].rearrange("p r (b t) -> p b r t", t=TS)).then_inc(qs_ready, 1)
                for blk in range(2):
                    k0 = 0 if blk else P
                    for h in range(16):
                        dve.wait_ge(scores_ready, 16 * blk + h + 1)
                        if blk:
                            dve.wait_ge(pt_turned, h + 1)
                        dve.scalar_tensor_tensor(sc[:, h, k0:256], dist[:, k0:256], SLOPES[h], ps[:, h % 4, k0:256],
                                                 ALU.mult, ALU.add).then_inc(scored, 1)
                    dve.wait_ge(scored, 16 * blk + 16)
                    attend(sc[:, :, k0:256], 16, sinks[:, 0:16])
                    dve.wait_ge(exps, 16 * blk + 16)
                    dve.wait_ge(sink_exp, blk + 1)
                    denominators(16)
                    for h in range(16):
                        dve.tensor_scalar(sc[:, h, k0:256], sc[:, h, k0:256], small[:, 5, h:h + 1], None, ALU.mult) \
                            .then_inc(probs_ready, 1)
                    dve.wait_ge(pv_done, 16 * blk + 16)
                    dve.wait_ge(qs_ready, 1)
                    dve.tensor_copy(zq[:, :, blk * P:(blk + 1) * P],
                                    ps[:, 2:4, :].rearrange("p a (r n) -> p (a r) n", n=P)).then_inc(yd_ready, 1)
                dve.wait_ge(scores_s_ready, 1)
                L.link(dve.tensor_tensor(sc[:, 0:4, 0:KEYS], ps[:, 0:4, 0:KEYS], bias_s[:], ALU.add))
                attend(sc[:, 0:4, 0:KEYS], 4, sinks[:, 16:20])
                dve.wait_ge(exps, 36)
                dve.wait_ge(sink_exp, 3)
                denominators(4)
                dve.tensor_tensor(sc[:, 0:4, 0:KEYS], sc[:, 0:4, 0:KEYS], small[:, 5, 0:4].unsqueeze(2).to_broadcast([P, 4, KEYS]),
                                  ALU.mult).then_inc(probs_s_ready, 1)
                dve.wait_ge(os_ready, 1)
                for s in range(NSEQ):
                    ins = dve.tensor_copy(zq[:, :, NP_TOK + TS * s:NP_TOK + TS * (s + 1)],
                                          ps[:, 0, 32 * s:32 * s + 32].rearrange("p (r t) -> p r t", t=TS))
                ins.then_inc(yd_ready, 1)
                dve.wait_ge(mixhi_done, CT + HEADS + 2)
                dve.tensor_tensor(act_lo[:, CT:KT, :], zq[:], act_hi[:, CT:KT, :].bitcast(F32), ALU.subtract).then_inc(act_ready, CT)
                dve.wait_ge(cache_stored, 16 * 6)

            cols = sg[:, 0, 0:KT * S9].rearrange("p (k s) -> p k s", s=S9)
            dve.wait_ge(cond_terms, 1)
            dve.scalar_tensor_tensor(cols, cond[:, :, 0:S9], 0.0, cols, ALU.min, ALU.subtract).then_inc(cond_log, 1)
            dve.wait_ge(cond_sig, 1)
            dve.tensor_tensor(cond[:, :, 0:S9], cond[:, :, 0:S9], cols, ALU.mult).then_inc(cond_ready, 1)
            dve.wait_ge(consts_landed, 48)
            ada_bias((None, 0))
            with dve.Fori(0, PRE - 1) as i:
                ada_bias((i, 1))
            split_lo(SEGS[0], 0, 0, 0)
            split_lo(SEGS[0], 0, 0, 1)
            norms = 0
            for seg in ["norm"] + PLAN:
                if seg == "norm":
                    dve.wait_ge(ada_biased, [PRE, 22, 48, 48, 48][norms])
                    norm(norms, final=norms == 4)
                    norms += 1
                    if norms == 1:
                        dve.wait_ge(history_landed, 16 * CT)
                        dve.wait_ge(history_zero, 1)
                elif seg == "mix0":
                    mix0()
                elif seg == "mix1":
                    mix1()
                else:
                    if seg.peel:
                        body(seg, None, 0)
                    turns = seg.bodies - 1 - seg.peel
                    if turns:
                        with dve.Fori(0, turns) as i:
                            L.enter(i, seg.dve_links)
                            body(seg, i, seg.peel)
                            L.leave(turns)
                    body(seg, None, seg.bodies - 1, last=True)



def tiles(w):
    k, n = w.shape
    return w.reshape(k // P, P, n // P, P).transpose(2, 1, 0, 3).reshape(n // P, P, k)


def paired(a, b):
    return np.concatenate([a, b], axis=2)


def columns(v):
    return v.reshape(-1, P).T


def kernel(**inputs):
    import concourse.bacc as bacc
    from concourse.bass_utils import run_bass_kernel_spmd

    a = {k: np.asarray(v) for k, v in inputs.items()}
    f = {}
    tokens = np.concatenate([a["x_prompt"][0], a["x_sample"].reshape(NSEQ * TS, D)])
    f["xT"] = tokens.T.reshape(KT, P, T).transpose(1, 0, 2)
    f["cT"] = np.concatenate([a["c_prompt"], a["c_sample"]]).T.reshape(KT, P, S9).transpose(1, 0, 2)
    conv_w = a["conv_w"].T.reshape(CT, P, TAPS).transpose(1, 0, 2).reshape(P, CT * TAPS)
    f["vec"] = np.concatenate([columns(a[n].reshape(-1)) for n in VEC if n != "conv_w"] + [conv_w], axis=1)
    f["w_ada"] = a["w_ada"].reshape(2, 4, 4, P, UNITS, ADA_N).transpose(0, 4, 1, 3, 2, 5).reshape(8 * UNITS, P, 4 * ADA_N)
    ab = tiles(a["w_in_ab"][:, :40 * P])
    f["w_ab"] = np.concatenate([paired(ab[0:8], ab[8:16]), paired(ab[16:20], ab[20:24]), paired(ab[24:40:2], ab[25:40:2])])
    f["w_zr"] = tiles(np.pad(a["w_in_ab"][:, 40 * P:], ((0, 0), (0, P - 16))))
    cd = a["w_in_cd"]
    q0, kv0 = 2 * CT * P, 3 * CT * P
    q = cd[:, q0:kv0].reshape(D, 2, CT, 64).transpose(0, 2, 1, 3).reshape(D, CT * P)
    u, v, q, kv = tiles(cd[:, 0:CT * P]), tiles(cd[:, CT * P:q0]), tiles(q), tiles(cd[:, kv0:])
    f["w_cd"] = np.concatenate([paired(kv[0:1], kv[1:2]), paired(q[0::2], q[1::2]), paired(u, v)])
    wo1 = a["w_out"][1]
    wo1 = np.concatenate([wo1[:CT * P], wo1[CT * P:].reshape(2, CT, 64, D).transpose(1, 0, 2, 3).reshape(CT * P, D)])
    wo = [tiles(a["w_out"][0]), tiles(wo1)]
    f["w_out"] = np.concatenate([paired(w[0::2], w[1::2]) for w in wo])
    f["w_gu"] = np.concatenate([paired(tiles(a["w_ffn_gate"][i]), tiles(a["w_ffn_up"][i])) for i in range(2)])
    f["w_dn"] = np.concatenate([tiles(half) for i in range(2) for half in np.split(a["w_ffn_down"][i], 2)])
    f["gla_w_gate"] = a["gla_w_gate"]
    f["state_convT"] = a["state_conv"].transpose(2, 0, 1).reshape(CT, P, NSEQ, HIST).transpose(1, 0, 2, 3)
    f["state_glaT"] = a["state_gla"].transpose(1, 2, 0, 3).reshape(HEADS, P, NSEQ * 256)
    f["cache_kT"] = a["cache_k"].transpose(2, 3, 0, 1).reshape(P, NSEQ, P)
    f["cache_vT"] = a["cache_v"].transpose(1, 0, 2, 3).reshape(P, NSEQ, P)
    f["sgu_wT"] = a["sgu_w"].transpose(2, 0, 1)
    f["sgu_wsT"] = np.tile(a["sgu_w"][:, :TS, :TS].transpose(2, 0, 1), (NSEQ, 1, NSEQ))
    f["sgu_bT"] = np.concatenate([a["sgu_b"], a["sgu_b"], np.tile(a["sgu_b"][:, :TS], (1, NSEQ))], axis=1)[None]
    sinks_p = np.broadcast_to(a["att_sinks"], (P, 16))
    sinks_s = np.tile(np.repeat(a["att_sinks"].reshape(2, 8), TS, axis=1).T, (4, 2))
    f["sinks"] = np.concatenate([sinks_p, sinks_s], axis=1)
    f["ident"] = np.eye(P)
    f["sel"] = np.tile(np.eye(32, S9), (4, 1))
    t_ = np.arange(T)
    f["chunk_start"] = np.broadcast_to(np.where(t_ < NP_TOK, t_ % 64 != 0, t_ % TS != 0), (P, T))
    s_, q_ = np.arange(64)[:, None], np.arange(64)[None]
    f["causal64"] = np.tile((s_ <= q_)[:, None], (2, 2, 1)).astype(np.uint32)
    i_, j_ = np.arange(32)[:, None], np.arange(32)[None]
    f["causal_s"] = ((i_ // TS == j_ // TS) & (i_ <= j_)).astype(np.uint32)
    f["seqmask"] = i_ // TS == np.arange(NSEQ)[None]
    d = np.arange(P)[:, None] - np.arange(256)[None] + P
    f["dist"] = np.where((d >= 0) & (d < P), -d, NEG)
    seq4, head, tok = np.arange(P) // 32, np.arange(P) // TS % 8, np.arange(P) % TS
    bias = np.full((P, 2, 2, KEYS), NEG)
    for pair in range(2):
        for g in range(2):
            slope = np.array(SLOPES)[g * 8 + head][:, None]
            dc = P + tok[:, None] - np.arange(P)[None]
            bias[:, pair, g, :P] = np.where(dc < P, -slope * dc, NEG)
            dn = tok[:, None] - j_ % TS
            own = (j_ // TS == (4 * pair + seq4)[:, None]) & (dn >= 0)
            bias[:, pair, g, P:] = np.where(own, -slope * dn, NEG)
    f["bias_s"] = bias.reshape(P, 4, KEYS)
    outs = {"y": (P, KT, T), "conv_p": (P, CT, HIST), "conv_s": (P, CT, NSEQ, HIST), "gla_p": (HEADS, P, 256),
            "gla_s": (HEADS, P, NSEQ * 256), "sgu_v": (P, CT, NSEQ * TS), "k_p": (P, P), "k_s_new": (P, NSEQ * TS),
            "k_s_old": (P, NSEQ, P - TS), "v_p": (P, P), "v_s_new": (NSEQ * TS, P), "v_s_old": (P - TS, NSEQ, P)}

    nc = bacc.Bacc("TRN2", target_bir_lowering=False, num_devices=1)
    arrays, t, o = {}, {}, {}
    for name, v in f.items():
        v = np.ascontiguousarray(v, dtype=v.dtype if v.dtype == np.uint32 else np.float32)
        arrays[f"in_{name}"] = v
        t[name] = nc.dram_tensor(f"in_{name}", v.shape, mybir.dt.from_np(v.dtype), kind="ExternalInput").ap()
    for name, shape in outs.items():
        o[name] = nc.dram_tensor(f"out_{name}", shape, F32, kind="ExternalOutput").ap()
    build(nc, t, o)
    res = run_bass_kernel_spmd(nc, [arrays], core_ids=[0]).results[0]
    r = {name: np.asarray(res[f"out_{name}"]) for name in outs}
    y = r["y"].transpose(2, 1, 0).reshape(T, D)
    k_s = np.concatenate([r["k_s_old"], r["k_s_new"].reshape(P, NSEQ, TS)], axis=2).transpose(1, 2, 0)
    v_s = np.concatenate([r["v_s_old"].transpose(1, 0, 2), r["v_s_new"].reshape(NSEQ, TS, P)], axis=1)
    return (y[:NP_TOK].reshape(1, NP_TOK, D), y[NP_TOK:].reshape(NSEQ, TS, D),
            r["conv_p"].transpose(2, 1, 0).reshape(1, HIST, CT * P),
            r["conv_s"].transpose(2, 3, 1, 0).reshape(NSEQ, HIST, CT * P),
            r["gla_p"].reshape(1, HEADS, P, 256),
            r["gla_s"].reshape(HEADS, P, NSEQ, 256).transpose(2, 0, 1, 3),
            r["sgu_v"].transpose(2, 1, 0).reshape(NSEQ, TS, CT * P),
            r["k_p"].T.reshape(1, P, 2, 64), k_s.reshape(NSEQ, P, 2, 64),
            r["v_p"].reshape(1, P, 2, 64), v_s.reshape(NSEQ, P, 2, 64))
```

```python
from contextlib import ExitStack

import concourse.bass as bass
from concourse import mybir
import numpy as np

F32 = mybir.dt.float32
F32R = mybir.dt.float32r
U32 = mybir.dt.uint32
ALU = mybir.AluOpType
ACT = mybir.ActivationFunctionType
AX = mybir.AxisListType

P = 128
D = 2048
KT = D // P
NP_TOK = 256
NSEQ, TS = 8, 4
T = NP_TOK + NSEQ * TS
S9 = 1 + NSEQ
TAPS, HIST = 31, 30
UW = HIST + NP_TOK
SW = HIST + TS
UE = UW + NSEQ * SW
CT = 8
FF_T = 44
BLK = FF_T // 2
HEADS = 4
SLOT = 2 * KT * P
ADA_N = 512
UNITS = 6 * D // ADA_N
PRE = 8
KEYS = P + NSEQ * TS
EPS = 1e-6
GELU_2C = 2.0 * (2.0 / np.pi) ** 0.5
GELU_K = GELU_2C * 0.044715
NEG = -1e30
SLOPES = [float(np.float32(2.0 ** (-8.0 * (h + 1) / 16))) for h in range(16)]

VEC = {}
_at = 0
for _name, _n in (("g_mix", 2 * KT), ("g_ffn", 2 * KT), ("g_final", KT), ("conv_b", CT), ("conv_ln_g", CT),
                  ("conv_ln_b", CT), ("gla_b_gate", HEADS), ("gla_g_norm", 2), ("sgu_ln_g", CT), ("sgu_ln_b", CT),
                  ("b_ada", 2 * 96), ("conv_w", CT * TAPS)):
    VEC[_name] = _at
    _at += _n
NVEC = _at


class Seg:

    def __init__(self, kind, layer, bodies, m, first, unit=None, group=0):
        self.kind, self.layer, self.bodies, self.m = kind, layer, bodies, m
        self.first = first
        self.unit = unit
        self.group = group
        self.steps = bodies * m
        self.ktiles = {"zr": 8, "down": BLK // 2}.get(kind, KT)
        self.two = kind not in ("zr", "down")
        self.width = 2 * self.ktiles * P
        self.act_links = {"gate": 4, "gu": 4, "sgu": 8}.get(kind, 0)
        self.dve_links = {"gate": 2 * TAPS - 1, "zconv": 2 * TAPS - 1, "gu": 2, "out": 4,
                          "down": 2 if group else 4}.get(kind, 0)


def plan():
    segs, norm = [], "norm"
    segs += [Seg("zr", 0, 1, 1, 0), Seg("gate", 0, 4, 2, 0, 8), Seg("zconv", 0, 4, 2, 8, 12, 0),
             Seg("z", 0, 2, 2, 16, 16, 16)]
    segs += ["mix0", Seg("out", 0, 4, 2, 0, 18), norm]
    for layer in range(2):
        if layer:
            segs += [Seg("kv", 1, 1, 1, 0), Seg("q", 1, 2, 2, 1), Seg("sgu", 1, 4, 2, 5), "mix1",
                     Seg("out", 1, 4, 2, 0), norm]
        segs += [Seg("gu", layer, 11, 2, 0, None if layer else 22),
                 Seg("down", layer, 8, 2, 0, None if layer else 33, 0)]
        if layer:
            segs += [Seg("gu", 1, 11, 2, 22)]
        else:
            segs += [Seg("gu", 0, 7, 2, 22, 41), Seg("gu", 0, 4, 2, 36)]
        segs += [Seg("down", layer, 8, 2, 16, None, 1), norm]
    return segs


PLAN = plan()
SEGS = [s for s in PLAN if isinstance(s, Seg)]
_n = _sig = _gel = _x = 0
_q = KT
for _s in SEGS:
    _s.n0, _s.sig0, _s.gel0, _s.q0, _s.x0 = _n, _sig, _gel, _q, _x
    _n += _s.steps
    if _s.kind in ("gate", "gu"):
        _sig += _s.steps
    if _s.kind == "sgu":
        _sig += 2 * _s.steps
        _gel += 2 * _s.steps
        _q += CT
    if _s.kind == "z":
        _q += CT
    if _s.kind == "out" or _s.kind == "down" and _s.group:
        _q += KT
        _x += KT
STEPS = _n
for _a, _b in zip(SEGS, SEGS[1:] + [None]):
    _a.next = _b
_kinds = set()
for _s in SEGS:
    _s.opens = _s.kind not in _kinds and _s.kind in ("gate", "out", "gu")
    _kinds.add(_s.kind)
    _s.peel = int(_s.bodies == 2 or _s.opens or _s.kind == "out")
for _a, _b in zip(PLAN, PLAN[1:]):
    if isinstance(_a, Seg):
        _a.mixed_next = _b in ("mix0", "mix1")
        _a.then_wait = not isinstance(_b, Seg) or "down" in (_a.kind, _b.kind)
SGU_SEG = next(s for s in SEGS if s.kind == "sgu")
Z_SEG = next(s for s in SEGS if s.kind == "z")
SQUARES = [0, 16, 24, 40, 56, 64, 80, 96]
NORM_STATS = [1, 3, 4, 6, 7]
GLA_A = 4 * 18


def lin(i, per, c):
    return c if i is None else i * per + c


class Links:

    def __init__(self, eng, sem):
        self.eng, self.sem, self.n, self.i, self.per = eng, sem, 0, None, 0

    def value(self, n):
        return n if self.i is None else self.i * self.per + n

    def mark(self, ins):
        ins.then_inc(self.sem, 1)
        self.n += 1
        return self.n

    def wait(self, n):
        self.eng.wait_ge(self.sem, self.value(n))

    def link(self, ins):
        self.wait(self.mark(ins))

    def enter(self, i, per):
        self.i, self.per, self.start = i, per, self.n

    def leave(self, turns):
        assert self.n - self.start == self.per, (self.n - self.start, self.per)
        self.n = self.start + turns * self.per
        self.i = None


def build(nc, t, o):
    ctx = ExitStack()
    with ctx:
        def sb(name, shape, dt=F32, stack=ctx):
            return stack.enter_context(nc.sbuf_tensor(name, shape, dt))

        sems = {}

        def sem(name):
            if name not in sems:
                sems[name] = ctx.enter_context(nc.semaphore(name))
            return sems[name]

        x = sb("x", [P, KT, T])
        with ExitStack() as a:
            act_hi = sb("act_hi", [P, KT, T], F32R, stack=a)
            act_lo = sb("act_lo", [P, KT, T], F32R, stack=a)
        with ExitStack() as a:
            free_hi = sb("free_hi", [P, KT * T], stack=a)
            free_lo = sb("free_lo", [P, KT * T], stack=a)
        sb("operand", [P, 2 * KT * T])
        raw = sb("raw", [P, 2, SLOT])
        w_hi = sb("w_hi", [P, 2, SLOT // 2], F32R)
        w_lo = sb("w_lo", [P, 2, SLOT // 2], F32R)
        aring = sb("aring", [P, 2, 4 * ADA_N])
        vec = sb("vec", [P, NVEC])
        mods = sb("mods", [P, 2 * 96, S9])
        cond = sb("cond", [P, KT, 32])
        adarow = sb("adarow", [P, ADA_N])
        ident = sb("ident", [P, P])
        ones = sb("ones", [P, P])
        sel = sb("sel", [P, S9])
        eps = sb("eps", [P, 1])
        one = sb("one", [P, 1])
        sg = sb("sg", [P, 2, T])
        prod = sb("prod", [P, T])
        sqb = sb("sqb", [P, 2, T])
        ssq = sb("ssq", [P, T])
        rstd = sb("rstd", [P, T])
        xtmp = sb("xtmp", [P, 2, NSEQ, TS])
        amod = sb("amod", [P, KT, S9])
        with ExitStack() as a:
            uext = sb("uext", [P, CT, UE], stack=a)
            z = sb("z", [P, 24, T], stack=a)
            zr = sb("zr", [16, T], stack=a)
            wgate = sb("wgate", [16, HEADS * P], stack=a)
            chunk_start = sb("chunk_start", [P, T], stack=a)
            causal64 = sb("causal64", [P, 2, 64], U32, stack=a)
            causal_s = sb("causal_s", [32, 32], U32, stack=a)
            seqmask = sb("seqmask", [32, NSEQ], stack=a)
            cacc = sb("cacc", [P, T], stack=a)
            own_rows = sb("own_rows", [P, 2, 32], stack=a)
        with ExitStack() as a:
            gs = sb("gs", [P, 4, 256], stack=a)
            vtok = sb("vtok", [P, 2, 256], stack=a)
            os_tok = sb("os_tok", [P, 2, 256], stack=a)
            vtok_s = sb("vtok_s", [32, 256], stack=a)
            kltok = sb("kltok", [P, 2, P], stack=a)
            klm = sb("klm", [32, NSEQ, P], stack=a)
            att = sb("att", [P, 2, P], stack=a)
            att_s = sb("att_s", [32, 32], stack=a)
        with ExitStack() as a:
            zu = sb("zu", [P, CT, T], stack=a)
            zv = sb("zv", [P, CT, T], stack=a)
            zq = sb("zq", [P, CT, T], stack=a)
            zkv = sb("zkv", [P, 2, T], stack=a)
            dist = sb("dist", [P, 256], stack=a)
            bias_s = sb("bias_s", [P, 4, KEYS], stack=a)
            sinks = sb("sinks", [P, 16 + 4], stack=a)
            vtok1 = sb("vtok1", [P, 2, P], stack=a)
            vnew = sb("vnew", [32, P], stack=a)
            small = sb("small", [P, 3, 6, 16], stack=a)
            qs = sb("qs", [P, NSEQ, CT, TS], stack=a)
            region1 = a.enter_context(ExitStack())
            wsp = sb("wsp", [P, 4, P], stack=region1)
            wsp_s = sb("wsp_s", [32, 4, 32], stack=region1)
            bsp = sb("bsp", [1, 4, T], stack=region1)
            vmix = sb("vmix", [P, 2, 256], stack=region1)
            vmix_s = sb("vmix_s", [32, 256], stack=region1)
            region1.close()
            kcache = sb("kcache", [P, NSEQ, P], stack=a)
            vcache = sb("vcache", [P, NSEQ, P], stack=a)
            ptp = sb("ptp", [P, 2, 512], stack=a)
        with ExitStack() as a:
            hid_hi = sb("hid_hi", [P, BLK, T], F32R, stack=a)
            hid_lo = sb("hid_lo", [P, BLK, T], F32R, stack=a)
        with ExitStack() as a:
            tn = sb("tn", [P, 2, 4, T], stack=a)
        sb("region", [P, 51968 // 4])
        ps = ctx.enter_context(nc.psum_tensor("ps", [P, 8, 512], F32))
        SNEW_BANKS = 0, 5
        MIX_BANKS = 4, 7
        ADA_BANK, SEL_BANK, MEAN_BANK, STAT_BANK, M_BANK = 4, 5, 5, 6, 7
        la = ps[:, 7, P:P + T]

        weights_landed = [sem("weights_landed0"), sem("weights_landed1")]
        ada_landed = [sem("ada_landed0"), sem("ada_landed1")]
        cond_w_landed = [sem(f"cond_w_landed{s}") for s in range(4)]
        y_stored = [sem("y_stored0"), sem("y_stored1")]
        (act_links, act_ready, ada_biased, ada_cols, ada_rows, ada_used, att_ready, att_turned, b_ready,
         cache_stored, centred, cond_landed, cond_log, cond_ready, cond_sig, cond_terms, consts_landed,
         conv_affined, conv_log, conv_ready, conv_sig, conv_stored, conv_terms, conv_y, drained, dve_links,
         e_ready, exps, gelu_arg, gelu_sq, gla_rs, gla_y, gla_yy, gsig_log, gsig_ready, gsig_terms,
         gstate_stored, half_done, hi_done, hid_hi_done, hid_ready, history_landed, history_zero, kl_ready,
         kl_turned, kv_landed, la_ready, la_terms, mean_ready, mean_used, mix0_consts, mix1_consts,
         mixed_ready, mixhi_done, ms_ready, nhi_done, normed, ones_set, os_copied, os_ready, os_turned,
         osq_ready, pool_links, probs_ready, probs_s_ready, pt_ready, pt_turned, pts_ready, pts_turned,
         pv_done, qk_ready, qs_ready, row_max, rstd_ready, s_chain, sadd_ready, scored, scores_ready,
         scores_s_ready, sgu_mixed, sguv_stored, sig_log, sig_ready, sig_terms, sink_exp, snew_ready,
         snew_used, split_done, sq_added, sq_ready, stat_ready, state_stored, tn_ready, tn_samples,
         tok_ready, v_ln, v_turned, vmix_ready, vmix_turned, vtok1_ready, vtok1_turned, wsp_ready, x_landed,
         x_updated, y_ready, yd_ready) = (
            sem(name) for name in (
                "act_links", "act_ready", "ada_biased", "ada_cols", "ada_rows", "ada_used", "att_ready",
                "att_turned", "b_ready", "cache_stored", "centred", "cond_landed", "cond_log", "cond_ready",
                "cond_sig", "cond_terms", "consts_landed", "conv_affined", "conv_log", "conv_ready", "conv_sig",
                "conv_stored", "conv_terms", "conv_y", "drained", "dve_links", "e_ready", "exps", "gelu_arg",
                "gelu_sq", "gla_rs", "gla_y", "gla_yy", "gsig_log", "gsig_ready", "gsig_terms", "gstate_stored",
                "half_done", "hi_done", "hid_hi_done", "hid_ready", "history_landed", "history_zero", "kl_ready",
                "kl_turned", "kv_landed", "la_ready", "la_terms", "mean_ready", "mean_used", "mix0_consts",
                "mix1_consts", "mixed_ready", "mixhi_done", "ms_ready", "nhi_done", "normed", "ones_set",
                "os_copied", "os_ready", "os_turned", "osq_ready", "pool_links", "probs_ready", "probs_s_ready",
                "pt_ready", "pt_turned", "pts_ready", "pts_turned", "pv_done", "qk_ready", "qs_ready", "row_max",
                "rstd_ready", "s_chain", "sadd_ready", "scored", "scores_ready", "scores_s_ready", "sgu_mixed",
                "sguv_stored", "sig_log", "sig_ready", "sig_terms", "sink_exp", "snew_ready", "snew_used",
                "split_done", "sq_added", "sq_ready", "stat_ready", "state_stored", "tn_ready", "tn_samples",
                "tok_ready", "v_ln", "v_turned", "vmix_ready", "vmix_turned", "vtok1_ready", "vtok1_turned",
                "wsp_ready", "x_landed", "x_updated", "y_ready", "yd_ready"))
        src = {"zr": t["w_zr"], "gate": t["w_ab"], "zconv": t["w_ab"], "z": t["w_ab"], "kv": t["w_cd"],
               "q": t["w_cd"], "sgu": t["w_cd"], "out": t["w_out"], "gu": t["w_gu"], "down": t["w_dn"]}
        LAYER_STEPS = {"out": KT // 2, "gu": FF_T, "down": 2 * KT}

        def flat(ap):
            return ap.rearrange("p a n -> p (a n)")

        def at(buf, j, lo=0, hi=None):
            hi = buf.shape[-1] if hi is None else hi
            return flat(buf[:, bass.ds(j, 1), lo:hi])

        def seqs(ap):
            return ap.rearrange("p (b t) -> p b t", t=TS)

        def flat_at(buf, j):
            return buf[:, bass.ds(j, 1)]

        def rows_s(j):
            return at(uext, j, UW, UE).rearrange("p (b w) -> p b w", w=SW)

        def taps_s(j, k):
            return rows_s(j)[:, :, k:k + TS]

        y_all = uext[:, :, 0:NP_TOK]
        y_all_s = uext[:, :, UW:UE].rearrange("p c (b w) -> p c b w", w=SW)[:, :, :, 0:TS]

        def unit_uses(u):
            return lin(u[0], 4, 4 * (u[1] - PRE) + (HEADS if u[1] >= 18 else 0))

        def first_unit(u):
            return u[0] is None and u[1] == 0

        def unit_no(u):
            return lin(u[0], 1, u[1])

        def steps_of(seg, i, base):
            for j in range(seg.m):
                k = seg.m * base + j
                yield lin(i, seg.m, seg.n0 + k), (seg.n0 + k) % 2, lin(i, seg.m, k)

        sc = [b[:, 0:16 * 256].rearrange("p (h n) -> p h n", n=256) for b in (free_hi, free_lo)]
        sc_s = free_hi[:, CT * T:CT * T + 4 * KEYS].rearrange("p (c n) -> p c n", n=KEYS)

        geb_of = [free_lo[:, j * T:(j + 1) * T] for j in (KT - 4, KT - 2)]
        gkl_of = [free_lo[:, j * T:(j + 1) * T] for j in (KT - 3, KT - 1)]
        gb, la_terms_of, la_sum = (free_hi[:, j * T:(j + 1) * T] for j in (KT - 4, KT - 2, KT - 1))

        def pre_slot(s):
            return raw[:, s // 2, (s % 2) * 4 * ADA_N:(s % 2 + 1) * 4 * ADA_N]

        block = ctx.enter_context(nc.Block())

        @block.sync
        def _(sp):
            def load_step(seg, n, par, ls):
                if not (isinstance(n, int) and n < 2):
                    sp.wait_ge(split_done, n * 2 - 2)
                rows = src[seg.kind][bass.ds(ls + (seg.first + seg.layer * LAYER_STEPS.get(seg.kind, 0)), 1)]
                sp.dma_start(raw[:, par, 0:seg.width], rows.rearrange("a p n -> p (a n)")) \
                    .then_inc(weights_landed[par], 16)

            def load_ada(u, s):
                if not (u[0] is None and u[1] == PRE and s < 2):
                    sp.wait_ge(ada_used, unit_no(u) * 4 + (s - 1))
                rows = t["w_ada"][bass.ds(unit_no(u) * 4 + s, 1)]
                sp.dma_start(aring[:, s % 2, :], rows.rearrange("a p n -> p (a n)")) \
                    .then_inc(ada_landed[s % 2], 16)

            def load_pre(u, s):
                if not first_unit(u):
                    sp.wait_ge(ada_used, unit_no(u) * 4 + (s - 3))
                rows = t["w_ada"][bass.ds(unit_no(u) * 4 + s, 1)]
                sp.dma_start(pre_slot(s), rows.rearrange("a p n -> p (a n)")).then_inc(cond_w_landed[s], 16)

            def body(seg, i, base, last=False):
                for j, (n, par, ls) in enumerate(steps_of(seg, i, base)):
                    if seg.kind == "zr":
                        sp.wait_ge(ada_used, 4 * PRE)
                    if j == 0 and base == 0 and i is None and seg.kind == "out":
                        pass
                    elif not (last and j == seg.m - 1):
                        load_step(seg, n + 1, 1 - par, ls + 1)
                    elif seg.next:
                        load_step(seg.next, n + 1, 1 - par, 0)
                    if seg.unit is not None:
                        load_ada((i, seg.unit + base), 2 * j)
                        load_ada((i, seg.unit + base), 2 * j + 1)

            def mix0():
                sp.wait_ge(conv_ready, CT)
                sp.dma_start(o["conv_p"], uext[:, :, NP_TOK:UW]).then_inc(conv_stored, 16)
                for j in range(CT):
                    sp.dma_start(o["conv_s"][:, j], rows_s(j)[:, :, TS:SW]).then_inc(conv_stored, 16)
                for h in range(HEADS):
                    if h < 2:
                        sp.wait_ge(ada_used, GLA_A + h - 1)
                    else:
                        sp.wait_ge(state_stored, 16 * (h - 1))
                    sp.dma_start(aring[:, h % 2, :], t["state_glaT"][h]).then_inc(ada_landed[h % 2], 16)
                    if h >= 1:
                        store_states(h - 1)
                store_states(HEADS - 1)
                sp.wait_ge(state_stored, 16 * HEADS)

            def store_states(h):
                sp.wait_ge(s_chain, h + 1)
                sp.dma_start(o["gla_p"][h], gs[:, 3, :]).then_inc(gstate_stored, 16)
                sp.wait_ge(snew_used, 2 * h + 2)
                sp.dma_start(o["gla_s"][h], aring[:, h % 2, :]).then_inc(state_stored, 16)

            def mix1():
                sp.wait_ge(sgu_mixed, CT)
                sp.dma_start(kcache[:], t["cache_kT"]).then_inc(kv_landed, 16)
                sp.dma_start(vcache[:], t["cache_vT"]).then_inc(kv_landed, 16)
                sp.dma_start(o["sgu_v"], zv[:, :, NP_TOK:T]).then_inc(sguv_stored, 16)
                sp.dma_start(o["k_p"], zkv[:, 0, P:NP_TOK]).then_inc(cache_stored, 16)
                sp.dma_start(o["k_s_new"], zkv[:, 0, NP_TOK:T]).then_inc(cache_stored, 16)
                sp.wait_ge(vtok1_ready, 1)
                sp.dma_start(o["v_p"], vtok1[:, 1, :]).then_inc(cache_stored, 16)
                sp.dma_start(o["v_s_new"], vnew[:]).then_inc(cache_stored, 16)
                sp.wait_ge(kv_landed, 32)
                sp.dma_start(o["k_s_old"], kcache[:, :, TS:P]).then_inc(cache_stored, 16)
                sp.dma_start(o["v_s_old"], vcache[TS:P]).then_inc(cache_stored, 16)

            sp.dma_start(cond[:, :, 0:S9], t["cT"]).then_inc(cond_landed, 16)
            sp.dma_start(sel[:], t["sel"]).then_inc(consts_landed, 16)
            sp.dma_start(vec[:], t["vec"]).then_inc(consts_landed, 16)
            sp.dma_start(ident[:], t["ident"]).then_inc(consts_landed, 16)
            for s in range(4):
                load_pre((None, 0), s)
            sp.dma_start(x[:], t["xT"]).then_inc(x_landed, 16)
            with sp.Fori(0, PRE - 1) as i:
                for s in range(4):
                    load_pre((i, 1), s)
            sp.wait_ge(ada_used, 4 * PRE - 3)
            load_step(SEGS[0], 0, 0, 0)
            for seg, after in zip(PLAN, PLAN[1:] + [None]):
                if seg in ("mix0", "mix1"):
                    load_step(after, after.n0 + 1, (after.n0 + 1) % 2, 1)
                if seg == "mix0":
                    mix0()
                elif seg == "mix1":
                    mix1()
                elif seg != "norm":
                    if seg.kind == "gate":
                        sp.wait_ge(act_ready, KT)
                        for name, place in (("gla_w_gate", wgate), ("chunk_start", chunk_start), ("causal64", causal64),
                                            ("causal_s", causal_s), ("seqmask", seqmask), ("own_rows", own_rows)):
                            sp.dma_start(place[:], t[name]).then_inc(mix0_consts, 16)
                        for j in range(CT):
                            sp.dma_start(rows_s(j)[:, :, 0:HIST], t["state_convT"][:, j]).then_inc(history_landed, 16)
                    if seg.kind == "q":
                        sp.wait_ge(act_ready, 4 * KT)
                        for name, place in (("dist", dist), ("bias_s", bias_s), ("sinks", sinks), ("sgu_wT", wsp),
                                            ("sgu_wsT", wsp_s), ("sgu_bT", bsp)):
                            sp.dma_start(place[:], t[name]).then_inc(mix1_consts, 16)
                    if seg.peel:
                        body(seg, None, 0)
                    turns = seg.bodies - 1 - seg.peel
                    if turns:
                        with sp.Fori(0, turns) as i:
                            body(seg, i, seg.peel)
                    body(seg, None, seg.bodies - 1, last=True)
            for g in range(4):
                sp.wait_ge(y_ready, g + 1)
                sp.dma_start(o["y"][:, 4 * g:4 * g + 4, :], tn[:, g % 2]).then_inc(y_stored[g % 2], 16)
            for stored in y_stored:
                sp.wait_ge(stored, 32)
            sp.wait_ge(conv_stored, 16 * (CT + 1))
            sp.wait_ge(gstate_stored, 16 * HEADS)
            sp.wait_ge(cache_stored, 16 * 6)
            sp.wait_ge(sguv_stored, 16)

        @block.gpsimd
        def _(pool):
            L = Links(pool, pool_links)
            pool.memset(ones[:], 1.0).then_inc(ones_set, 1)
            pool.memset(eps[:], EPS).then_inc(ones_set, 1)
            pool.memset(one[:], 1.0).then_inc(ones_set, 1)
            pool.memset(cond[:, :, S9:32], 0.0).then_inc(ones_set, 1)

            def sum_squares(n, q):
                for k in range(n):
                    pool.wait_ge(sq_ready, q + k + 1)
                    if k == 0:
                        if q:
                            pool.wait_ge(stat_ready, SQUARES.index(q))
                        pool.tensor_copy(ssq[:], sqb[:, (q + k) % 2]).then_inc(sq_added, 1)
                    else:
                        pool.wait_ge(sq_added, q + k)
                        pool.tensor_tensor(ssq[:], ssq[:], sqb[:, (q + k) % 2], ALU.add).then_inc(sq_added, 1)

            sum_squares(KT, 0)
            pool.wait_ge(act_ready, KT)
            pool.memset(uext[:, :, 0:HIST], 0.0).then_inc(history_zero, 1)
            sum_squares(CT, 16)
            sum_squares(KT, 24)
            sum_squares(KT, 40)
            pool.wait_ge(mix1_consts, 16 * 6)
            pool.affine_select(out=wsp[:], in_=wsp[:], pattern=[[0, 4], [1, P]], compare_op=ALU.is_ge, fill=0.0,
                               base=0, channel_multiplier=-1).then_inc(wsp_ready, 1)
            L.link(pool.affine_select(out=wsp_s[:], in_=wsp_s[:], pattern=[[0, 4], [1, 32]], compare_op=ALU.is_ge,
                                      fill=0.0, base=0, channel_multiplier=-1))
            pool.affine_select(out=wsp_s[:], in_=wsp_s[:], pattern=[[0, 4], [-TS, NSEQ], [0, TS]],
                               compare_op=ALU.is_ge, fill=0.0, base=0, channel_multiplier=1).then_inc(wsp_ready, 1)
            sum_squares(CT, 56)
            sum_squares(KT, 64)
            sum_squares(KT, 80)

        @block.tensor
        def _(pe):
            sets = [0]
            stats = [0]

            def half(seg, n, par, h, first, hidden=None):
                if h == 0 and not (isinstance(n, int) and n < 2):
                    pe.wait_ge(drained, n - 1)
                pe.wait_ge(split_done, n * 2 + (h + 1))
                hi, lo = (hid_hi, hid_lo) if seg.kind == "down" else (act_hi, act_lo)
                bank = ps[:, 2 * par + (h if seg.two else 0), 0:T]
                for k in range(seg.ktiles):
                    kt = k if seg.two else h * seg.ktiles + k
                    if first and kt % 4 == 0 and (h == 0 or not seg.two):
                        pe.wait_ge(act_ready, sets[0] * KT + kt + 4)
                    if hidden is not None:
                        pe.wait_ge(hid_ready, hidden + kt + 1)
                    cols = slice(k * P, (k + 1) * P)
                    begin = k == 0 and (seg.two or h == 0)
                    end = k == seg.ktiles - 1 and (seg.two or h == 1)
                    pe.matmul(bank, w_hi[:, h, cols], hi[:, kt, :], start=begin, stop=False)
                    pe.matmul(bank, w_lo[:, h, cols], hi[:, kt, :], start=False, stop=False)
                    mm = pe.matmul(bank, w_hi[:, h, cols], lo[:, kt, :], start=False, stop=end)
                mm.then_inc(half_done, 1)

            def ada_slot(u, s, pre=False):
                if pre:
                    slot = pre_slot(s)
                    pe.wait_ge(cond_w_landed[s], unit_no(u) * 16 + 16)
                else:
                    slot = aring[:, s % 2, :]
                    pe.wait_ge(ada_landed[s % 2], (unit_uses(u) + (s - s % 2)) * 8 + 16)
                if s == 0 and not first_unit(u):
                    pe.wait_ge(ada_rows, unit_no(u))
                for j in range(4):
                    mm = pe.matmul(ps[32 * j:32 * j + 32, ADA_BANK, :], cond[:, 4 * s + j, :],
                                   slot[:, j * ADA_N:(j + 1) * ADA_N], start=(s == 0), stop=(s == 3))
                mm.then_inc(ada_used, 1)

            def ada_turn(u):
                pe.wait_ge(ada_rows, unit_no(u) + 1)
                if not first_unit(u):
                    pe.wait_ge(ada_biased, unit_no(u))
                for q in range(4):
                    mm = pe.matmul(ps[:, SEL_BANK, 16 * q:16 * q + S9], adarow[:, q * P:(q + 1) * P], sel[:],
                                   start=True, stop=True)
                mm.then_inc(ada_cols, 1)

            def stat():
                k = stats[0]
                pe.wait_ge(sq_added, SQUARES[k + 1])
                if k:
                    pe.wait_ge(rstd_ready, k)
                pe.matmul(ps[:, STAT_BANK, 0:T], ones[:], ssq[:], start=True, stop=True).then_inc(stat_ready, 1)
                stats[0] += 1

            def conv_mean():
                pe.wait_ge(conv_ready, CT)
                for j in range(CT):
                    pe.matmul(ps[:, M_BANK, 0:NP_TOK], ones[:], y_all[:, j], start=(j == 0), stop=(j == CT - 1))
                for j in range(CT):
                    mm = pe.matmul(ps[:, M_BANK, NP_TOK:T], ones[:], y_all_s[:, j], start=(j == 0), stop=(j == CT - 1))
                mm.then_inc(mean_ready, 1)

            def body(seg, i, base, first=False, hidden=None):
                for j, (n, par, ls) in enumerate(steps_of(seg, i, base)):
                    u = None if seg.unit is None else (i, seg.unit + base)
                    half(seg, n, par, 0, first and j == 0, hidden if j == 0 else None)
                    if seg.kind == "z" and ls == 2:
                        stat()
                    if u and j == 0:
                        ada_slot(u, 0)
                    if u and j == 1:
                        ada_slot(u, 2)
                        ada_slot(u, 3)
                    half(seg, n, par, 1, first and j == 0, hidden if j == 0 else None)
                    if seg.kind == "z" and ls == 0:
                        conv_mean()
                    if u and j == 0:
                        ada_slot(u, 1)
                    if u and j == 1:
                        ada_turn(u)

            def mix0():

                def gate(h):
                    pe.matmul(la, wgate[:, h * P:(h + 1) * P], zr[:], start=True, stop=True).then_inc(la_ready, 1)

                pe.wait_ge(mix0_consts, 16 * 6)
                pe.wait_ge(mean_used, 1)
                gate(0)
                pe.wait_ge(drained, Z_SEG.n0 + Z_SEG.steps)
                pe.wait_ge(rstd_ready, 2)
                for h in range(HEADS):
                    if h:
                        pe.wait_ge(tok_ready, 3 * h)
                        pe.wait_ge(snew_used, 2 * h)
                        pe.wait_ge(att_ready, h)
                    else:
                        pe.wait_ge(ada_biased, 18)
                    v, gkl_h = [z[:, 8 + 2 * h + b, :] for b in range(2)], gkl_of[h % 2]
                    for b in range(2):
                        for c in range(2):
                            pe.transpose(ps[:, 5, (2 * c + b) * P:(2 * c + b + 1) * P], v[b][:, c * P:(c + 1) * P], ident[:])
                        mm = pe.transpose(ps[0:32, 6, 256 + b * P:256 + (b + 1) * P], v[b][:, NP_TOK:T], ident[:])
                    mm.then_inc(v_turned, 1)
                    pe.wait_ge(kl_ready, h + 1)
                    pe.wait_ge(tok_ready, 3 * h + 1)
                    for c in range(2):
                        pe.transpose(ps[:, 6, c * P:(c + 1) * P], gkl_h[:, c * P:(c + 1) * P], ident[:])
                    pe.transpose(ps[0:32, 7, 0:P], gkl_h[:, NP_TOK:T], ident[:]).then_inc(kl_turned, 1)
                    pe.wait_ge(qk_ready, h + 1)
                    q, k = z[:, 2 * h, :], z[:, 2 * h + 1, :]
                    if h:
                        pe.wait_ge(gla_rs, h)
                    for c in range(4):
                        cs = slice(64 * c, 64 * c + 64)
                        pe.matmul(ps[64 * (c % 2):64 * (c % 2) + 64, 4, 64 * (c // 2):64 * (c // 2) + 64],
                                  k[:, cs], q[:, cs], start=True, stop=True)
                    pe.matmul(ps[0:32, 4, P:P + 32], k[:, NP_TOK:T], q[:, NP_TOK:T], start=True, stop=True) \
                        .then_inc(att_turned, 1)
                    pe.wait_ge(ada_landed[h % 2], 16 * ((GLA_A - 4 * PRE + h) // 2 + 1))
                    for s in range(NSEQ):
                        j, r = s % 4, s // 4
                        mm = pe.matmul(ps[32 * j:32 * j + 32, 5, 256 * r:256 * r + 256], q[:, NP_TOK:T],
                                       aring[:, h % 2, 256 * s:256 * (s + 1)], start=True, stop=True)
                    mm.then_inc(os_turned, 1)
                    pe.wait_ge(tok_ready, 3 * h + 3)
                    if h:
                        pe.wait_ge(snew_used, 2 * h)
                    for c in range(4):
                        rows = slice(64 * (c % 2), 64 * (c % 2) + 64)
                        mm = pe.matmul(ps[:, c % 2, 256 * (c // 2):256 * (c // 2) + 256], kltok[rows, c // 2, :],
                                       vtok[rows, c // 2, :], start=True, stop=True)
                    mm.then_inc(sadd_ready, 1)
                    if h < HEADS - 1:
                        gate(h + 1)
                    pe.wait_ge(att_ready, h + 1)
                    pe.wait_ge(s_chain, h + 1)
                    pe.wait_ge(os_copied, h + 1)
                    if h:
                        pe.wait_ge(gla_y, h)
                    for b in range(2):
                        vs = slice(b * P, (b + 1) * P)
                        for c in range(4):
                            if c % 2 == 0:
                                pe.matmul(ps[:, 2 + b, 64 * c:64 * c + P], vtok[:, c // 2, vs], att[:, c // 2, :],
                                          start=True, stop=False, skip_group_check=True)
                            if c:
                                pe.matmul(ps[:, 2 + b, 64 * c:64 * c + 64], gs[:, c - 1, vs], q[:, 64 * c:64 * c + 64],
                                          start=False, stop=True, skip_group_check=True)
                        pe.matmul(ps[:, 2 + b, NP_TOK:T], vtok_s[:, vs], att_s[:], start=True, stop=False)
                        for r in range(2):
                            mm = pe.matmul(ps[:, 2 + b, NP_TOK:T], os_tok[:, r, vs], own_rows[:, r, :], start=False,
                                           stop=(r == 1))
                    mm.then_inc(gla_yy, 1)
                    for r in range(2):
                        for s in range(4):
                            mm = pe.matmul(ps[:, SNEW_BANKS[r] + s // 2, 256 * (s % 2):256 * (s % 2) + 256], klm[:, 4 * r + s, :],
                                           vtok_s[:], start=True, stop=True)
                        mm.then_inc(snew_ready, 1)
                        if r:
                            pe.wait_ge(osq_ready, h + 1)
                    for b in range(2):
                        mm = pe.matmul(ps[:, 4, 0:T], ones[:], sqb[:, b], start=(b == 0), stop=(b == 1))
                    mm.then_inc(ms_ready, 1)
                pe.wait_ge(snew_used, 2 * HEADS)
                pe.wait_ge(gla_y, HEADS)
                pe.wait_ge(gla_rs, HEADS)

            def attention_scores(blk, first, last):
                k0 = 0 if blk else P
                for h in range(first, last):
                    gp = slice(64 * (h // 8), 64 * (h // 8) + 64)
                    if 16 * blk + h >= 4:
                        pe.wait_ge(scored, 16 * blk + h - 3)
                    pe.matmul(ps[:, h % 4, k0:256], zq[gp, h % 8, blk * P:(blk + 1) * P],
                              zkv[gp, 0, blk * P - P + k0:(blk + 1) * P], start=True, stop=True).then_inc(scores_ready, 1)

            def attention_values(blk):
                for h in range(17):
                    turn = 16 * blk + h
                    if h < 16:
                        pe.wait_ge(probs_ready, turn + 1)
                        if turn >= 2:
                            pe.wait_ge(pt_ready, turn - 1)
                        for kb in range(1 - blk, 2):
                            mm = pe.transpose(ps[:, 6 + turn % 2, kb * P:(kb + 1) * P], sc[blk][:, h, kb * P:(kb + 1) * P], ident[:])
                        mm.then_inc(pt_turned, 1)
                    if h:
                        g, r = (h - 1) // 8, (h - 1) % 8
                        pe.wait_ge(pt_ready, turn)
                        if h == 1:
                            pe.wait_ge(scored, 32)
                        for kb in range(1 - blk, 2):
                            mm = pe.matmul(ps[64 * g:64 * g + 64, 2 + r // 4, (r % 4) * P:(r % 4 + 1) * P],
                                           vtok1[:, blk - 1 + kb, 64 * g:64 * g + 64], ptp[:, (turn - 1) % 2, kb * P:(kb + 1) * P],
                                           start=(kb == 1 - blk), stop=(kb == 1))
                        mm.then_inc(pv_done, 1)

            def mix1():
                pe.wait_ge(drained, SGU_SEG.n0 + SGU_SEG.steps)
                for j in range(CT):
                    mm = pe.matmul(ps[:, MEAN_BANK, 0:T], ones[:], zv[:, j, :], start=(j == 0), stop=(j == CT - 1))
                mm.then_inc(mean_ready, 1)
                attention_scores(0, 0, 16)
                attention_scores(1, 0, 4)
                stat()
                attention_scores(1, 4, 16)
                pe.wait_ge(mix1_consts, 16 * 6)
                pe.wait_ge(wsp_ready, 2)
                pe.wait_ge(mean_used, 2)
                pe.wait_ge(rstd_ready, stats[0])
                for g in range(4):
                    pe.wait_ge(v_ln, 2 * g + 2)
                    if g:
                        pe.wait_ge(vmix_ready, g)
                    for b in range(2):
                        for c in range(2):
                            pe.transpose(ps[:, 5, (2 * c + b) * P:(2 * c + b + 1) * P], zv[:, 2 * g + b, c * P:(c + 1) * P], ident[:])
                        mm = pe.transpose(ps[0:32, 6, b * P:(b + 1) * P], zv[:, 2 * g + b, NP_TOK:T], ident[:])
                    mm.then_inc(vmix_turned, 1)
                    pe.wait_ge(vmix_ready, g + 1)
                    for b in range(2):
                        if g:
                            pe.wait_ge(sgu_mixed, 2 * g + b - 1)
                        bank = ps[:, MIX_BANKS[b], 0:T]
                        vs = slice(b * P, (b + 1) * P)
                        pe.matmul(bank, ones[0:1, :], bsp[0:1, g, :], start=True, stop=False)
                        for c in range(2):
                            pe.matmul(bank[:, c * P:(c + 1) * P], vmix[:, c, vs], wsp[:, g, :], start=False, stop=False)
                        pe.matmul(bank[:, NP_TOK:T], vmix_s[:, vs], wsp_s[:, g, :], start=False, stop=True) \
                            .then_inc(mixed_ready, 1)
                pe.wait_ge(vmix_ready, 4)
                for c in range(2):
                    pe.transpose(ps[:, 5, c * P:(c + 1) * P], zkv[:, 1, c * P:(c + 1) * P], ident[:])
                pe.transpose(ps[0:32, 5, 256:384], zkv[:, 1, NP_TOK:T], ident[:]).then_inc(vtok1_turned, 1)
                pe.wait_ge(vtok1_ready, 1)
                pe.wait_ge(sgu_mixed, CT)
                attention_values(0)
                pe.wait_ge(kv_landed, 32)
                pe.wait_ge(qs_ready, 1)
                for s in range(NSEQ):
                    for g in range(2):
                        gp = slice(64 * g, 64 * g + 64)
                        out = ps[32 * (s % 4):32 * (s % 4) + 32, g, 256 * (s // 4):256 * (s // 4) + KEYS]
                        rows = qs[gp, s].rearrange("p r t -> p (r t)")
                        pe.matmul(out[:, 0:P], rows, kcache[gp, s, :], start=True, stop=True)
                        mm = pe.matmul(out[:, P:KEYS], rows, zkv[gp, 0, NP_TOK:T], start=True, stop=True)
                mm.then_inc(scores_s_ready, 1)
                pe.wait_ge(yd_ready, 1)
                attention_values(1)
                pe.wait_ge(probs_s_ready, 1)
                for c in range(4):
                    pe.transpose(ps[:, 4, c * P:(c + 1) * P], sc_s[:, c, 0:P], ident[:])
                for c in range(4):
                    mm = pe.transpose(ps[0:32, 5, c * P:(c + 1) * P], sc_s[:, c, P:KEYS], ident[:])
                mm.then_inc(pts_turned, 1)
                pe.wait_ge(pts_ready, 1)
                for s in range(NSEQ):
                    for g in range(2):
                        c = 2 * (s // 4) + g
                        out = ps[64 * g:64 * g + 64, 0, 32 * s:32 * s + 32]
                        cols = slice(c * P + 32 * (s % 4), c * P + 32 * (s % 4) + 32)
                        pe.matmul(out, vcache[:, s, 64 * g:64 * g + 64], ptp[:, 0, cols], start=True, stop=False)
                        mm = pe.matmul(out, vnew[:, 64 * g:64 * g + 64], ptp[0:32, 1, cols], start=False, stop=True)
                mm.then_inc(os_ready, 1)
                pe.wait_ge(act_ready, KT * (sets[0] + 1))

            pe.wait_ge(consts_landed, 48)
            pe.wait_ge(cond_ready, 1)
            pe.wait_ge(ones_set, 4)
            for s in range(4):
                ada_slot((None, 0), s, pre=True)
            ada_turn((None, 0))
            with pe.Fori(0, PRE - 1) as i:
                for s in range(4):
                    ada_slot((i, 1), s, pre=True)
                ada_turn((i, 1))
            stat()
            fresh, blocks = True, 0
            for seg in PLAN:
                if seg in ("norm", "mix0", "mix1"):
                    {"norm": stat, "mix0": mix0, "mix1": mix1}[seg]()
                    fresh = True
                    continue
                if seg.kind == "down":
                    blocks += 1
                start = 0
                if (seg.opens or seg.bodies == 2) and not fresh:
                    body(seg, None, 0)
                    start = 1
                if seg.kind == "down":
                    body(seg, None, 0, hidden=BLK * (blocks - 1))
                    start = 1
                if fresh and seg.kind != "down":
                    body(seg, None, 0, first=True)
                    start = 1
                    sets[0] += 1
                    fresh = False
                if seg.bodies > start:
                    if seg.bodies - start > 1:
                        with pe.Fori(0, seg.bodies - start) as i:
                            body(seg, i, start)
                    else:
                        body(seg, None, start)

        @block.scalar
        def _(act):
            L = Links(act, act_links)
            sums = [0]

            def split(seg, n, par, h):
                act.wait_ge(weights_landed[par], (n - par) * 8 + 16)
                if not (isinstance(n, int) and n == 0):
                    act.wait_ge(half_done, n * 2 + (h - 1))
                w = seg.width // 2
                act.activation(w_hi[:, h, 0:w], raw[:, par, h * w:(h + 1) * w], ACT.Copy).then_inc(hi_done, 1)

            def log_terms(out, in_, scale=1.0, bias=0.0):
                L.link(act.activation(out, in_, ACT.Abs, scale=scale, bias=bias))
                L.link(act.activation(out, out, ACT.Exp, scale=-1.0))
                return act.activation(out, out, ACT.Ln, bias=one[0:out.shape[0], :])

            def make_rstd(n, bank=STAT_BANK):
                L.link(act.activation(rstd[:], ps[:, bank, 0:T], ACT.Ln, scale=1.0 / n, bias=eps[:]))
                return act.activation(rstd[:], rstd[:], ACT.Exp, scale=-0.5)

            def stat_rstd(n):
                sums[0] += 1
                act.wait_ge(stat_ready, sums[0])
                make_rstd(n).then_inc(rstd_ready, 1)

            def wait_square(q):
                if not (isinstance(q, int) and q < 2):
                    act.wait_ge(sq_added, q - 1)

            def epilogue(seg, n, par, ls):
                b0, b1 = ps[:, 2 * par, 0:T], ps[:, 2 * par + 1, 0:T]
                act.wait_ge(half_done, n * 2 + 2)
                if seg.kind != "zr":
                    act.wait_ge(drained, n)
                if seg.kind == "zr":
                    act.activation(zr[:], ps[0:16, 2 * par, 0:T], ACT.Copy).then_inc(drained, 1)
                elif seg.kind in ("zconv", "z"):
                    act.activation(at(z, ls * 2 + seg.group), b0, ACT.Copy)
                    act.activation(at(z, ls * 2 + (seg.group + 1)), b1, ACT.Copy).then_inc(drained, 1)
                elif seg.kind == "kv":
                    act.activation(zkv[:, 0, :], b0, ACT.Copy)
                    act.activation(zkv[:, 1, :], b1, ACT.Copy).then_inc(drained, 1)
                elif seg.kind == "q":
                    act.activation(at(zq, ls * 2), b0, ACT.Copy, scale=0.125)
                    act.activation(at(zq, ls * 2 + 1), b1, ACT.Copy, scale=0.125).then_inc(drained, 1)
                elif seg.kind in ("gate", "gu"):
                    k = ls + seg.sig0
                    log_terms(sg[:, 0], b1 if seg.kind == "gate" else b0).then_inc(sig_terms, 1)
                    act.wait_ge(sig_log, k + 1)
                    act.activation(sg[:, 0], sg[:, 0], ACT.Exp).then_inc(sig_ready, 1)
                    if seg.kind == "gu":
                        act.wait_ge(drained, n + 1)
                        act.activation(at(hid_hi, ls + seg.first % BLK), prod[:], ACT.Copy).then_inc(hid_hi_done, 1)
                elif seg.kind == "sgu":
                    for b, bank in enumerate((b0, b1)):
                        act.activation(sqb[:, b], bank, ACT.Square, scale=GELU_K ** 0.5).then_inc(gelu_sq, 1)
                    for b in range(2):
                        act.wait_ge(gelu_arg, ls * 2 + (seg.gel0 + b + 1))
                        log_terms(sg[:, b], sqb[:, b]).then_inc(sig_terms, 1)
                    for b in range(2):
                        act.wait_ge(sig_log, ls * 2 + (seg.sig0 + b + 1))
                        act.activation(sg[:, b], sg[:, b], ACT.Exp).then_inc(sig_ready, 1)
                elif seg.kind == "out" or seg.group:
                    for b in range(2 if seg.two else 1):
                        j = ls * 2 + b if seg.two else ls
                        act.wait_ge(x_updated, j + (seg.x0 + 1))
                        q = j + seg.q0
                        wait_square(q)
                        act.activation(sqb[:, b if seg.two else (seg.q0 + par + seg.n0) % 2], at(x, j), ACT.Square).then_inc(sq_ready, 1)

            def ada_copy(u):
                act.wait_ge(ada_used, unit_no(u) * 4 + 4)
                if not first_unit(u):
                    act.wait_ge(ada_cols, unit_no(u))
                act.activation(adarow[:], ps[:, ADA_BANK, :], ACT.Copy).then_inc(ada_rows, 1)

            def conv_squares():
                for j in range(CT):
                    q = 16 + j
                    wait_square(q)
                    act.activation(sqb[:, q % 2, 0:NP_TOK], y_all[:, j], ACT.Square)
                    act.activation(seqs(sqb[:, q % 2, NP_TOK:T]), y_all_s[:, j], ACT.Square).then_inc(sq_ready, 1)

            def conv_affine():
                for j in range(CT):
                    gj, bj = VEC["conv_ln_g"] + j, VEC["conv_ln_b"] + j
                    for y in (y_all[:, j], y_all_s[:, j]):
                        ins = act.activation(y, y, ACT.Identity, scale=vec[:, gj:gj + 1], bias=vec[:, bj:bj + 1])
                ins.then_inc(conv_affined, 1)

            def conv_silu(k):
                if k < CT // 2:
                    s, js = (sg, sqb)[k % 2], slice(2 * k, 2 * k + 2)
                    if k >= 2:
                        act.wait_ge(conv_y, k - 1)
                    L.mark(act.activation(s[:, :, 0:NP_TOK], y_all[:, js], ACT.Abs))
                    for b in range(2):
                        ins = act.activation(seqs(s[:, b, NP_TOK:T]), y_all_s[:, 2 * k + b], ACT.Abs)
                        L.mark(ins)
                    L.wait(L.n)
                    L.link(act.activation(s[:], s[:], ACT.Exp, scale=-1.0))
                    act.activation(s[:], s[:], ACT.Ln, bias=one[:]).then_inc(conv_terms, 1)
                if k:
                    s = (sg, sqb)[(k - 1) % 2]
                    act.wait_ge(conv_log, k)
                    act.activation(s[:], s[:], ACT.Exp).then_inc(conv_sig, 1)

            def body(seg, i, base, last=False):
                for j, (n, par, ls) in enumerate(steps_of(seg, i, base)):
                    end = last and j == seg.m - 1
                    nxt = seg.next if end else seg
                    hurry = end and seg.then_wait
                    if nxt:
                        split(nxt, n + 1, 1 - par, 0)
                    if seg.unit is not None and j == 1:
                        ada_copy((i, seg.unit + base))
                    if seg.kind == "z" and ls == 2:
                        stat_rstd(CT * P)
                        act.wait_ge(normed, 1)
                        conv_affine()
                    if seg.kind == "z" and ls == 3:
                        for k in range(2, CT // 2 + 1):
                            conv_silu(k)
                    if nxt and not hurry:
                        split(nxt, n + 1, 1 - par, 1)
                    epilogue(seg, n, par, ls)
                    if seg.kind == "z" and ls == 1:
                        act.wait_ge(centred, 1)
                        conv_squares()
                    if seg.kind == "z" and ls == 2:
                        act.wait_ge(conv_affined, 1)
                        for k in range(2):
                            conv_silu(k)
                    if nxt and hurry and not seg.mixed_next:
                        split(nxt, n + 1, 1 - par, 1)

            def norm(k, final=False):
                stat_rstd(D)
                layer, part = divmod(k, 2)
                shift = layer * 96 + part * 48
                for g in range(4):
                    act.wait_ge(tn_ready, 4 * k + g + 1)
                    for b in range(4):
                        j = 4 * g + b
                        if final:
                            ins = act.activation(tn[:, g % 2, b, :], tn[:, g % 2, b, :], ACT.Copy,
                                                 scale=vec[:, VEC["g_final"] + j:VEC["g_final"] + j + 1])
                        else:
                            ins = act.activation(tn[:, g % 2, b, 0:NP_TOK], tn[:, g % 2, b, 0:NP_TOK], ACT.Identity,
                                                 scale=amod[:, j, 0:1], bias=mods[:, shift + j, 0:1])
                    if final:
                        ins.then_inc(y_ready, 1)
                        continue
                    L.link(ins)
                    act.wait_ge(tn_samples, 4 * k + g + 1)
                    act.activation(act_hi[:, 4 * g:4 * g + 4, :], tn[:, g % 2], ACT.Copy).then_inc(nhi_done, 1)

            def mix0(after):
                def gate_terms(h):
                    act.wait_ge(la_ready, h + 1)
                    bg = VEC["gla_b_gate"] + h
                    log_terms(la_terms_of, la, bias=vec[:, bg:bg + 1]).then_inc(la_terms, 1)

                def gate_exps(h):
                    act.wait_ge(b_ready, h + 1)
                    act.activation(geb_of[h % 2], gb, ACT.Exp, scale=1.0 / 16)
                    act.activation(prod[:], gb, ACT.Exp, scale=-1.0 / 16)
                    act.activation(la_terms_of, la_terms_of, ACT.Exp, scale=1.0 / 16).then_inc(e_ready, 1)

                gate_terms(0)
                act.wait_ge(conv_y, CT // 2)
                act.activation(act_hi[:, 0:CT, 0:NP_TOK], y_all, ACT.Copy)
                for s in range(NSEQ):
                    ins = act.activation(act_hi[:, 0:CT, NP_TOK + TS * s:NP_TOK + TS * (s + 1)], y_all_s[:, :, s], ACT.Copy)
                ins.then_inc(mixhi_done, CT)
                gate_exps(0)
                act.wait_ge(act_ready, KT + CT)
                act.wait_ge(conv_stored, 16 * (CT + 1))

                def values_to_tok(h):
                    act.wait_ge(v_turned, h + 1)
                    act.activation(vtok[:].rearrange("p c n -> p (c n)"), ps[:, 5, :], ACT.Copy)
                    act.activation(vtok_s[:], ps[0:32, 6, 256:512], ACT.Copy).then_inc(tok_ready, 1)

                values_to_tok(0)
                for h in range(HEADS):
                    act.wait_ge(kl_turned, h + 1)
                    act.activation(kltok[:].rearrange("p c n -> p (c n)"), ps[:, 6, 0:256], ACT.Copy).then_inc(tok_ready, 1)
                    act.wait_ge(os_turned, h + 1)
                    act.activation(os_tok[:].rearrange("p r n -> p (r n)"), ps[:, 5, :], ACT.Copy).then_inc(os_copied, 1)
                    act.wait_ge(qk_ready, h + 1)
                    log_terms(sg[:], z[:, 16 + 2 * h:18 + 2 * h, :]).then_inc(gsig_terms, 1)
                    act.wait_ge(gsig_log, h + 1)
                    act.activation(sg[:], sg[:], ACT.Exp).then_inc(gsig_ready, 1)
                    if h < HEADS - 1:
                        gate_terms(h + 1)
                        gate_exps(h + 1)
                    if h == 0:
                        split(after, after.n0, after.n0 % 2, 1)
                    act.wait_ge(gla_yy, h + 1)
                    act.activation(sqb[:], ps[:, 2:4, 0:T], ACT.Square).then_inc(osq_ready, 1)
                    act.wait_ge(ms_ready, h + 1)
                    make_rstd(256, 4).then_inc(gla_rs, 1)
                    if h < HEADS - 1:
                        values_to_tok(h + 1)
                    act.wait_ge(gla_y, h + 1)
                    act.activation(act_hi[:, CT + 2 * h:CT + 2 * h + 2, :], sqb[:], ACT.Copy).then_inc(mixhi_done, 1)

            def exps_of(blk, first, last):
                k0 = 0 if blk else P
                if first == 0:
                    act.wait_ge(row_max, blk + 1)
                    act.activation(small[:, blk, 2, :], small[:, blk, 2, :], ACT.Exp).then_inc(sink_exp, 1)
                for h in range(first, last):
                    act.activation(sc[blk][:, h, k0:256], sc[blk][:, h, k0:256], ACT.Exp, bias=small[:, blk, 1, h:h + 1],
                                   accum_out=small[:, blk, 3, h:h + 1]).then_inc(exps, 1)

            def turned_copies(blk, first, last):
                k0 = 0 if blk else P
                for turn in range(16 * blk + first, 16 * blk + last):
                    act.wait_ge(pt_turned, turn + 1)
                    if turn >= 2:
                        act.wait_ge(pv_done, turn - 1)
                    act.activation(ptp[:, turn % 2, k0:256], ps[:, 6 + turn % 2, k0:256], ACT.Copy).then_inc(pt_ready, 1)

            def mix1(after):
                act.wait_ge(centred, 2)
                for j in range(CT):
                    q = 56 + j
                    wait_square(q)
                    act.activation(sqb[:, q % 2], zv[:, j, :], ACT.Square).then_inc(sq_ready, 1)
                stat_rstd(CT * P)
                act.wait_ge(normed, 2)
                for j in range(CT):
                    gj, bj = VEC["sgu_ln_g"] + j, VEC["sgu_ln_b"] + j
                    act.activation(zv[:, j, :], zv[:, j, :], ACT.Identity, scale=vec[:, gj:gj + 1],
                                   bias=vec[:, bj:bj + 1]).then_inc(v_ln, 1)
                attention_exps = [(0, 0, 8), (0, 8, 16), (1, 0, 8), (1, 8, 16)]
                for g in range(4):
                    act.wait_ge(vmix_turned, g + 1)
                    if g:
                        act.wait_ge(mixed_ready, 2 * g)
                    act.activation(vmix[:].rearrange("p c n -> p (c n)"), ps[:, 5, :], ACT.Copy)
                    act.activation(vmix_s[:], ps[0:32, 6, 0:256], ACT.Copy).then_inc(vmix_ready, 1)
                    exps_of(*attention_exps[g])
                split(after, after.n0, after.n0 % 2, 1)
                act.wait_ge(vtok1_turned, 1)
                act.activation(vtok1[:].rearrange("p c n -> p (c n)"), ps[:, 5, 0:256], ACT.Copy)
                act.activation(vnew[:], ps[0:32, 5, 256:384], ACT.Copy).then_inc(vtok1_ready, 1)
                turned_copies(0, 0, 16)
                turned_copies(1, 0, 8)
                act.wait_ge(row_max, 3)
                act.activation(small[:, 2, 2, 0:4], small[:, 2, 2, 0:4], ACT.Exp).then_inc(sink_exp, 1)
                for c in range(4):
                    act.activation(sc_s[:, c, :], sc_s[:, c, :], ACT.Exp, bias=small[:, 2, 1, c:c + 1],
                                   accum_out=small[:, 2, 3, c:c + 1]).then_inc(exps, 1)
                turned_copies(1, 8, 16)
                act.wait_ge(pts_turned, 1)
                act.wait_ge(pv_done, 32)
                act.activation(ptp[:, 0, :], ps[:, 4, :], ACT.Copy)
                act.activation(ptp[0:32, 1, :], ps[0:32, 5, :], ACT.Copy).then_inc(pts_ready, 1)
                act.wait_ge(sgu_mixed, CT)
                act.activation(act_hi[:, 0:CT, :], zu[:], ACT.Copy).then_inc(mixhi_done, 1)
                act.wait_ge(yd_ready, 3)
                act.activation(act_hi[:, CT:KT, :], zq[:], ACT.Copy).then_inc(mixhi_done, 1)

            act.preload_act_table_set("natural_log_exp_and_others")
            act.wait_ge(ones_set, 4)
            act.wait_ge(cond_landed, 16)
            cols = sg[:, 0, 0:KT * S9].rearrange("p (k s) -> p k s", s=S9)
            log_terms(cols, cond[:, :, 0:S9]).then_inc(cond_terms, 1)
            act.wait_ge(cond_log, 1)
            act.activation(cols, cols, ACT.Exp).then_inc(cond_sig, 1)
            def squares_of_x(j):
                for b in range(2):
                    wait_square(j + b)
                    act.activation(sqb[:, b], at(x, j + b), ACT.Square).then_inc(sq_ready, 1)

            act.wait_ge(cond_ready, 1)
            ada_copy((None, 0))
            act.wait_ge(x_landed, 16)
            squares_of_x(0)
            with act.Fori(0, PRE - 1) as i:
                ada_copy((i, 1))
                squares_of_x(2 * i + 2)
            split(SEGS[0], 0, 0, 0)
            split(SEGS[0], 0, 0, 1)
            norms = 0
            for seg, after in zip(["norm"] + PLAN, PLAN + [None]):
                if seg == "norm":
                    norm(norms, final=norms == 4)
                    norms += 1
                elif seg == "mix0":
                    mix0(after)
                elif seg == "mix1":
                    mix1(after)
                else:
                    if seg.peel:
                        body(seg, None, 0)
                    turns = seg.bodies - 1 - seg.peel
                    if turns:
                        with act.Fori(0, turns) as i:
                            L.enter(i, seg.act_links)
                            body(seg, i, seg.peel)
                            L.leave(turns)
                    body(seg, None, seg.bodies - 1, last=True)

        @block.vector
        def _(dve):
            L = Links(dve, dve_links)

            def split_lo(seg, n, par, h):
                dve.wait_ge(hi_done, n * 2 + (h + 1))
                w = seg.width // 2
                dve.tensor_tensor(w_lo[:, h, 0:w], raw[:, par, h * w:(h + 1) * w], w_hi[:, h, 0:w].bitcast(F32),
                                  ALU.subtract).then_inc(split_done, 1)

            def resid(seg, bank, j, b, first_inc, last_inc):
                g = (seg.layer * 96 + (2 if seg.kind == "out" else 5) * KT) + j
                tmp = xtmp[:, b]
                if last_inc:
                    if not (isinstance(j, int) and j + seg.x0 < 1):
                        dve.wait_ge(x_updated, j + seg.x0)
                if L.n:
                    L.wait(L.n)
                m = L.mark(dve.tensor_tensor(tmp, seqs(bank[:, NP_TOK:T]),
                                             at(mods, g, 1, S9).unsqueeze(2).to_broadcast([P, NSEQ, TS]), ALU.mult))
                ins = dve.scalar_tensor_tensor(at(x, j, 0, NP_TOK), bank[:, 0:NP_TOK], at(mods, g, 0, 1),
                                               at(x, j, 0, NP_TOK), ALU.mult, ALU.add)
                if first_inc:
                    ins.then_inc(first_inc, 1)
                L.wait(m)
                ins = dve.tensor_tensor(seqs(at(x, j, NP_TOK, T)), seqs(at(x, j, NP_TOK, T)), tmp, ALU.add)
                if last_inc:
                    ins.then_inc(last_inc, 1)
                else:
                    L.mark(ins)

            def epilogue(seg, n, par, ls):
                if seg.kind in ("zr", "zconv", "z", "kv", "q"):
                    return
                b0, b1 = ps[:, 2 * par, 0:T], ps[:, 2 * par + 1, 0:T]
                dve.wait_ge(half_done, n * 2 + 2)
                dve.wait_ge(drained, n)
                if seg.kind in ("gate", "gu"):
                    k = ls + seg.sig0
                    s, gate_bank = sg[:, 0], b1 if seg.kind == "gate" else b0
                    dve.wait_ge(sig_terms, k + 1)
                    dve.scalar_tensor_tensor(s, gate_bank, 0.0, s, ALU.min, ALU.subtract).then_inc(sig_log, 1)
                    dve.wait_ge(sig_ready, k + 1)
                    if seg.kind == "gate":
                        dve.tensor_tensor(at(uext, ls, HIST, UW), b0[:, 0:NP_TOK], s[:, 0:NP_TOK], ALU.mult)
                        dve.tensor_tensor(rows_s(ls)[:, :, HIST:SW], seqs(b0[:, NP_TOK:T]), seqs(s[:, NP_TOK:T]),
                                          ALU.mult).then_inc(drained, 1)
                    else:
                        hid = ls + (seg.sig0 - CT - (2 * CT if seg.layer else 0))
                        if not (isinstance(hid, int) and hid == 0):
                            dve.wait_ge(hid_ready, hid)
                        L.link(dve.tensor_tensor(prod[:], b0, s, ALU.mult))
                        dve.tensor_tensor(prod[:], prod[:], b1, ALU.mult).then_inc(drained, 1)
                        j = ls + seg.first % BLK
                        dve.wait_ge(hid_hi_done, hid + 1)
                        dve.tensor_tensor(at(hid_lo, j), prod[:], at(hid_hi, j).bitcast(F32), ALU.subtract) \
                            .then_inc(hid_ready, 1)
                elif seg.kind == "sgu":
                    for b, bank in enumerate((b0, b1)):
                        dve.wait_ge(gelu_sq, ls * 2 + (seg.gel0 + b + 1))
                        dve.scalar_tensor_tensor(sqb[:, b], sqb[:, b], GELU_2C, bank, ALU.add, ALU.mult) \
                            .then_inc(gelu_arg, 1)
                    for b in range(2):
                        dve.wait_ge(sig_terms, ls * 2 + (seg.sig0 + b + 1))
                        dve.scalar_tensor_tensor(sg[:, b], sqb[:, b], 0.0, sg[:, b], ALU.min, ALU.subtract) \
                            .then_inc(sig_log, 1)
                    for b, (bank, out) in enumerate(((b0, zu), (b1, zv))):
                        dve.wait_ge(sig_ready, ls * 2 + (seg.sig0 + b + 1))
                        ins = dve.tensor_tensor(at(out, ls), bank, sg[:, b], ALU.mult)
                    ins.then_inc(drained, 1)
                elif seg.kind == "out":
                    resid(seg, b0, ls * 2, 0, None, x_updated)
                    resid(seg, b1, ls * 2 + 1, 1, drained, x_updated)
                else:
                    resid(seg, b0, ls, 0, drained, x_updated if seg.group else None)

            def conv(j, taps, marks):
                w = VEC["conv_w"]
                if 0 in taps:
                    if not (isinstance(j, int) and j == 0):
                        dve.wait_ge(conv_ready, j)
                    if L.n:
                        L.wait(L.n)
                for k in taps:
                    wk = flat_at(vec, j * TAPS + (w + k))
                    for s in range(2):
                        row = taps_s(j, k) if s else at(uext, j, k, k + NP_TOK)
                        acc = seqs(cacc[:, NP_TOK:T]) if s else cacc[:, 0:NP_TOK]
                        out = acc if k < TAPS - 1 else taps_s(j, 0) if s else at(uext, j, 0, NP_TOK)
                        if marks[s]:
                            L.wait(marks[s])
                        if k == 0:
                            ins = dve.tensor_scalar(out, row, wk, flat_at(vec, j + VEC["conv_b"]), ALU.mult, ALU.add)
                        else:
                            ins = dve.scalar_tensor_tensor(out, row, wk, acc, ALU.mult, ALU.add)
                        if k == TAPS - 1 and s:
                            ins.then_inc(conv_ready, 1)
                        else:
                            marks[s] = L.mark(ins)

            def ada_bias(u):
                dve.wait_ge(ada_cols, unit_no(u) + 1)
                b = bass.ds(unit_no(u) * 4 + VEC["b_ada"], 4)
                dve.tensor_tensor(mods[:, bass.ds(unit_no(u) * 4, 4), :],
                                  ps[:, SEL_BANK, 0:64].rearrange("p (q s) -> p q s", s=16)[:, :, 0:S9],
                                  vec[:, b].unsqueeze(2).to_broadcast([P, 4, S9]), ALU.add).then_inc(ada_biased, 1)

            def body(seg, i, base, last=False):
                marks = [0, 0]
                convolves, opening = seg.kind in ("gate", "zconv"), seg.kind == "gate" and i is None and base == 0
                tile = lin(i, 1, base + (4 if seg.kind == "zconv" else 0))
                for j, (n, par, ls) in enumerate(steps_of(seg, i, base)):
                    end = last and j == seg.m - 1
                    nxt = seg.next if end else seg
                    hurry = end and seg.then_wait
                    if nxt:
                        split_lo(nxt, n + 1, 1 - par, 0)
                        if seg.kind == "z" and ls == 2:
                            dve.wait_ge(rstd_ready, 2)
                            apply_stat(y_all, y_all_s, rstd, ALU.mult).then_inc(normed, 1)
                        if seg.kind == "z" and ls == 3:
                            for k in range(2, CT // 2 + 1):
                                conv_silu(k)
                        if convolves and not (opening and j == 0):
                            conv(tile, range(8) if j == 0 else range(16, 24) if not opening else range(16, 20), marks)
                        if not hurry:
                            split_lo(nxt, n + 1, 1 - par, 1)
                    if seg.kind == "z" and ls == 0:
                        centre(1, y_all, y_all_s, M_BANK)
                    if seg.kind == "z" and ls == 2:
                        for k in range(2):
                            conv_silu(k)
                    epilogue(seg, n, par, ls)
                    if nxt and hurry and not seg.mixed_next:
                        split_lo(nxt, n + 1, 1 - par, 1)
                    if seg.unit is not None and j == 1:
                        ada_bias((i, seg.unit + base))
                    if convolves and opening and j == 0:
                        dve.wait_ge(drained, n + 1)
                        conv(tile, range(16), marks)
                    elif convolves:
                        conv(tile, range(8, 16) if j == 0 else range(24, TAPS) if not opening else range(20, TAPS), marks)

            def norm(k, final=False):
                layer, part = divmod(k, 2)
                if not final:
                    scale = layer * 96 + part * 48 + KT
                    g = VEC["g_ffn" if part else "g_mix"] + KT * layer
                    L.link(dve.scalar_tensor_tensor(amod[:], mods[:, scale:scale + KT, :], 1.0,
                                                    vec[:, g:g + KT].unsqueeze(2).to_broadcast([P, KT, S9]),
                                                    ALU.add, ALU.mult))
                shift = layer * 96 + part * 48
                base = KT * [0, 2, 3, 5, 6][k]
                if base:
                    dve.wait_ge(act_ready, base)
                dve.wait_ge(rstd_ready, NORM_STATS[k])

                def scaled(g):
                    if final and g >= 2:
                        dve.wait_ge(y_stored[g % 2], 16)
                    elif g >= 2:
                        dve.wait_ge(act_ready, base + 4 * (g - 1))
                    dve.tensor_tensor(tn[:, g % 2], x[:, 4 * g:4 * g + 4, :],
                                      rstd[:].unsqueeze(1).to_broadcast([P, 4, T]), ALU.mult).then_inc(tn_ready, 1)

                def samples(g):
                    dve.wait_ge(tn_ready, 4 * k + g + 1)
                    cols = tn[:, g % 2, :, NP_TOK:T].rearrange("p k (b t) -> p k b t", t=TS)
                    js = slice(4 * g, 4 * g + 4)
                    L.link(dve.tensor_tensor(cols, cols, amod[:, js, 1:S9].unsqueeze(3).to_broadcast([P, 4, NSEQ, TS]), ALU.mult))
                    dve.tensor_tensor(cols, cols, mods[:, shift + 4 * g:shift + 4 * g + 4, 1:S9].unsqueeze(3)
                                      .to_broadcast([P, 4, NSEQ, TS]), ALU.add).then_inc(tn_samples, 1)

                def lo(g):
                    dve.wait_ge(nhi_done, 4 * k + g + 1)
                    js = slice(4 * g, 4 * g + 4)
                    dve.tensor_tensor(act_lo[:, js, :], tn[:, g % 2], act_hi[:, js, :].bitcast(F32), ALU.subtract) \
                        .then_inc(act_ready, 4)

                for g in range(4):
                    scaled(g)
                    if not final:
                        samples(g)
                        if g:
                            lo(g - 1)
                if not final:
                    lo(3)

            def centre(k, y, y_s, bank):
                dve.wait_ge(mean_ready, k)
                dve.tensor_scalar(prod[:], ps[:, bank, 0:T], 1.0 / (CT * P), None, ALU.mult).then_inc(mean_used, 1)
                dve.wait_ge(mean_used, k)
                apply_stat(y, y_s, prod, ALU.subtract).then_inc(centred, 1)

            def apply_stat(y, y_s, by, op):
                if y_s is None:
                    return dve.tensor_tensor(y, y, by[:].unsqueeze(1).to_broadcast([P, CT, T]), op)
                dve.tensor_tensor(y, y, by[:, 0:NP_TOK].unsqueeze(1).to_broadcast([P, CT, NP_TOK]), op)
                for s in range(NSEQ):
                    cols = by[:, NP_TOK + TS * s:NP_TOK + TS * (s + 1)].unsqueeze(1).to_broadcast([P, CT, TS])
                    ins = dve.tensor_tensor(y_s[:, :, s], y_s[:, :, s], cols, op)
                return ins

            def conv_silu(k):
                if k < CT // 2:
                    s, js = (sg, sqb)[k % 2], slice(2 * k, 2 * k + 2)
                    dve.wait_ge(conv_terms, k + 1)
                    dve.scalar_tensor_tensor(s[:, :, 0:NP_TOK], y_all[:, js], 0.0, s[:, :, 0:NP_TOK], ALU.min, ALU.subtract)
                    for b in range(2):
                        ss = seqs(s[:, b, NP_TOK:T])
                        ins = dve.scalar_tensor_tensor(ss, y_all_s[:, 2 * k + b], 0.0, ss, ALU.min, ALU.subtract)
                    ins.then_inc(conv_log, 1)
                if k:
                    s, js = (sg, sqb)[(k - 1) % 2], slice(2 * k - 2, 2 * k)
                    dve.wait_ge(conv_sig, k)
                    dve.tensor_tensor(y_all[:, js], y_all[:, js], s[:, :, 0:NP_TOK], ALU.mult)
                    for b in range(2):
                        y = y_all_s[:, 2 * k - 2 + b]
                        ins = dve.tensor_tensor(y, y, seqs(s[:, b, NP_TOK:T]), ALU.mult)
                    ins.then_inc(conv_y, 1)

            def mix0(after):
                def gate_sum(h):
                    bg = VEC["gla_b_gate"] + h
                    dve.wait_ge(la_terms, h + 1)
                    L.link(dve.tensor_scalar(la_sum, la, vec[:, bg:bg + 1], 0.0, ALU.add, ALU.min))
                    L.link(dve.tensor_tensor(la_sum, la_sum, la_terms_of, ALU.subtract))
                    L.link(dve.tensor_tensor_scan(gb, chunk_start[:], la_sum, 0.0, ALU.mult, ALU.add))
                    chunks = gb[:, 0:NP_TOK].rearrange("p (c s) -> p c s", s=64)
                    dve.tensor_tensor(la_terms_of[:, 0:NP_TOK].rearrange("p (c s) -> p c s", s=64),
                                      chunks[:, :, 63:64].to_broadcast([P, 4, 64]), chunks, ALU.subtract)
                    dve.tensor_tensor(seqs(la_terms_of[:, NP_TOK:T]), seqs(gb[:, NP_TOK:T])[:, :, 3:4].to_broadcast([P, NSEQ, TS]),
                                      seqs(gb[:, NP_TOK:T]), ALU.subtract).then_inc(b_ready, 1)

                def gate_keys(h):
                    q, k = z[:, 2 * h, :], z[:, 2 * h + 1, :]
                    dve.wait_ge(e_ready, h + 1)
                    dve.tensor_tensor(gkl_of[h % 2], k, la_terms_of, ALU.mult).then_inc(kl_ready, 1)
                    dve.wait_ge(kl_ready, h + 1)
                    dve.tensor_tensor(k, k, prod[:], ALU.mult)
                    dve.scalar_tensor_tensor(q, q, float(P) ** -0.5, geb_of[h % 2], ALU.mult, ALU.mult).then_inc(qk_ready, 1)

                dve.wait_ge(mix0_consts, 16 * 6)
                dve.wait_ge(half_done, 2 * (Z_SEG.n0 + Z_SEG.steps))
                gate_sum(0)
                dve.wait_ge(mixhi_done, CT)
                dve.tensor_tensor(act_lo[:, 0:CT, 0:NP_TOK], y_all, act_hi[:, 0:CT, 0:NP_TOK].bitcast(F32), ALU.subtract)
                for s in range(NSEQ):
                    cols = slice(NP_TOK + TS * s, NP_TOK + TS * (s + 1))
                    ins = dve.tensor_tensor(act_lo[:, 0:CT, cols], y_all_s[:, :, s], act_hi[:, 0:CT, cols].bitcast(F32), ALU.subtract)
                ins.then_inc(act_ready, CT)
                dve.wait_ge(drained, Z_SEG.n0 + Z_SEG.steps)
                gate_keys(0)
                dve.wait_ge(conv_stored, 16 * (CT + 1))
                dve.wait_ge(act_ready, KT + CT)
                L.link(dve.memset(att[:], 0.0))
                L.link(dve.memset(att_s[:], 0.0))
                for h in range(HEADS):
                    decay = geb_of[h % 2]
                    dve.wait_ge(kl_turned, h + 1)
                    dve.tensor_tensor(klm[:], ps[0:32, 7, 0:P].unsqueeze(1).to_broadcast([32, NSEQ, P]),
                                      seqmask[:].unsqueeze(2).to_broadcast([32, NSEQ, P]), ALU.mult).then_inc(tok_ready, 1)
                    dve.wait_ge(att_turned, h + 1)
                    for c in range(2):
                        rows = slice(64 * c, 64 * c + 64)
                        dve.copy_predicated(att[rows, :, rows], causal64[rows], ps[rows, 4, 0:P].rearrange("p (c s) -> p c s", s=64))
                    dve.copy_predicated(att_s[:], causal_s[:], ps[0:32, 4, P:P + 32]).then_inc(att_ready, 1)
                    dve.wait_ge(sadd_ready, h + 1)
                    if h:
                        dve.wait_ge(gstate_stored, 16 * h)
                    adds = [ps[:, c % 2, 256 * (c // 2):256 * (c // 2) + 256] for c in range(4)]
                    L.link(dve.tensor_copy(gs[:, 0, :], adds[0]))
                    for c in range(1, 4):
                        ins = dve.scalar_tensor_tensor(gs[:, c, :], gs[:, c - 1, :], decay[:, 64 * c + 63:64 * c + 64],
                                                       adds[c], ALU.mult, ALU.add)
                        if c < 3:
                            L.link(ins)
                    ins.then_inc(s_chain, 1)
                    dve.wait_ge(gsig_terms, h + 1)
                    dve.scalar_tensor_tensor(sg[:], z[:, 16 + 2 * h:18 + 2 * h, :], 0.0, sg[:], ALU.min, ALU.subtract) \
                        .then_inc(gsig_log, 1)
                    if h < HEADS - 1:
                        gate_sum(h + 1)
                        gate_keys(h + 1)
                    if h == 0:
                        split_lo(after, after.n0, after.n0 % 2, 1)
                    dve.wait_ge(gla_yy, h + 1)
                    for r in range(2):
                        dve.wait_ge(snew_ready, 2 * h + r + 1)
                        for s in range(4):
                            b = 4 * r + s
                            st = aring[:, h % 2, 256 * b:256 * (b + 1)]
                            ins = dve.scalar_tensor_tensor(st, st, decay[:, NP_TOK + TS * b + 3:NP_TOK + TS * b + 4],
                                                           ps[:, SNEW_BANKS[r] + s // 2, 256 * (s % 2):256 * (s % 2) + 256], ALU.mult, ALU.add)
                        ins.then_inc(snew_used, 1)
                    dve.wait_ge(gsig_ready, h + 1)
                    for b in range(2):
                        gn = VEC["gla_g_norm"] + b
                        ins = dve.scalar_tensor_tensor(sg[:, b], z[:, 16 + 2 * h + b, :], vec[:, gn:gn + 1], sg[:, b],
                                                       ALU.mult, ALU.mult)
                    L.link(ins)
                    dve.wait_ge(gla_rs, h + 1)
                    m = L.mark(dve.tensor_tensor(sqb[:], ps[:, 2:4, 0:T], rstd[:].unsqueeze(1).to_broadcast([P, 2, T]), ALU.mult))
                    L.wait(m)
                    dve.tensor_tensor(sqb[:], sqb[:], sg[:], ALU.mult).then_inc(gla_y, 1)
                    dve.wait_ge(mixhi_done, CT + h + 1)
                    js = slice(CT + 2 * h, CT + 2 * h + 2)
                    dve.tensor_tensor(act_lo[:, js, :], sqb[:], act_hi[:, js, :].bitcast(F32), ALU.subtract) \
                        .then_inc(act_ready, 2)
                dve.wait_ge(gstate_stored, 16 * HEADS)

            def attend(w, rows, n, sink):
                m = small[:, w]
                L.link(dve.tensor_reduce(m[:, 0, 0:n], rows, AX.X, ALU.max))
                L.link(dve.tensor_tensor(m[:, 0, 0:n], m[:, 0, 0:n], sink, ALU.max))
                L.link(dve.tensor_scalar(m[:, 1, 0:n], m[:, 0, 0:n], -1.0, None, ALU.mult))
                dve.tensor_tensor(m[:, 2, 0:n], sink, m[:, 0, 0:n], ALU.subtract).then_inc(row_max, 1)

            def denominators(w, n):
                dve.wait_ge(exps, (16, 32, 36)[w])
                dve.wait_ge(sink_exp, w + 1)
                L.link(dve.tensor_tensor(small[:, w, 4, 0:n], small[:, w, 3, 0:n], small[:, w, 2, 0:n], ALU.add))
                L.link(dve.reciprocal(small[:, w, 5, 0:n], small[:, w, 4, 0:n]))

            def probabilities(blk):
                k0 = 0 if blk else P
                denominators(blk, 16)
                for h in range(16):
                    dve.tensor_scalar(sc[blk][:, h, k0:256], sc[blk][:, h, k0:256], small[:, blk, 5, h:h + 1], None, ALU.mult) \
                        .then_inc(probs_ready, 1)

            def values_out(blk):
                dve.wait_ge(pv_done, 16 * blk + 16)
                dve.wait_ge(qs_ready, 1)
                dve.tensor_copy(zq[:, :, blk * P:(blk + 1) * P],
                                ps[:, 2:4, :].rearrange("p a (r n) -> p (a r) n", n=P)).then_inc(yd_ready, 1)

            def add_distances(blk, first, last):
                k0 = 0 if blk else P
                for h in range(first, last):
                    dve.wait_ge(scores_ready, 16 * blk + h + 1)
                    dve.scalar_tensor_tensor(sc[blk][:, h, k0:256], dist[:, k0:256], SLOPES[h], ps[:, h % 4, k0:256],
                                             ALU.mult, ALU.add).then_inc(scored, 1)

            def mix1(after):
                centre(2, zv[:], None, MEAN_BANK)
                dve.wait_ge(mix1_consts, 16 * 6)
                add_distances(0, 0, 16)
                add_distances(1, 0, 8)
                dve.wait_ge(rstd_ready, 5)
                apply_stat(zv[:], None, rstd, ALU.mult).then_inc(normed, 1)
                add_distances(1, 8, 16)
                dve.tensor_copy(qs[:], zq[:, :, NP_TOK:T].rearrange("p r (b t) -> p b r t", t=TS)).then_inc(qs_ready, 1)
                for blk in range(2):
                    k0 = 0 if blk else P
                    dve.wait_ge(scored, 16 * blk + 16)
                    attend(blk, sc[blk][:, :, k0:256], 16, sinks[:, 0:16])
                for j in range(CT):
                    dve.wait_ge(mixed_ready, j + 1)
                    dve.tensor_tensor(zu[:, j, :], zu[:, j, :], ps[:, MIX_BANKS[j % 2], 0:T], ALU.mult).then_inc(sgu_mixed, 1)
                    if j == 5:
                        probabilities(0)
                probabilities(1)
                split_lo(after, after.n0, after.n0 % 2, 1)
                values_out(0)
                dve.wait_ge(scores_s_ready, 1)
                for pair in range(2):
                    m = L.mark(dve.tensor_tensor(sc_s[:, 2 * pair:2 * pair + 2], ps[:, 0:2, 256 * pair:256 * pair + KEYS],
                                                 bias_s[:, 2 * pair:2 * pair + 2], ALU.add))
                L.wait(m)
                attend(2, sc_s, 4, sinks[:, 16:20])
                denominators(2, 4)
                dve.tensor_tensor(sc_s, sc_s, small[:, 2, 5, 0:4].unsqueeze(2).to_broadcast([P, 4, KEYS]),
                                  ALU.mult).then_inc(probs_s_ready, 1)
                values_out(1)
                dve.wait_ge(mixhi_done, CT + HEADS + 1)
                dve.tensor_tensor(act_lo[:, 0:CT, :], zu[:], act_hi[:, 0:CT, :].bitcast(F32), ALU.subtract).then_inc(act_ready, CT)
                dve.wait_ge(os_ready, 1)
                for s in range(NSEQ):
                    ins = dve.tensor_copy(zq[:, :, NP_TOK + TS * s:NP_TOK + TS * (s + 1)],
                                          ps[:, 0, 32 * s:32 * s + 32].rearrange("p (r t) -> p r t", t=TS))
                ins.then_inc(yd_ready, 1)
                dve.wait_ge(mixhi_done, CT + HEADS + 2)
                dve.tensor_tensor(act_lo[:, CT:KT, :], zq[:], act_hi[:, CT:KT, :].bitcast(F32), ALU.subtract).then_inc(act_ready, CT)
                dve.wait_ge(cache_stored, 16 * 6)
                dve.wait_ge(sguv_stored, 16)

            cols = sg[:, 0, 0:KT * S9].rearrange("p (k s) -> p k s", s=S9)
            dve.wait_ge(cond_terms, 1)
            dve.scalar_tensor_tensor(cols, cond[:, :, 0:S9], 0.0, cols, ALU.min, ALU.subtract).then_inc(cond_log, 1)
            dve.wait_ge(cond_sig, 1)
            dve.tensor_tensor(cond[:, :, 0:S9], cond[:, :, 0:S9], cols, ALU.mult).then_inc(cond_ready, 1)
            dve.wait_ge(consts_landed, 48)
            ada_bias((None, 0))
            with dve.Fori(0, PRE - 1) as i:
                ada_bias((i, 1))
            split_lo(SEGS[0], 0, 0, 0)
            split_lo(SEGS[0], 0, 0, 1)
            norms = 0
            for seg, after in zip(["norm"] + PLAN, PLAN + [None]):
                if seg == "norm":
                    dve.wait_ge(ada_biased, [PRE, 22, 48, 48, 48][norms])
                    norm(norms, final=norms == 4)
                    norms += 1
                    if norms == 1:
                        dve.wait_ge(history_landed, 16 * CT)
                        dve.wait_ge(history_zero, 1)
                elif seg == "mix0":
                    mix0(after)
                elif seg == "mix1":
                    mix1(after)
                else:
                    if seg.peel:
                        body(seg, None, 0)
                    turns = seg.bodies - 1 - seg.peel
                    if turns:
                        with dve.Fori(0, turns) as i:
                            L.enter(i, seg.dve_links)
                            body(seg, i, seg.peel)
                            L.leave(turns)
                    body(seg, None, seg.bodies - 1, last=True)



def tiles(w):
    k, n = w.shape
    return w.reshape(k // P, P, n // P, P).transpose(2, 1, 0, 3).reshape(n // P, P, k)


def paired(a, b):
    return np.concatenate([a, b], axis=2)


def columns(v):
    return v.reshape(-1, P).T


def kernel(**inputs):
    import concourse.bacc as bacc
    from concourse.bass_utils import run_bass_kernel_spmd

    a = {k: np.asarray(v) for k, v in inputs.items()}
    f = {}
    tokens = np.concatenate([a["x_prompt"][0], a["x_sample"].reshape(NSEQ * TS, D)])
    f["xT"] = tokens.T.reshape(KT, P, T).transpose(1, 0, 2)
    f["cT"] = np.concatenate([a["c_prompt"], a["c_sample"]]).T.reshape(KT, P, S9).transpose(1, 0, 2)
    conv_w = a["conv_w"].T.reshape(CT, P, TAPS).transpose(1, 0, 2).reshape(P, CT * TAPS)
    f["vec"] = np.concatenate([columns(a[n].reshape(-1)) for n in VEC if n != "conv_w"] + [conv_w], axis=1)
    f["w_ada"] = a["w_ada"].reshape(2, 4, 4, P, UNITS, ADA_N).transpose(0, 4, 1, 3, 2, 5).reshape(8 * UNITS, P, 4 * ADA_N)
    ab = tiles(a["w_in_ab"][:, :40 * P])
    f["w_ab"] = np.concatenate([paired(ab[0:8], ab[8:16]), paired(ab[16:20], ab[20:24]), paired(ab[24:40:2], ab[25:40:2])])
    f["w_zr"] = tiles(np.pad(a["w_in_ab"][:, 40 * P:], ((0, 0), (0, P - 16))))
    cd = a["w_in_cd"]
    q0, kv0 = 2 * CT * P, 3 * CT * P
    q = cd[:, q0:kv0].reshape(D, 2, CT, 64).transpose(0, 2, 1, 3).reshape(D, CT * P)
    u, v, q, kv = tiles(cd[:, 0:CT * P]), tiles(cd[:, CT * P:q0]), tiles(q), tiles(cd[:, kv0:])
    f["w_cd"] = np.concatenate([paired(kv[0:1], kv[1:2]), paired(q[0::2], q[1::2]), paired(u, v)])
    wo1 = a["w_out"][1]
    wo1 = np.concatenate([wo1[:CT * P], wo1[CT * P:].reshape(2, CT, 64, D).transpose(1, 0, 2, 3).reshape(CT * P, D)])
    wo = [tiles(a["w_out"][0]), tiles(wo1)]
    f["w_out"] = np.concatenate([paired(w[0::2], w[1::2]) for w in wo])
    f["w_gu"] = np.concatenate([paired(tiles(a["w_ffn_gate"][i]), tiles(a["w_ffn_up"][i])) for i in range(2)])
    f["w_dn"] = np.concatenate([tiles(half) for i in range(2) for half in np.split(a["w_ffn_down"][i], 2)])
    f["gla_w_gate"] = a["gla_w_gate"]
    f["state_convT"] = a["state_conv"].transpose(2, 0, 1).reshape(CT, P, NSEQ, HIST).transpose(1, 0, 2, 3)
    f["state_glaT"] = a["state_gla"].transpose(1, 2, 0, 3).reshape(HEADS, P, NSEQ * 256)
    f["cache_kT"] = a["cache_k"].transpose(2, 3, 0, 1).reshape(P, NSEQ, P)
    f["cache_vT"] = a["cache_v"].transpose(1, 0, 2, 3).reshape(P, NSEQ, P)
    f["sgu_wT"] = a["sgu_w"].transpose(2, 0, 1)
    f["sgu_wsT"] = np.tile(a["sgu_w"][:, :TS, :TS].transpose(2, 0, 1), (NSEQ, 1, NSEQ))
    f["sgu_bT"] = np.concatenate([a["sgu_b"], a["sgu_b"], np.tile(a["sgu_b"][:, :TS], (1, NSEQ))], axis=1)[None]
    sinks_p = np.broadcast_to(a["att_sinks"], (P, 16))
    sinks_s = np.tile(np.repeat(a["att_sinks"].reshape(2, 8), TS, axis=1).T, (4, 2))
    f["sinks"] = np.concatenate([sinks_p, sinks_s], axis=1)
    f["ident"] = np.eye(P)
    f["sel"] = np.tile(np.eye(32, S9), (4, 1))
    t_ = np.arange(T)
    f["chunk_start"] = np.broadcast_to(np.where(t_ < NP_TOK, t_ % 64 != 0, t_ % TS != 0), (P, T))
    s_, q_ = np.arange(64)[:, None], np.arange(64)[None]
    f["causal64"] = np.tile((s_ <= q_)[:, None], (2, 2, 1)).astype(np.uint32)
    i_, j_ = np.arange(32)[:, None], np.arange(32)[None]
    f["causal_s"] = ((i_ // TS == j_ // TS) & (i_ <= j_)).astype(np.uint32)
    rows = np.arange(P)[:, None, None]
    f["own_rows"] = (rows % 32 == np.arange(32)) & (rows % 32 // TS == 4 * np.arange(2)[:, None] + rows // 32)
    f["seqmask"] = i_ // TS == np.arange(NSEQ)[None]
    d = np.arange(P)[:, None] - np.arange(256)[None] + P
    f["dist"] = np.where((d >= 0) & (d < P), -d, NEG)
    seq4, head, tok = np.arange(P) // 32, np.arange(P) // TS % 8, np.arange(P) % TS
    bias = np.full((P, 2, 2, KEYS), NEG)
    for pair in range(2):
        for g in range(2):
            slope = np.array(SLOPES)[g * 8 + head][:, None]
            dc = P + tok[:, None] - np.arange(P)[None]
            bias[:, pair, g, :P] = np.where(dc < P, -slope * dc, NEG)
            dn = tok[:, None] - j_ % TS
            own = (j_ // TS == (4 * pair + seq4)[:, None]) & (dn >= 0)
            bias[:, pair, g, P:] = np.where(own, -slope * dn, NEG)
    f["bias_s"] = bias.reshape(P, 4, KEYS)
    outs = {"y": (P, KT, T), "conv_p": (P, CT, HIST), "conv_s": (P, CT, NSEQ, HIST), "gla_p": (HEADS, P, 256),
            "gla_s": (HEADS, P, NSEQ * 256), "sgu_v": (P, CT, NSEQ * TS), "k_p": (P, P), "k_s_new": (P, NSEQ * TS),
            "k_s_old": (P, NSEQ, P - TS), "v_p": (P, P), "v_s_new": (NSEQ * TS, P), "v_s_old": (P - TS, NSEQ, P)}

    nc = bacc.Bacc("TRN2", target_bir_lowering=False, num_devices=1)
    arrays, t, o = {}, {}, {}
    for name, v in f.items():
        v = np.ascontiguousarray(v, dtype=v.dtype if v.dtype == np.uint32 else np.float32)
        arrays[f"in_{name}"] = v
        t[name] = nc.dram_tensor(f"in_{name}", v.shape, mybir.dt.from_np(v.dtype), kind="ExternalInput").ap()
    for name, shape in outs.items():
        o[name] = nc.dram_tensor(f"out_{name}", shape, F32, kind="ExternalOutput").ap()
    build(nc, t, o)
    res = run_bass_kernel_spmd(nc, [arrays], core_ids=[0]).results[0]
    r = {name: np.asarray(res[f"out_{name}"]) for name in outs}
    y = r["y"].transpose(2, 1, 0).reshape(T, D)
    k_s = np.concatenate([r["k_s_old"], r["k_s_new"].reshape(P, NSEQ, TS)], axis=2).transpose(1, 2, 0)
    v_s = np.concatenate([r["v_s_old"].transpose(1, 0, 2), r["v_s_new"].reshape(NSEQ, TS, P)], axis=1)
    return (y[:NP_TOK].reshape(1, NP_TOK, D), y[NP_TOK:].reshape(NSEQ, TS, D),
            r["conv_p"].transpose(2, 1, 0).reshape(1, HIST, CT * P),
            r["conv_s"].transpose(2, 3, 1, 0).reshape(NSEQ, HIST, CT * P),
            r["gla_p"].reshape(1, HEADS, P, 256),
            r["gla_s"].reshape(HEADS, P, NSEQ, 256).transpose(2, 0, 1, 3),
            r["sgu_v"].transpose(2, 1, 0).reshape(NSEQ, TS, CT * P),
            r["k_p"].T.reshape(1, P, 2, 64), k_s.reshape(NSEQ, P, 2, 64),
            r["v_p"].reshape(1, P, 2, 64), v_s.reshape(NSEQ, P, 2, 64))
```
